# Optimizing a Trainium2 kernel written in Bass

```python
import math
import jax
import jax.numpy as jnp
from jax import lax
import numpy as np

D_MODEL = 2048
BATCH = 1
SEQ = 256
DEPTH = 1
DEC_BATCH = 8
DEC_SEQ = 8
PAST_LEN = 2048
PAGE_SIZE = 128

SSM_WIDTH = 1024
SSM_GROUP_SIZE = 16
SSM_GROUPS = SSM_WIDTH // SSM_GROUP_SIZE
SSM_STATE = 64
DT_MIN = 0.001
DT_MAX = 0.1

HEAD_DIM = 128
HEADS_PER_GROUP = 4
WINDOWS = (128, 512, 2048)
DILATIONS = (1, 4, 16)
N_DIL_GROUPS = len(WINDOWS)
N_ATTN_HEADS = N_DIL_GROUPS * HEADS_PER_GROUP
QKV_WIDTH = N_ATTN_HEADS * HEAD_DIM
ATTN_OUT_WIDTH = HEADS_PER_GROUP * HEAD_DIM
ATTN_Q_BLOCK = 128

IN_SPLITS = (SSM_WIDTH, SSM_WIDTH + QKV_WIDTH, SSM_WIDTH + 2 * QKV_WIDTH,
             SSM_WIDTH + 3 * QKV_WIDTH, SSM_WIDTH + 3 * QKV_WIDTH + D_MODEL)
IN_WIDTH = SSM_WIDTH + 3 * QKV_WIDTH + 2 * D_MODEL

PEER_HEADS = 8
PEER_N_KEYS = 128
PEER_EXPERTS = PEER_N_KEYS ** 2
PEER_TOPK = 16
PEER_HALF_DIM = 128
PEER_QUERY_DIM = 2 * PEER_HALF_DIM
PEER_TOKEN_BLOCK = 128

DEEPNORM_ALPHA = (2.0 * DEPTH) ** 0.25
DEEPNORM_BETA = (8.0 * DEPTH) ** -0.25
LN_EPS = 1e-5

kernel_name = "dilated_attn_s5_peer_hybrid_step"

def _layer_norm(x, g, b):
    xf = x.astype(jnp.float32)
    mu = jnp.mean(xf, axis=-1, keepdims=True)
    var = jnp.mean(jnp.square(xf - mu), axis=-1, keepdims=True)
    y = (xf - mu) * lax.rsqrt(var + LN_EPS) * g.astype(jnp.float32) + b.astype(jnp.float32)
    return y.astype(x.dtype)

def _complex_linear_combine(e1, e2):
    ar1, ai1, br1, bi1 = e1
    ar2, ai2, br2, bi2 = e2
    return (ar1 * ar2 - ai1 * ai2,
            ar1 * ai2 + ai1 * ar2,
            ar2 * br1 - ai2 * bi1 + br2,
            ar2 * bi1 + ai2 * br1 + bi2)

def _s5_branch(u, h0, log_dt, a_re, a_im, b_re, b_im, c_re, c_im, d_skip, w_glu):
    f32 = jnp.float32
    bsz, n_pos, _ = u.shape
    uf = u.astype(f32)
    ar = a_re.astype(f32)
    ai = a_im.astype(f32)
    dt = jnp.exp(log_dt.astype(f32))[:, None]
    mag = jnp.exp(ar * dt)
    abar_re = mag * jnp.cos(ai * dt)
    abar_im = mag * jnp.sin(ai * dt)
    den = ar * ar + ai * ai
    f_re = ((abar_re - 1.0) * ar + abar_im * ai) / den
    f_im = (abar_im * ar - (abar_re - 1.0) * ai) / den
    br = b_re.astype(f32)
    bi = b_im.astype(f32)
    bb_re = f_re[..., None] * br - f_im[..., None] * bi
    bb_im = f_re[..., None] * bi + f_im[..., None] * br
    ug = uf.reshape(bsz, n_pos, SSM_GROUPS, SSM_GROUP_SIZE)
    bu_re = jnp.einsum('blgh,gph->lbgp', ug, bb_re)
    bu_im = jnp.einsum('blgh,gph->lbgp', ug, bb_im)
    if h0 is not None:
        h0r = h0[..., 0].astype(f32)
        h0i = h0[..., 1].astype(f32)
        bu_re = bu_re.at[0].add(abar_re * h0r - abar_im * h0i)
        bu_im = bu_im.at[0].add(abar_re * h0i + abar_im * h0r)
    a_seq_re = jnp.broadcast_to(abar_re, (n_pos, 1, SSM_GROUPS, SSM_STATE))
    a_seq_im = jnp.broadcast_to(abar_im, (n_pos, 1, SSM_GROUPS, SSM_STATE))
    _, _, h_re, h_im = lax.associative_scan(
        _complex_linear_combine, (a_seq_re, a_seq_im, bu_re, bu_im), axis=0)
    y = (jnp.einsum('lbgp,ghp->blgh', h_re, c_re.astype(f32))
         - jnp.einsum('lbgp,ghp->blgh', h_im, c_im.astype(f32)))
    y = y.reshape(bsz, n_pos, SSM_WIDTH) + d_skip.astype(f32) * uf
    g = jax.nn.gelu(y)
    out = g * jax.nn.sigmoid(g @ w_glu.astype(f32))
    final = jnp.stack([h_re[-1], h_im[-1]], axis=-1)
    return out.astype(u.dtype), final.astype(u.dtype)

def _alibi_slopes():
    return 2.0 ** (-8.0 * jnp.arange(1, N_ATTN_HEADS + 1, dtype=jnp.float32) / N_ATTN_HEADS)

def _dilated_mixture(q, k_pads, v_pads, local, qpos):
    scale = HEAD_DIM ** -0.5
    slopes = _alibi_slopes()
    outs, lses = [], []
    for g in range(N_DIL_GROUPS):
        d = DILATIONS[g]
        offs = jnp.arange(WINDOWS[g] // d + 1, dtype=jnp.int32) * d
        idx = WINDOWS[g] + local[:, None] - offs[None, :]
        valid = (qpos[:, None] - offs[None, :]) >= 0
        kg = jnp.take(k_pads[g], idx, axis=1)
        vg = jnp.take(v_pads[g], idx, axis=1)
        qg = q[:, :, g * HEADS_PER_GROUP:(g + 1) * HEADS_PER_GROUP]
        s = jnp.einsum('bqhd,bqkhd->bhqk', qg, kg, preferred_element_type=jnp.float32) * scale
        s = s - slopes[g * HEADS_PER_GROUP:(g + 1) * HEADS_PER_GROUP, None, None] * offs.astype(jnp.float32)
        s = jnp.where(valid, s, -jnp.inf)
        lse = jax.nn.logsumexp(s, axis=-1)
        p = jnp.exp(s - lse[..., None])
        outs.append(jnp.einsum('bhqk,bqkhd->bqhd', p, vg.astype(jnp.float32)))
        lses.append(lse)
    w = jax.nn.softmax(jnp.stack(lses, axis=0), axis=0)
    w = jnp.transpose(w, (0, 1, 3, 2))[..., None]
    out = jnp.sum(w * jnp.stack(outs, axis=0), axis=0)
    return out.astype(q.dtype)

def _split_group(t, g):
    return t[:, :, g * HEADS_PER_GROUP:(g + 1) * HEADS_PER_GROUP]

def _prompt_attention(q, k, v):
    bsz, n_pos = q.shape[0], q.shape[1]
    k_pads, v_pads, new_kv = [], [], []
    for g in range(N_DIL_GROUPS):
        kg = _split_group(k, g)
        vg = _split_group(v, g)
        pad = ((0, 0), (WINDOWS[g], 0), (0, 0), (0, 0))
        k_pads.append(jnp.pad(kg, pad))
        v_pads.append(jnp.pad(vg, pad))
        keep = min(WINDOWS[g], n_pos)
        new_kv.append(jnp.stack([kg[:, n_pos - keep:], vg[:, n_pos - keep:]], axis=2))

    def block(t0):
        qb = lax.dynamic_slice_in_dim(q, t0, ATTN_Q_BLOCK, axis=1)
        pos = t0 + jnp.arange(ATTN_Q_BLOCK, dtype=jnp.int32)
        return _dilated_mixture(qb, k_pads, v_pads, pos, pos)

    starts = jnp.arange(n_pos // ATTN_Q_BLOCK, dtype=jnp.int32) * ATTN_Q_BLOCK
    o = lax.map(block, starts)
    o = jnp.transpose(o, (1, 0, 2, 3, 4)).reshape(bsz, n_pos, ATTN_OUT_WIDTH)
    return o, new_kv

def _sample_attention(q, k, v, kv_caches):
    bsz, n_new = q.shape[0], q.shape[1]
    k_pads, v_pads, new_kv = [], [], []
    for g in range(N_DIL_GROUPS):
        kg = _split_group(k, g)
        vg = _split_group(v, g)
        buf = kv_caches[g]
        fill = jnp.zeros((bsz, WINDOWS[g] - buf.shape[1], HEADS_PER_GROUP, HEAD_DIM), k.dtype)
        k_pads.append(jnp.concatenate([fill, buf[:, :, 0].astype(k.dtype), kg], axis=1))
        v_pads.append(jnp.concatenate([fill, buf[:, :, 1].astype(v.dtype), vg], axis=1))
        new_kv.append(jnp.stack([kg, vg], axis=2))
    local = jnp.arange(n_new, dtype=jnp.int32)
    o = _dilated_mixture(q, k_pads, v_pads, local, PAST_LEN + local)
    return o.reshape(bsz, n_new, ATTN_OUT_WIDTH), new_kv

def _peer(x2d, w_q, sub_keys_1, sub_keys_2, u_tab, v_tab):
    n_tok = x2d.shape[0]
    pad = (-n_tok) % PEER_TOKEN_BLOCK
    xp = jnp.pad(x2d, ((0, pad), (0, 0))).reshape(-1, PEER_TOKEN_BLOCK, D_MODEL)
    k1 = sub_keys_1.astype(jnp.float32)
    k2 = sub_keys_2.astype(jnp.float32)

    def block(xb):
        q = jnp.dot(xb, w_q, preferred_element_type=jnp.float32)
        q = q.reshape(PEER_TOKEN_BLOCK, PEER_HEADS, 2, PEER_HALF_DIM)
        s1 = jnp.einsum('thd,kd->thk', q[:, :, 0], k1)
        s2 = jnp.einsum('thd,kd->thk', q[:, :, 1], k2)
        v1, i1 = lax.top_k(s1, PEER_TOPK)
        v2, i2 = lax.top_k(s2, PEER_TOPK)
        cand = (v1[..., :, None] + v2[..., None, :]).reshape(PEER_TOKEN_BLOCK, PEER_HEADS, -1)
        cidx = (i1[..., :, None] * PEER_N_KEYS + i2[..., None, :]).reshape(PEER_TOKEN_BLOCK, PEER_HEADS, -1)
        top, pos = lax.top_k(cand, PEER_TOPK)
        eidx = jnp.take_along_axis(cidx, pos, axis=-1)
        gate = jax.nn.softmax(top, axis=-1)
        ug = u_tab[eidx]
        act = jax.nn.gelu(jnp.einsum('td,thkd->thk', xb, ug, preferred_element_type=jnp.float32))
        vg = v_tab[eidx]
        out = jnp.einsum('thk,thkd->td', gate * act, vg.astype(jnp.float32))
        return out.astype(xb.dtype)

    out = lax.map(block, xp).reshape(-1, D_MODEL)
    return out[:n_tok]

def _decoder_layer(x, kv_caches, h0, w_in, ssm_log_dt, ssm_a_re, ssm_a_im, ssm_b_re, ssm_b_im,
                   ssm_c_re, ssm_c_im, ssm_d, ssm_w_glu, w_branch_ssm, w_branch_attn, w_out,
                   ln1_g, ln1_b, peer_w_q, peer_sub_keys_1, peer_sub_keys_2, peer_u, peer_v,
                   ln2_g, ln2_b):
    bsz, n_pos, _ = x.shape
    z = jnp.einsum('bld,dn->bln', x, w_in)
    u, q, k, v, gate_s, gate_a = jnp.split(z, IN_SPLITS, axis=-1)
    q = q.reshape(bsz, n_pos, N_ATTN_HEADS, HEAD_DIM)
    k = k.reshape(bsz, n_pos, N_ATTN_HEADS, HEAD_DIM)
    v = v.reshape(bsz, n_pos, N_ATTN_HEADS, HEAD_DIM)
    ssm_out, ssm_state = _s5_branch(u, h0, ssm_log_dt, ssm_a_re, ssm_a_im, ssm_b_re, ssm_b_im,
                                    ssm_c_re, ssm_c_im, ssm_d, ssm_w_glu)
    if kv_caches is None:
        attn_out, new_kv = _prompt_attention(q, k, v)
    else:
        attn_out, new_kv = _sample_attention(q, k, v, kv_caches)
    merged = (jax.nn.sigmoid(gate_s) * jnp.einsum('bln,nd->bld', ssm_out, w_branch_ssm)
              + jax.nn.sigmoid(gate_a) * jnp.einsum('bln,nd->bld', attn_out, w_branch_attn))
    mix = jnp.einsum('bld,de->ble', merged, w_out)
    h = _layer_norm(DEEPNORM_ALPHA * x + mix, ln1_g, ln1_b)
    f = _peer(h.reshape(-1, D_MODEL), peer_w_q, peer_sub_keys_1, peer_sub_keys_2,
              peer_u, peer_v).reshape(bsz, n_pos, D_MODEL)
    y = _layer_norm(DEEPNORM_ALPHA * h + f, ln2_g, ln2_b)
    return y, new_kv, ssm_state

def setup_inputs(seed: int = 0) -> dict:
    key = jax.random.key(seed)
    ks = jax.random.split(key, 32)
    f32 = jnp.float32

    def nrm(k, shape, s):
        return jax.random.normal(k, shape, f32) * s

    kv_shape = lambda w: (DEC_BATCH, min(w, PAST_LEN), 2, HEADS_PER_GROUP, HEAD_DIM)
    col_scale = jnp.concatenate([
        jnp.ones((SSM_WIDTH + 2 * QKV_WIDTH,), f32),
        jnp.full((QKV_WIDTH,), DEEPNORM_BETA, f32),
        jnp.ones((2 * D_MODEL,), f32)])
    return {
        'x_prompt': nrm(ks[0], (BATCH, SEQ, D_MODEL), 1.0),
        'x_sample': nrm(ks[1], (DEC_BATCH, DEC_SEQ, D_MODEL), 1.0),
        'cache_kv_w128': nrm(ks[2], kv_shape(WINDOWS[0]), 1.0),
        'cache_kv_w512': nrm(ks[3], kv_shape(WINDOWS[1]), 1.0),
        'cache_kv_w2048': nrm(ks[4], kv_shape(WINDOWS[2]), 1.0),
        'state_ssm': nrm(ks[5], (DEC_BATCH, SSM_GROUPS, SSM_STATE, 2), 0.5),
        'w_in': nrm(ks[6], (D_MODEL, IN_WIDTH), D_MODEL ** -0.5) * col_scale,
        'ssm_log_dt': jax.random.uniform(ks[7], (SSM_GROUPS,), f32, math.log(DT_MIN), math.log(DT_MAX)),
        'ssm_a_re': -0.5 * jnp.exp(nrm(ks[8], (SSM_GROUPS, SSM_STATE), 0.01)),
        'ssm_a_im': math.pi * jnp.arange(SSM_STATE, dtype=f32)[None, :] + nrm(ks[9], (SSM_GROUPS, SSM_STATE), 0.01),
        'ssm_b_re': nrm(ks[10], (SSM_GROUPS, SSM_STATE, SSM_GROUP_SIZE), (2 * SSM_GROUP_SIZE) ** -0.5),
        'ssm_b_im': nrm(ks[11], (SSM_GROUPS, SSM_STATE, SSM_GROUP_SIZE), (2 * SSM_GROUP_SIZE) ** -0.5),
        'ssm_c_re': nrm(ks[12], (SSM_GROUPS, SSM_GROUP_SIZE, SSM_STATE), SSM_STATE ** -0.5),
        'ssm_c_im': nrm(ks[13], (SSM_GROUPS, SSM_GROUP_SIZE, SSM_STATE), SSM_STATE ** -0.5),
        'ssm_d': nrm(ks[14], (SSM_WIDTH,), 0.5),
        'ssm_w_glu': nrm(ks[15], (SSM_WIDTH, SSM_WIDTH), SSM_WIDTH ** -0.5),
        'w_branch_ssm': nrm(ks[16], (SSM_WIDTH, D_MODEL), SSM_WIDTH ** -0.5),
        'w_branch_attn': nrm(ks[17], (ATTN_OUT_WIDTH, D_MODEL), ATTN_OUT_WIDTH ** -0.5),
        'w_out': nrm(ks[18], (D_MODEL, D_MODEL), D_MODEL ** -0.5 * DEEPNORM_BETA),
        'ln1_g': 1.0 + nrm(ks[19], (D_MODEL,), 0.01),
        'ln1_b': nrm(ks[20], (D_MODEL,), 0.01),
        'peer_w_q': nrm(ks[21], (D_MODEL, PEER_HEADS * PEER_QUERY_DIM), D_MODEL ** -0.5),
        'peer_sub_keys_1': nrm(ks[22], (PEER_N_KEYS, PEER_HALF_DIM), PEER_HALF_DIM ** -0.5),
        'peer_sub_keys_2': nrm(ks[23], (PEER_N_KEYS, PEER_HALF_DIM), PEER_HALF_DIM ** -0.5),
        'peer_u': nrm(ks[24], (PEER_EXPERTS, D_MODEL), D_MODEL ** -0.5),
        'peer_v': nrm(ks[25], (PEER_EXPERTS, D_MODEL), DEEPNORM_BETA),
        'ln2_g': 1.0 + nrm(ks[26], (D_MODEL,), 0.01),
        'ln2_b': nrm(ks[27], (D_MODEL,), 0.01),
    }

def reference(x_prompt, x_sample, cache_kv_w128, cache_kv_w512, cache_kv_w2048, state_ssm,
              w_in, ssm_log_dt, ssm_a_re, ssm_a_im, ssm_b_re, ssm_b_im, ssm_c_re, ssm_c_im,
              ssm_d, ssm_w_glu, w_branch_ssm, w_branch_attn, w_out, ln1_g, ln1_b,
              peer_w_q, peer_sub_keys_1, peer_sub_keys_2, peer_u, peer_v, ln2_g, ln2_b):
    y_prompt, y_sample = x_prompt, x_sample
    for _layer in range(DEPTH):
        y_prompt, kv_p, ssm_p = _decoder_layer(
            y_prompt, None, None, w_in, ssm_log_dt, ssm_a_re, ssm_a_im, ssm_b_re, ssm_b_im,
            ssm_c_re, ssm_c_im, ssm_d, ssm_w_glu, w_branch_ssm, w_branch_attn, w_out,
            ln1_g, ln1_b, peer_w_q, peer_sub_keys_1, peer_sub_keys_2, peer_u, peer_v, ln2_g, ln2_b)
        y_sample, kv_s, ssm_s = _decoder_layer(
            y_sample, (cache_kv_w128, cache_kv_w512, cache_kv_w2048), state_ssm,
            w_in, ssm_log_dt, ssm_a_re, ssm_a_im, ssm_b_re, ssm_b_im,
            ssm_c_re, ssm_c_im, ssm_d, ssm_w_glu, w_branch_ssm, w_branch_attn, w_out,
            ln1_g, ln1_b, peer_w_q, peer_sub_keys_1, peer_sub_keys_2, peer_u, peer_v, ln2_g, ln2_b)
    return (y_prompt, y_sample, kv_p[0], kv_p[1], kv_p[2], ssm_p, kv_s[0], kv_s[1], kv_s[2], ssm_s)


_drawn_inputs = setup_inputs


def setup_inputs(seed=0):
    import zlib

    import numpy as np

    out = dict(_drawn_inputs(seed))
    spreads = {}
    factors = {}
    for name, (base, spread) in spreads.items():
        noise = np.random.default_rng([zlib.crc32(name.encode()), seed]).standard_normal(out[name].shape)
        drawn = base * np.exp(spread * noise) if base else spread * noise
        out[name] = jnp.asarray(drawn.astype(out[name].dtype))
    for name, factor in factors.items():
        out[name] = (out[name] * factor).astype(out[name].dtype)
    return out
```

```python
from contextlib import ExitStack, contextmanager

import numpy as np

import concourse.bass as bass
from concourse import mybir

F32 = mybir.dt.float32
I32 = mybir.dt.int32
U32 = mybir.dt.uint32
ALU = mybir.AluOpType
ACT = mybir.ActivationFunctionType
AX = mybir.AxisListType

P = 128
D = 2048
KT = D // P
SEQ = 256
NB, NS = 8, 8
SAMPLE = NB * NS
T = SEQ + SAMPLE
PT = SEQ // P
TOK_TILES = [(0, P), (1, P), (2, SAMPLE)]

WS = 1024
QUADS = WS // P
STILES = 64 * 64 // P
PER_QUAD = STILES // QUADS
NFIN = 1 + NB

HD = 128
NG, NJ = 3, 4
WINDOWS, DILS = (128, 512, 2048), (1, 4, 16)
NHEAD = NG * NJ
QKV_TILES = 3 * NHEAD
CLASSES = (1, 4, NS)
CBLK = sum(CLASSES)
CSLOTS = 2
FAR = 1.0e30

PH, PK, PTOP = 8, 128, 16
EXPERTS = PH * PTOP
CHUNK = 4
URING, VRING = 4, 8

ALPHA = 2.0 ** 0.25
EPS = 1e-5
NEG = -3.0e38
ROUND = 1.5 * 2.0 ** 23
TWO_PI_HI = 6.28125
TWO_PI_LO = 2.0 * float(np.pi) - TWO_PI_HI
PI_SAFE = 3.1415925

RING = 4
WSLOT = KT * P
N_PRE = 4
N_SSM = N_PRE + QUADS * RING
N_X = QUADS + QKV_TILES
N_GLU = N_X + QUADS // 2
N_MERGE = N_GLU + 3 * KT
N_OUT = N_MERGE + KT
N_PQ = N_OUT + KT


class Chain:

    def __init__(self, eng, sem):
        self.eng, self.sem, self.done, self.base, self.i, self.per = eng, sem, 0, 0, None, 0

    def link(self, ins):
        self.done += 1
        ins.then_inc(self.sem, 1)
        if self.i is None:
            self.eng.wait_ge(self.sem, self.done)
        else:
            self.eng.wait_ge(self.sem, self.i * self.per + self.done)

    @contextmanager
    def loop(self, steps, per):
        base = self.done
        with self.eng.Fori(0, steps) as i:
            self.i, self.per = i, per
            yield i
        assert self.done - base == per, (self.done - base, per)
        self.i, self.done = None, base + steps * per


class Region:

    def __init__(self, arena, lo, hi):
        self.arena, self.at, self.hi = arena, lo, hi

    def take(self, *shape):
        n = int(np.prod(shape))
        lo = self.at
        self.at += n + n % 2
        assert self.at <= self.hi, (self.at, self.hi, shape)
        v = self.arena[:, lo:lo + n]
        if len(shape) > 1:
            c = "abcd"[:len(shape)]
            v = v.rearrange(f"p ({' '.join(c)}) -> p {' '.join(c)}", **dict(zip(c[1:], shape[1:])))
        return v


def spread(ap, dim, n):
    shape = list(ap.shape)
    return ap.unsqueeze(dim).to_broadcast(shape[:dim] + [n] + shape[dim:])


def layer_kernel(nc, A, O):
    with ExitStack() as ctx:
        COLS = 53200
        arena = ctx.enter_context(nc.sbuf_tensor("arena", [P, COLS], F32))
        ps = ctx.enter_context(nc.psum_tensor("ps", [P, 8, 512], F32))

        def sem(name):
            return ctx.enter_context(nc.semaphore(name))

        r = Region(arena, 0, COLS)
        xT = r.take(KT, T)
        ring = r.take(RING, WSLOT)
        ident = r.take(P)
        lo_qkv = r.at
        qkv = r.take(QKV_TILES, T)
        lo_g = r.at
        gT = r.take(QUADS, T)
        lo_a = r.at

        r = Region(arena, lo_a, COLS)
        rot = r.take(2, STILES, SEQ)
        hi_rot = r.at
        mag = r.take(STILES)
        fre = r.take(STILES)
        fim = r.take(STILES)
        h0m = r.take(STILES, 2, NB)
        rotx = r.take(2, 2, T)
        magx = r.take(2, T)
        mask = r.take(T)
        lo_m = r.at
        m1 = r.take(2, T)
        m2 = r.take(2, T)
        gw = r.take(2, T)
        hs = r.take(2, 2, T)
        hi_m = r.at
        uq = r.take(T)
        ypre = r.take(T)
        braw = r.take(2, P)
        craw = r.take(2, P)
        bbq = r.take(2, P)
        btq = r.take(2, P)
        ccq = r.take(2, P)
        dskip = r.take(QUADS)
        fin = r.take(STILES, 2, NFIN)
        r = Region(arena, lo_qkv + 8 * T, lo_g)
        half = r.take(2, STILES, SEQ // 2)
        r = Region(arena, lo_m, hi_m)
        s_h0 = r.take(STILES, 2, NB)
        s_dt, s_are, s_aim, s_x, s_n, s_r, s_u, s_sin, s_cos, s_br, s_bi, s_den, s_p, s_q = (
            r.take(STILES) for _ in range(14))

        r = Region(arena, lo_a, hi_rot)
        kc = r.take(CSLOTS, CBLK, P)
        vc = r.take(CSLOTS, CBLK, P)
        lo_qz = r.at
        qz0 = r.take(NB * 72)
        qz1 = r.take(NB * 264)
        qz2 = r.take(SAMPLE * 65)
        hi_qz = r.at
        qs = r.take(NG, T)
        vs = r.take(NG, T)
        r = Region(arena, hi_rot, COLS)
        so = r.take(QUADS, T)
        dist = r.take(NG, SEQ)
        dist_c = r.take(NG, P)
        dist_n = r.take(NG, SAMPLE)
        slopes = r.take(NJ, NG)
        nsl = r.take(NG)
        vtok = r.take(PT, NG, P)
        vnew = r.take(NG, P)
        s0 = r.take(NG, P)
        sc = r.take(NG, P)
        sn = r.take(NG, SAMPLE)
        scn = arena[:, r.at - NG * (P + SAMPLE):r.at]
        st = r.take(3, 4)
        sig = r.take(2, T)
        assert r.at <= COLS - STILES * 2 * NFIN
        r = Region(arena, lo_g, lo_a)
        s1 = r.take(NG, SEQ)
        pt0 = r.take(NG, P)
        pt1 = r.take(NG * PT, P)
        ptc = r.take(NG, SAMPLE)
        ptn = r.take(NG, SAMPLE)

        r = Region(arena, lo_a, hi_rot)
        mT = r.take(KT, T)
        gsg = r.take(2, 2, T)
        gp = r.take(2, 2, T)
        sq = r.take(KT, T)
        var, rv, rs, nt = (r.take(T) for _ in range(4))
        ln1 = r.take(2, KT)
        onesm = r.take(P)

        r = Region(arena, lo_qkv, lo_a)
        htok = r.take(3, D)
        v16 = r.take(2, PTOP)
        i16 = r.take(2, PTOP)
        if16 = r.take(2, PTOP)
        t16 = r.take(PTOP)
        p16 = r.take(PTOP)
        ab = r.take(2, PTOP)
        abf = r.take(2, PTOP)
        e12 = r.take(2, PTOP)
        iota = r.take(PTOP)
        gsum = r.take(PH)
        oh = r.take(2, PTOP, PTOP)
        cand = r.take(PTOP, PTOP)
        sc2 = r.take(2, PK)
        eidx = r.take(3, EXPERTS)
        gate = r.take(3, EXPERTS)
        idxs = r.take(2, 2 * CHUNK)
        act_ = r.take(2, CHUNK)
        gel = r.take(2, CHUNK)
        wgt = r.take(2, CHUNK)
        bns = r.take(4, 6)
        bna = r.take(2)
        lnr = r.take(4)
        r = Region(arena, lo_a, COLS)
        sx = r.take(3, 2 * PH, PK)
        qh = r.take(2, T)
        k12 = r.take(2, PK)
        diag = r.take(CHUNK, P)
        adiag = r.take(P)
        g2 = r.take(D)
        b2 = r.take(D)
        bufs = [r.take(D) for _ in range(6)]
        r = Region(arena, 0, KT * T + RING * WSLOT)
        bufs += [r.take(D) for _ in range(6)]
        ub, vb = bufs[:URING], bufs[URING:]
        assert len(vb) == VRING
        yt = Region(arena, lo_a, COLS).take(D)

        wsem = [sem(f"weights_{k}") for k in range(RING)]
        used = sem("tile_multiplied")
        evac = sem("tile_evacuated")
        x_in = [sem(f"x_in_{c}") for c in range(4)]
        small_in = sem("ssm_small_in")
        dvc, acc, poc = sem("dve_chain"), sem("act_chain"), sem("pool_chain")
        su_dt, su_trig, su_rot, su_act = sem("dt"), sem("trig"), sem("tables"), sem("setup_act")
        su_arg = sem("trig_args")
        b_in, c_in = sem("b_in"), sem("c_in")
        bb_ready, bt_done, bt_ready = sem("b_scaled"), sem("b_transposed"), sem("b_staged")
        cc_ready = sem("c_staged")
        bu_ready, bu_free = sem("bu_ready"), sem("bu_free")
        rotx_ready, magx_ready = sem("rotx_ready"), sem("magx_ready")
        h_ready, y_done, fin_done = sem("h_ready"), sem("y_done"), sem("final_copied")
        ypre_ready, g_ready = sem("ypre_ready"), sem("gelu_ready")
        stored = sem("outputs_stored")
        sig_ready, so_ready, glu_done = sem("glu_sigmoid"), sem("s5_out"), sem("glu_multiplied")
        att_in = sem("attention_constants")
        kcs = [sem(f"k_cache_{k}") for k in range(CSLOTS)]
        vcs = [sem(f"v_cache_{k}") for k in range(CSLOTS)]
        k_used, v_used = sem("k_cache_used"), sem("v_cache_used")
        qz_zero, qs_ready, vs_ready, qz_ready = sem("qz_zero"), sem("qs"), sem("vs"), sem("qz")
        nsl_ready = sem("slopes_staged")
        vt_done, vt_ready = sem("v_transposed"), sem("v_token_major")
        sc0_done, sc1_done, scs_done = sem("scores_0"), sem("scores_1"), sem("scores_sample")
        mx, ex = sem("softmax_max"), sem("softmax_exp")
        p_ready = sem("probabilities")
        pt_done, pt_ready = sem("p_transposed"), sem("p_staged")
        o_done, o_ready = sem("attended"), sem("attention_out")
        sg_ready, merged = sem("gates_sigmoid"), sem("merged")
        ln_in = sem("ln1_in")
        resid, mean_done, cent, sq_ready, var_done = (
            sem("residual"), sem("mean"), sem("centred"), sem("squared"), sem("variance"))
        rv_ready, rs_ready, nrm, h_done = sem("rv"), sem("rsqrt"), sem("normed"), sem("h_feature")
        qh_ready, psc_done, sx_ready = sem("query_staged"), sem("subkey_scores"), sem("scores_out")
        ht_done, ht_ready = sem("h_transposed"), sem("h_token_major")
        peer_in = sem("peer_small_in")
        gd_ready, ge_ready, topk_done = sem("gate_diff"), sem("gate_exp"), sem("topk")
        usem = [sem(f"u_rows_{k}") for k in range(URING)]
        vsem = [sem(f"v_rows_{k}") for k in range(VRING)]
        u_used, v_used2 = sem("u_rows_used"), sem("v_rows_used")
        gelu_ready, dg_ready = sem("expert_gelu"), sem("diagonals")
        seeded = sem("alpha_h_seeded")
        l2_in, l2_sq, y_ready, y_out = sem("ln2_in"), sem("ln2_sqrt"), sem("y_ready"), sem("y_out")

        passed = sem("waits_passed")

        def hold(eng):
            eng.sem_inc(passed, 1)

        def slot(k):
            return ring[:, k, :].rearrange("p (k m) -> p k m", m=P)

        block = ctx.enter_context(nc.Block())

        @block.sync
        def _(sp):
            def load(k, src, cols=WSLOT):
                sp.dma_start(ring[:, k, 0:cols], src).then_inc(wsem[k], 16)

            for c in range(4):
                sp.dma_start(xT[:, 4 * c:4 * c + 4, :], A["xT"][:, 4 * c:4 * c + 4, :]).then_inc(x_in[c], 16)
                load(c, A["w_x"][c])
                if c == 0:
                    for dst, name in ((s_dt, "log_dt"), (s_are, "a_re"), (s_aim, "a_im"),
                                      (s_h0, "h0"), (mask, "mask"), (dskip, "dskip"), (ident, "ident")):
                        sp.dma_start(dst, A[name]).then_inc(small_in, 16)
                    sp.dma_start(braw, A["ssm_b"][0]).then_inc(b_in, 16)
                    sp.dma_start(craw, A["ssm_c"][0]).then_inc(c_in, 16)
            with sp.Fori(0, QUADS) as i:
                for k in range(RING):
                    sp.wait_ge(used, i * RING + (k + 1))
                    load(k, A["w_x"][i * RING + (N_PRE + k)])
                sp.wait_ge(bb_ready, i + 1)
                sp.dma_start(braw, A["ssm_b"][i + 1]).then_inc(b_in, 16)
                sp.wait_ge(cc_ready, i + 1)
                sp.dma_start(craw, A["ssm_c"][i + 1]).then_inc(c_in, 16)
            with sp.Fori(0, (N_X - N_SSM) // RING) as i:
                for k in range(RING):
                    sp.wait_ge(used, i * RING + (N_SSM - RING + k + 1))
                    load(k, A["w_x"][i * RING + (N_SSM + k)])
            sp.wait_ge(fin_done, STILES + 2)
            sp.dma_start(O["ssm"], fin).then_inc(stored, 16)
            sp.wait_ge(g_ready, QUADS)
            for dst, name in ((dist, "dist"), (slopes, "slopes")):
                sp.dma_start(dst, A[name]).then_inc(att_in, 16)
            sp.dma_start(dist_c[0:SAMPLE], A["dist_c"]).then_inc(att_in, 16)
            sp.dma_start(dist_n[0:SAMPLE], A["dist_n"]).then_inc(att_in, 16)
            for n in range(N_X, N_GLU):
                sp.wait_ge(used, n - RING + 1)
                load(n % RING, A["w_glu"][n - N_X])
            sp.wait_ge(evac, N_X)
            sp.dma_start(O["kv"], qkv[:, NHEAD:, :]).then_inc(stored, 16)
            for k in range(RING):
                sp.wait_ge(used, N_GLU - RING + k + 1)
                load(k, A["w_merge"][k])
            with sp.Fori(0, NJ) as j:
                for b in range(NB):
                    sp.wait_ge(k_used, j * NB + (b + 1))
                    sp.dma_start(kc[:, b % CSLOTS], A["k_cache"][j * NB + b]).then_inc(kcs[b % CSLOTS], 16)
                for b in range(NB):
                    sp.wait_ge(v_used, j * NB + (b + 1))
                    sp.dma_start(vc[:, b % CSLOTS], A["v_cache"][j * NB + b]).then_inc(vcs[b % CSLOTS], 16)
            for n in range(N_GLU + RING, N_GLU + 3 * RING):
                sp.wait_ge(used, n - RING + 1)
                load(n % RING, A["w_merge"][n - N_GLU])
            with sp.Fori(0, KT // 4 - 1) as i:
                for k in range(3 * RING):
                    n0 = N_GLU + 3 * RING + k
                    sp.wait_ge(used, i * (3 * RING) + (n0 - RING + 1))
                    load(k % RING, A["w_merge"][i * (3 * RING) + (n0 - N_GLU)])
            sp.wait_ge(used, N_GLU + 1)
            sp.wait_ge(o_ready, NJ)
            sp.dma_start(ln1, A["ln1"]).then_inc(ln_in, 16)
            sp.dma_start(onesm, A["ones"]).then_inc(ln_in, 16)
            steps = KT // RING + 1
            with sp.Fori(0, steps) as i:
                for k in range(RING):
                    sp.wait_ge(used, i * RING + (N_MERGE - RING + k + 1))
                    load(k, A["w_op"][i * RING + k])
            sp.wait_ge(h_done, KT)
            sp.dma_start(k12, A["sub_keys"]).then_inc(peer_in, 16)
            sp.dma_start(iota, A["iota"]).then_inc(peer_in, 16)
            sp.dma_start(g2, A["ln2"][0]).then_inc(l2_in, 16)
            sp.dma_start(b2, A["ln2"][1]).then_inc(l2_in, 16)
            with sp.Fori(0, 2 * KT // RING - steps) as i:
                for k in range(RING):
                    sp.wait_ge(used, i * RING + (N_MERGE + (steps - 1) * RING + k + 1))
                    load(k, A["w_op"][i * RING + (steps * RING + k)])
            for a, rows in TOK_TILES:
                sp.wait_ge(y_ready, a + 1)
                sp.dma_start(O["y"][a * P:a * P + rows, :], yt[0:rows, :]).then_inc(y_out, 16)
            sp.wait_ge(stored, 2 * 16)
            sp.wait_ge(y_out, 3 * 16)

        @block.tensor
        def _(pe):
            for s, n in ((y_done, 2), (k_used, CSLOTS), (v_used, CSLOTS), (psc_done, 2), (v_used2, VRING)):
                pe.sem_inc(s, n)

            def matmuls(out, lhs, rhs, n, skip=False):
                for k in range(n):
                    ins = pe.matmul(out, lhs(k), rhs(k), start=(k == 0), stop=(k == n - 1))
                return ins

            def project(k, bank):
                return matmuls(ps[:, bank, 0:T], lambda t: slot(k)[:, t, :], lambda t: xT[:, t, :], KT)

            for n in range(N_PRE):
                pe.wait_ge(wsem[n], 16)
                if n == 0:
                    for c in range(4):
                        pe.wait_ge(x_in[c], 16)
                if n >= 2:
                    pe.wait_ge(evac, n - 1)
                project(n, n % 2).then_inc(used, 1)

            def tile(i, k):
                pe.wait_ge(wsem[k], i * 16 + 32)
                pe.wait_ge(evac, i * RING + (N_PRE + k - 1))
                project(k, k % 2).then_inc(used, 1)

            def b_u(i, j):
                pe.wait_ge(bu_free, i * PER_QUAD + (j + 1))
                lo = 32 * j
                for part in range(2):
                    ins = pe.matmul(ps[:, 2 + 2 * (j % 2) + part, 0:T], btq[lo:lo + 32, part, :],
                                    uq[lo:lo + 32, :], start=True, stop=True)
                ins.then_inc(bu_ready, 1)

            def c_h(i, j):
                lo = 32 * j
                pe.wait_ge(h_ready, i * PER_QUAD + (j + 3))
                for part in range(2):
                    ins = pe.matmul(ps[lo:lo + 32, 6, 0:T], ccq[:, part, lo:lo + 32], hs[:, j % 2, part, :],
                                    start=(part == 0), stop=(part == 1))
                ins.then_inc(y_done, 1)

            with pe.Fori(0, QUADS) as i:
                tile(i, 0)
                pe.wait_ge(bb_ready, i + 1)
                pe.wait_ge(bt_ready, i)
                for part in range(2):
                    ins = pe.transpose(ps[:, 7, part * P:part * P + P], bbq[:, part, :], ident)
                ins.then_inc(bt_done, 1)
                pe.wait_ge(bt_ready, i + 1)
                pe.wait_ge(evac, i * RING + (N_PRE + 1))
                b_u(i, 0)
                b_u(i, 1)
                tile(i, 1)
                pe.wait_ge(cc_ready, i + 1)
                pe.wait_ge(ypre_ready, i)
                c_h(i, 0)
                b_u(i, 2)
                tile(i, 2)
                c_h(i, 1)
                b_u(i, 3)
                tile(i, 3)
                c_h(i, 2)
                c_h(i, 3)
            with pe.Fori(0, (N_X - N_SSM) // RING) as i:
                for k in range(RING):
                    pe.wait_ge(wsem[k], i * 16 + (16 * (N_SSM // RING) + 16))
                    pe.wait_ge(evac, i * RING + (N_SSM + k - 1))
                    project(k, k % 2).then_inc(used, 1)

            pe.wait_ge(g_ready, QUADS)
            for m in range(QUADS):
                n = N_X + m // 2
                if m % 2 == 0:
                    pe.wait_ge(wsem[n % RING], 16 * (n // RING + 1))
                if m < 2:
                    pe.wait_ge(evac, N_X)
                else:
                    pe.wait_ge(sig_ready, m - 1)
                half_slot = slot(n % RING)[:, (m % 2) * QUADS:(m % 2 + 1) * QUADS, :]
                ins = matmuls(ps[:, m % 2, 0:T], lambda t, s=half_slot: s[:, t, :], lambda t: gT[:, t, :], QUADS)
                ins.then_inc(used if m % 2 else glu_done, 1)

            pe.wait_ge(sig_ready, QUADS)
            with pe.Fori(0, NJ) as j:
                pe.wait_ge(vs_ready, j + 1)
                pe.wait_ge(o_ready, j)
                for a in range(PT):
                    for g in range(NG):
                        pe.transpose(ps[:, a, g * P:g * P + P], vs[:, g, a * P:a * P + P], ident)
                for g in range(NG):
                    ins = pe.transpose(ps[0:SAMPLE, 2, g * P:g * P + P], vs[:, g, SEQ:T], ident)
                ins.then_inc(vt_done, 1)
                pe.wait_ge(qs_ready, j + 1)
                for g in range(NG):
                    ins = pe.matmul(ps[:, 3, g * P:g * P + P], qs[:, g, 0:P], qkv[:, j + (NHEAD + 4 * g), 0:P],
                                    start=(g == 0), stop=(g == NG - 1), skip_group_check=True)
                ins.then_inc(sc0_done, 1)
                for g in range(NG):
                    ins = pe.matmul(ps[:, 4 + g // 2, (g % 2) * SEQ:(g % 2) * SEQ + SEQ], qs[:, g, P:SEQ],
                                    qkv[:, j + (NHEAD + 4 * g), 0:SEQ],
                                    start=(g % 2 == 0), stop=(g > 0), skip_group_check=True)
                ins.then_inc(sc1_done, 1)
                for g in range(NG):
                    pe.matmul(ps[0:SAMPLE, 7, g * SAMPLE:(g + 1) * SAMPLE], qs[:, g, SEQ:T],
                              qkv[:, j + (NHEAD + 4 * g), SEQ:T],
                              start=(g == 0), stop=(g == NG - 1), skip_group_check=True)
                pe.wait_ge(qz_ready, j + 1)
                for b in range(NB):
                    pe.wait_ge(kcs[b % CSLOTS], j * (16 * NB // CSLOTS) + 16 * (b // CSLOTS + 1))
                    blk = 0
                    for g, qz in enumerate((qz0, qz1, qz2)):
                        for c in range(CLASSES[g]):
                            w = 64 * (b * CLASSES[g] + c)
                            ins = pe.matmul(ps[0:SAMPLE, 6, g * P:g * P + P], qz[:, w:w + 64],
                                            kc[:, b % CSLOTS, blk, :], start=(b == 0 and blk == 0),
                                            stop=(b == NB - 1 and blk == CBLK - 1), skip_group_check=True)
                            blk += 1
                    ins.then_inc(k_used, 1)
                pe.wait_ge(p_ready, j * 3 + 1)
                for g in range(NG):
                    ins = pe.transpose(ps[:, 3, g * P:g * P + P], s0[:, g, :], ident)
                ins.then_inc(pt_done, 1)
                pe.wait_ge(p_ready, j * 3 + 2)
                for g in range(NG):
                    for a in range(PT):
                        t = g * PT + a
                        ins = pe.transpose(ps[:, 4 + t // 4, (t % 4) * P:(t % 4) * P + P],
                                           s1[:, g, a * P:a * P + P], ident)
                ins.then_inc(pt_done, 1)
                pe.wait_ge(vt_ready, j + 1)
                pe.wait_ge(pt_ready, j * 3 + 1)
                for g in range(NG):
                    pe.matmul(ps[:, 0, 0:P], vtok[:, 0, g, :], pt0[:, g, :],
                              start=(g == 0), stop=(g == NG - 1), skip_group_check=True)
                pe.wait_ge(pt_ready, j * 3 + 2)
                for t in range(NG * PT):
                    pe.matmul(ps[:, 0, P:SEQ], vtok[:, t % PT, t // PT, :], pt1[:, t, :],
                              start=False, stop=(t == NG * PT - 1), skip_group_check=True)
                pe.wait_ge(p_ready, j * 3 + 3)
                hold(pe)
                for g in range(NG):
                    pe.transpose(ps[:, 1, g * SAMPLE:(g + 1) * SAMPLE], sc[0:SAMPLE, g, :],
                                 ident[0:SAMPLE, 0:SAMPLE])
                for g in range(NG):
                    ins = pe.transpose(ps[0:SAMPLE, 2, g * SAMPLE:(g + 1) * SAMPLE], sn[0:SAMPLE, g, :],
                                       ident[0:SAMPLE, 0:SAMPLE])
                ins.then_inc(pt_done, 1)
                pe.wait_ge(pt_ready, j * 3 + 3)
                hold(pe)
                for g in range(NG):
                    pe.matmul(ps[:, 0, SEQ:T], vnew[0:SAMPLE, g, :], ptn[0:SAMPLE, g, :],
                              start=False, stop=False, skip_group_check=True)
                for b in range(NB):
                    pe.wait_ge(vcs[b % CSLOTS], j * (16 * NB // CSLOTS) + 16 * (b // CSLOTS + 1))
                    blk = 0
                    for g in range(NG):
                        n = CLASSES[g]
                        for c in range(n):
                            lo, hi = b * NS + c, (b + 1) * NS
                            last = b == NB - 1 and blk == CBLK - 1
                            ins = pe.matmul(ps[:, 0, SEQ + lo:SEQ + hi:n], vc[:, b % CSLOTS, blk, :],
                                            ptc[:, g, lo:hi:n], start=False, stop=last, skip_group_check=True)
                            blk += 1
                    ins.then_inc(v_used, 1)

            def merge_tile(i, k):
                p = 4 * (k % 2)

                def at(t):
                    n = 3 * k + t
                    pe.wait_ge(wsem[n % RING], i * (3 * 16) + 16 * (N_GLU // RING + n // RING + 1))
                    return slot(n % RING)

                s = at(0)
                pe.wait_ge(merged, i * 4 + (k + 1))
                matmuls(ps[:, p, 0:T], lambda t: s[:, t, :], lambda t: xT[:, t, :], KT).then_inc(used, 1)
                s = at(1)
                matmuls(ps[:, p + 1, 0:T], lambda t: s[:, t, :], lambda t: xT[:, t, :], KT).then_inc(used, 1)
                s = at(2)
                matmuls(ps[:, p + 2, 0:T], lambda t: s[:, t, :], lambda t: so[:, t, :], QUADS)
                matmuls(ps[:, p + 3, 0:T], lambda t: s[:, QUADS + t, :], lambda t: qkv[:, t, :],
                        NJ).then_inc(used, 1)

            pe.wait_ge(so_ready, QUADS)
            pe.wait_ge(o_ready, NJ)
            with pe.Fori(0, KT // 4) as i:
                for k in range(4):
                    merge_tile(i, k)

            pe.wait_ge(merged, KT + 2)
            with pe.Fori(0, KT // RING) as i:
                for k in range(RING):
                    pe.wait_ge(wsem[k], i * 16 + (16 * (N_MERGE // RING) + 16))
                    pe.wait_ge(resid, i * RING + (k + 1))
                    matmuls(ps[:, k, 0:T], lambda t: slot(k)[:, t, :], lambda t: mT[:, t, :],
                            KT).then_inc(used, 1)
            pe.wait_ge(ln_in, 2 * 16)
            pe.wait_ge(resid, KT + RING)
            matmuls(ps[:, 4, 0:T], lambda t: onesm, lambda t: xT[:, t, :], KT).then_inc(mean_done, 1)
            pe.wait_ge(sq_ready, 1)
            matmuls(ps[:, 5, 0:T], lambda t: onesm, lambda t: sq[:, t, :], KT).then_inc(var_done, 1)

            pe.wait_ge(h_done, KT)
            pe.wait_ge(peer_in, 2 * 16)
            with pe.Fori(0, KT // RING) as i:
                for k in range(RING):
                    p = k % 2
                    pe.wait_ge(wsem[k], i * 16 + (16 * (N_OUT // RING) + 16))
                    pe.wait_ge(qh_ready, i * RING + (k + 1))
                    matmuls(ps[:, p, 0:T], lambda t: slot(k)[:, t, :], lambda t: xT[:, t, :],
                            KT).then_inc(used, 1)
                    pe.wait_ge(qh_ready, i * RING + (k + 3))
                    pe.wait_ge(sx_ready, i * RING + (k + 1))
                    for a, rows in TOK_TILES:
                        ins = pe.matmul(ps[0:rows, 2 + p, a * PK:(a + 1) * PK], qh[:, p, a * P:a * P + rows],
                                        k12[:, p, :], start=(a == 0), stop=(a == 2), skip_group_check=True)
                    ins.then_inc(psc_done, 1)
            for a, rows in TOK_TILES:
                for q in range(4):
                    n = 4 * a + q
                    if n >= 4:
                        pe.wait_ge(ht_ready, n - 3)
                    for t in range(4):
                        ins = pe.transpose(ps[0:rows, 4 + q, t * P:(t + 1) * P],
                                           xT[:, 4 * q + t, a * P:a * P + rows], ident)
                    ins.then_inc(ht_done, 1)

            pe.wait_ge(ht_ready, 12)
            for a, rows in TOK_TILES:
                b0 = 4 * (a % 2)
                if a == 0:
                    pe.wait_ge(sx_ready, KT + 2)
                if a == 2:
                    pe.wait_ge(y_ready, 1)
                pe.wait_ge(seeded, 1)
                for q in range(4):
                    ins = pe.matmul(ps[0:rows, b0 + q, :], adiag[0:rows, 0:rows], htok[0:rows, a, q * 512:(q + 1) * 512],
                                    start=True, stop=False, skip_group_check=True)
                with pe.Fori(0, EXPERTS // (2 * CHUNK)) as i:
                    for c in range(2):
                        for k in range(CHUNK):
                            n = a * EXPERTS + c * CHUNK + k
                            v = c * CHUNK + k
                            pe.wait_ge(vsem[v], i * 16 + (16 * (a * EXPERTS // VRING) + 16))
                            pe.wait_ge(dg_ready, i * 8 + (n + 1))
                            hold(pe)
                            for q in range(4):
                                ins = pe.matmul(ps[0:rows, b0 + q, :], diag[0:rows, k, 0:rows],
                                                vb[v][0:rows, q * 512:(q + 1) * 512],
                                                start=False, stop=True, skip_group_check=True)
                            ins.then_inc(v_used2, 1)

        @block.scalar
        def _(act):
            act.sem_inc(qh_ready, 2)
            act.sem_inc(sx_ready, 2)
            act.wait_ge(small_in, 7 * 16)
            act.activation(s_dt, s_dt, ACT.Exp).then_inc(su_dt, 1)
            act.wait_ge(su_arg, 1)
            act.activation(mag, s_u, ACT.Exp).then_inc(su_act, 1)
            act.wait_ge(su_arg, 2)
            act.activation(s_sin, s_r, ACT.Sin)
            act.activation(s_cos, s_p, ACT.Sin).then_inc(su_trig, 1)

            def evacuate(dst, bank):
                act.activation(dst, ps[:, bank, 0:T], ACT.Copy).then_inc(evac, 1)

            for n in range(N_PRE):
                act.wait_ge(used, n + 1)
                evacuate(qkv[:, n, :], n % 2)

            def mag_row(i, j):
                act.wait_ge(h_ready, i * PER_QUAD + (j + 1))
                hold(act)
                act.activation(magx[:, j % 2, :], mask, ACT.Copy,
                               scale=mag[:, bass.ds(i * PER_QUAD + j, 1)]).then_inc(magx_ready, 1)

            def head_tile(i, k):
                act.wait_ge(used, i * RING + (N_PRE + k + 1))
                hold(act)
                evacuate(qkv[:, i * (RING - 1) + (N_PRE + k - 1), :], k % 2)

            act.wait_ge(su_act, 1)
            with act.Fori(0, QUADS) as i:
                act.wait_ge(used, i * RING + (N_PRE + 1))
                act.wait_ge(bu_ready, i * PER_QUAD)
                act.wait_ge(ypre_ready, i)
                evacuate(uq, 0)
                mag_row(i, 0)
                mag_row(i, 1)
                act.wait_ge(bt_done, i + 1)
                act.activation(btq, ps[:, 7, 0:2 * P].rearrange("p (a b) -> p a b", a=2), ACT.Copy).then_inc(bt_ready, 1)
                act.wait_ge(c_in, i * 16 + 16)
                act.wait_ge(y_done, i * PER_QUAD + 2)
                act.activation(ccq[:, 0, :], craw[:, 0, :], ACT.Copy)
                act.activation(ccq[:, 1, :], craw[:, 1, :], ACT.Copy, scale=-1.0).then_inc(cc_ready, 1)
                head_tile(i, 1)
                mag_row(i, 2)
                head_tile(i, 2)
                mag_row(i, 3)
                head_tile(i, 3)
                act.wait_ge(ypre_ready, i + 1)
                hold(act)
                act.activation(gT[:, i, :], ypre, ACT.Gelu_apprx_tanh).then_inc(g_ready, 1)
            with act.Fori(0, (N_X - N_SSM) // RING) as i:
                for k in range(RING):
                    act.wait_ge(used, i * RING + (N_SSM + k + 1))
                    hold(act)
                    evacuate(qkv[:, i * RING + (N_SSM - QUADS + k), :], k % 2)

            for m in range(QUADS):
                if m % 2 == 0:
                    act.wait_ge(glu_done, m // 2 + 1)
                else:
                    act.wait_ge(used, N_X + m // 2 + 1)
                if m >= 2:
                    act.wait_ge(so_ready, m - 1)
                act.activation(sig[:, m % 2, :], ps[:, m % 2, 0:T], ACT.Sigmoid).then_inc(sig_ready, 1)

            q_heads = qkv[:, 0:NHEAD, :].rearrange("p (g j) t -> p g j t", j=NJ)
            act.wait_ge(evac, N_X)
            with act.Fori(0, NJ) as j:
                act.wait_ge(k_used, j * NB + 2)
                hold(act)
                act.activation(qs, q_heads[:, :, j, :], ACT.Copy, scale=HD ** -0.5).then_inc(qs_ready, 1)
                act.wait_ge(vt_done, j + 1)
                act.activation(vtok.rearrange("p a g d -> p a (g d)"), ps[:, 0:PT, 0:NG * P], ACT.Copy)
                act.activation(vnew[0:SAMPLE], ps[0:SAMPLE, 2, 0:NG * P].rearrange("p (g d) -> p g d", g=NG),
                               ACT.Copy).then_inc(vt_ready, 1)
                for w, s, rows in ((0, s0, P), (1, s1, P)):
                    act.wait_ge(mx, j * 3 + (w + 1))
                    act.activation(s, s, ACT.Exp, bias=st[:, w, 0:1], accum_out=st[:, w, 1:2]).then_inc(ex, 1)
                act.wait_ge(pt_done, j * 3 + 1)
                act.activation(pt0, ps[:, 3, 0:NG * P].rearrange("p (g d) -> p g d", g=NG), ACT.Copy).then_inc(pt_ready, 1)
                act.wait_ge(pt_done, j * 3 + 2)
                act.activation(pt1[:, 0:4, :], ps[:, 4, :].rearrange("p (g d) -> p g d", g=4), ACT.Copy)
                act.activation(pt1[:, 4:6, :], ps[:, 5, 0:2 * P].rearrange("p (g d) -> p g d", g=2),
                               ACT.Copy).then_inc(pt_ready, 1)
                act.wait_ge(mx, j * 3 + 3)
                act.activation(scn[0:SAMPLE], scn[0:SAMPLE], ACT.Exp, bias=st[0:SAMPLE, 2, 0:1],
                               accum_out=st[0:SAMPLE, 2, 1:2]).then_inc(ex, 1)
                act.wait_ge(pt_done, j * 3 + 3)
                act.activation(ptc, ps[:, 1, 0:NG * SAMPLE].rearrange("p (g d) -> p g d", g=NG), ACT.Copy)
                act.activation(ptn[0:SAMPLE], ps[0:SAMPLE, 2, 0:NG * SAMPLE].rearrange("p (g d) -> p g d", g=NG),
                               ACT.Copy).then_inc(pt_ready, 1)
                act.wait_ge(v_used, j * NB + (NB + 2))
                hold(act)
                act.activation(qkv[:, j, :], ps[:, 0, 0:T], ACT.Copy).then_inc(o_ready, 1)

            with act.Fori(0, KT // 4) as i:
                for k in range(4):
                    act.wait_ge(used, i * 12 + (N_GLU + 3 * k + 2))
                    act.wait_ge(merged, i * 4 + (k + 1))
                    b0 = 4 * (k % 2)
                    act.activation(gsg[:, k % 2], ps[:, b0:b0 + 2, 0:T], ACT.Sigmoid).then_inc(sg_ready, 1)

            act.wait_ge(cent, 1)
            act.activation(sq, xT, ACT.Square).then_inc(sq_ready, 1)
            act.wait_ge(rv_ready, 1)
            act.activation(rs, rv, ACT.Sqrt).then_inc(rs_ready, 1)
            act.wait_ge(nrm, 1)
            with act.Fori(0, KT) as i:
                act.activation(xT[:, i, :], xT[:, i, :], ACT.Identity, bias=ln1[:, 1, bass.ds(i, 1)],
                               scale=ln1[:, 0, bass.ds(i, 1)]).then_inc(h_done, 1)

            with act.Fori(0, KT // RING) as i:
                for k in range(RING):
                    p = k % 2
                    act.wait_ge(used, i * RING + (N_OUT + k + 1))
                    act.wait_ge(psc_done, i * RING + (k + 1))
                    act.activation(qh[:, p, :], ps[:, p, 0:T], ACT.Copy).then_inc(qh_ready, 1)
                    act.wait_ge(psc_done, i * RING + (k + 3))
                    hold(act)
                    act.activation(sx[:, 0:PT, i * RING + k, :],
                                   ps[:, 2 + p, 0:PT * PK].rearrange("p (a k) -> p a k", a=PT), ACT.Copy)
                    act.activation(sx[0:SAMPLE, PT, i * RING + k, :], ps[0:SAMPLE, 2 + p, PT * PK:3 * PK],
                                   ACT.Copy).then_inc(sx_ready, 1)
            act.wait_ge(stored, 2 * 16)
            for a, rows in TOK_TILES:
                for q in range(4):
                    act.wait_ge(ht_done, 4 * a + q + 1)
                    act.activation(htok[0:rows, a, q * 512:(q + 1) * 512], ps[0:rows, 4 + q, :],
                                   ACT.Copy).then_inc(ht_ready, 1)
            for a, rows in TOK_TILES:
                act.wait_ge(gd_ready, a + 1)
                act.activation(gate[0:rows, a, :], gate[0:rows, a, :], ACT.Exp).then_inc(ge_ready, 1)
            for a, rows in TOK_TILES:
                with act.Fori(0, EXPERTS // (2 * CHUNK)) as i:
                    for c in range(2):
                        act.wait_ge(u_used, i * 8 + (a * EXPERTS + CHUNK * (c + 1) + URING))
                        act.activation(gel[0:rows, c, :], act_[0:rows, c, :],
                                       ACT.Gelu_apprx_tanh).then_inc(gelu_ready, 1)
                act.wait_ge(l2_sq, a + 1)
                act.activation(lnr[0:rows, 1:2], lnr[0:rows, 0:1], ACT.Sqrt).then_inc(rs_ready, 1)

        @block.gpsimd
        def _(pool):
            pool.sem_inc(fin_done, 2)
            chain = Chain(pool, poc)
            pool.wait_ge(su_rot, 1)

            def rotation(i, j):
                pool.wait_ge(h_ready, i * PER_QUAD + (j + 1))
                hold(pool)
                s = i * PER_QUAD + j
                dst = rotx[:, j % 2]
                pool.tensor_copy(dst[:, :, 0:SEQ], rot[:, :, s, :])
                pool.tensor_copy(dst[:, :, SEQ:T].rearrange("p c (b l) -> p c b l", b=NB),
                                 spread(rot[:, :, s, 0:NS], 2, NB)).then_inc(rotx_ready, 1)

            def keep_final(i, j):
                pool.wait_ge(h_ready, i * PER_QUAD + (j + 3))
                hold(pool)
                pool.tensor_copy(fin[:, i * PER_QUAD + j], hs[:, j % 2, :, SEQ - 1:T:NS]).then_inc(fin_done, 1)

            with pool.Fori(0, QUADS) as i:
                rotation(i, 0)
                rotation(i, 1)
                keep_final(i, 0)
                rotation(i, 2)
                keep_final(i, 1)
                rotation(i, 3)
                keep_final(i, 2)
                keep_final(i, 3)

            pool.wait_ge(fin_done, STILES + 2)
            chain.link(pool.memset(arena[:, lo_qz:hi_qz], 0.0))
            v_heads = qkv[:, 2 * NHEAD:, :].rearrange("p (g j) t -> p g j t", j=NJ)
            pool.wait_ge(evac, N_X)
            with pool.Fori(0, NJ) as j:
                pool.wait_ge(vt_done, j)
                hold(pool)
                pool.tensor_copy(vs, v_heads[:, :, j, :]).then_inc(vs_ready, 1)
                pool.wait_ge(qs_ready, j + 1)
                pool.wait_ge(k_used, j * NB + 2)
                hold(pool)
                pool.tensor_copy(qz0.rearrange("p (b w) -> p b w", b=NB)[:, :, 0:NS],
                                 qs[:, 0, SEQ:T].rearrange("p (b l) -> p b l", b=NB))
                z1 = qz1.rearrange("p (b w) -> p b w", b=NB)[:, :, 0:260].rearrange("p b (c v) -> p b c v", c=4)
                pool.tensor_copy(z1[:, :, :, 0:5:4],
                                 qs[:, 1, SEQ:T].rearrange("p (b e c) -> p b c e", b=NB, c=4))
                pool.tensor_copy(qz2.rearrange("p (n v) -> p n v", v=65)[:, :, 0], qs[:, 2, SEQ:T]).then_inc(qz_ready, 1)

            pool.wait_ge(ht_done, 12)
            for a, rows in TOK_TILES:
                pool.wait_ge(topk_done, a + 1)
                with chain.loop(EXPERTS // (4 * CHUNK), 2) as i:
                    for e in range(0, 4 * CHUNK, CHUNK):
                        half = idxs[0:rows, e // (2 * CHUNK), :].bitcast(I32)
                        if e % (2 * CHUNK) == 0:
                            chain.link(pool.tensor_copy(half, eidx[0:rows, a, bass.ds(i * 16 + e, 8)].bitcast(I32)))
                        for table, bufs_, used_, sems in (("peer_u", ub, u_used, usem), ("peer_v", vb, v_used2, vsem)):
                            for k in range(CHUNK):
                                n = e + k
                                s = n % len(bufs_)
                                off = bass.IndirectOffsetOnAxis(half[:, n % 8:n % 8 + 1], 0)
                                pool.wait_ge(used_, i * 16 + (a * EXPERTS + n + 1))
                                hold(pool)
                                pool.indirect_dma_start(bufs_[s][0:rows, :], None, A[table], off).then_inc(sems[s], 16)

        @block.vector
        def _(dve):
            for s, n in ((bu_free, 2), (h_ready, 2), (merged, 2), (resid, RING), (u_used, URING)):
                dve.sem_inc(s, n)
            chain = Chain(dve, dvc)
            link = chain.link
            TT, TS, STT = dve.tensor_tensor, dve.tensor_scalar, dve.scalar_tensor_tensor

            dve.wait_ge(su_dt, 1)
            TT(s_u, s_are, s_dt, ALU.mult).then_inc(su_arg, 1)
            link(TT(s_x, s_aim, s_dt, ALU.mult))
            link(TS(s_n, s_x, 1.0 / (2.0 * float(np.pi)), ROUND, ALU.mult, ALU.add))
            link(TS(s_n, s_n, -ROUND, None, ALU.add))
            link(STT(s_r, s_n, -TWO_PI_HI, s_x, ALU.mult, ALU.add))
            link(STT(s_r, s_n, -TWO_PI_LO, s_r, ALU.mult, ALU.add))
            link(TS(s_r, s_r, PI_SAFE, -PI_SAFE, ALU.min, ALU.max))
            link(STT(s_p, s_r, -1.0, s_r, ALU.mult, ALU.max))
            TS(s_p, s_p, -1.0, float(np.pi) / 2, ALU.mult, ALU.add).then_inc(su_arg, 1)
            link(TT(s_den, s_are, s_are, ALU.mult))
            link(TT(s_q, s_aim, s_aim, ALU.mult))
            link(TT(s_den, s_den, s_q, ALU.add))
            link(dve.reciprocal(s_den, s_den))
            dve.wait_ge(su_act, 1)
            link(TT(h0m.rearrange("p s c b -> p s (c b)"), s_h0.rearrange("p s c b -> p s (c b)"),
                    spread(mag, 2, 2 * NB), ALU.mult))
            dve.wait_ge(su_trig, 1)
            TT(s_br, mag, s_cos, ALU.mult)
            link(TT(s_bi, mag, s_sin, ALU.mult))
            link(TS(s_br, s_br, -1.0, None, ALU.add))
            TT(fre, s_br, s_are, ALU.mult)
            TT(fim, s_bi, s_are, ALU.mult)
            TT(s_q, s_bi, s_aim, ALU.mult)
            link(TT(s_n, s_br, s_aim, ALU.mult))
            TT(fre, fre, s_q, ALU.add)
            link(TT(fim, fim, s_n, ALU.subtract))
            TT(fre, fre, s_den, ALU.mult)
            link(TT(fim, fim, s_den, ALU.mult))
            dve.tensor_copy(rot[:, 0, :, 0], s_cos)
            link(dve.tensor_copy(rot[:, 1, :, 0], s_sin))
            n = 1
            while n < SEQ:
                c, s = rot[:, 0, :, 0:n], rot[:, 1, :, 0:n]
                cn = rot[:, 0, :, n - 1:n].to_broadcast([P, STILES, n])
                sn_ = rot[:, 1, :, n - 1:n].to_broadcast([P, STILES, n])
                a_, b_ = half[:, 0, :, 0:n], half[:, 1, :, 0:n]
                TT(a_, c, cn, ALU.mult)
                link(TT(b_, s, sn_, ALU.mult))
                link(TT(rot[:, 0, :, n:2 * n], a_, b_, ALU.subtract))
                TT(a_, c, sn_, ALU.mult)
                link(TT(b_, s, cn, ALU.mult))
                link(TT(rot[:, 1, :, n:2 * n], a_, b_, ALU.add))
                n *= 2
            dve.sem_inc(su_rot, 1)

            def states(i, j):
                p = j % 2
                s = i * PER_QUAD + j
                bu = ps[:, 2 + 2 * p:4 + 2 * p, 0:T]
                cos, sin = spread(rotx[:, p, 0, :], 1, 2), spread(rotx[:, p, 1, :], 1, 2)
                dve.wait_ge(bu_ready, i * PER_QUAD + (j + 1))
                dve.wait_ge(rotx_ready, i * PER_QUAD + (j + 1))
                dve.wait_ge(h_ready, i * PER_QUAD + (j + 2))
                TT(m1, bu, cos, ALU.mult)
                TT(m2, bu, sin, ALU.mult).then_inc(bu_free, 1)
                dve.wait_ge(bu_free, i * PER_QUAD + (j + 3))
                TT(gw[:, 0, :], m1[:, 0, :], m2[:, 1, :], ALU.add)
                link(TT(gw[:, 1, :], m1[:, 1, :], m2[:, 0, :], ALU.subtract))
                starts = gw[:, :, SEQ:T:NS]
                link(TT(starts, starts, h0m[:, s], ALU.add))
                dve.wait_ge(magx_ready, i * PER_QUAD + (j + 1))
                for c in range(2):
                    ins = dve.tensor_tensor_scan(m1[:, c, :], magx[:, p, :], gw[:, c, :], 0.0, ALU.mult, ALU.add)
                link(ins)
                TT(m2, m1, cos, ALU.mult)
                link(TT(gw, m1, sin, ALU.mult))
                dve.wait_ge(y_done, i * PER_QUAD + (j + 1))
                dve.wait_ge(fin_done, i * PER_QUAD + (j + 1))
                TT(hs[:, p, 0, :], m2[:, 0, :], gw[:, 1, :], ALU.subtract)
                TT(hs[:, p, 1, :], m2[:, 1, :], gw[:, 0, :], ALU.add).then_inc(h_ready, 1)

            with chain.loop(QUADS, 1 + 4 * PER_QUAD) as i:
                quad = bass.ds(i * PER_QUAD, PER_QUAD)
                br = braw.rearrange("p c (j k) -> p c j k", j=PER_QUAD)
                t1 = m1[:, :, 0:P].rearrange("p c (j k) -> p c j k", j=PER_QUAD)
                t2 = m2[:, :, 0:P].rearrange("p c (j k) -> p c j k", j=PER_QUAD)
                dve.wait_ge(b_in, i * 16 + 16)
                dve.wait_ge(h_ready, i * PER_QUAD + 2)
                TT(t1, br, spread(spread(fre[:, quad], 2, 32), 1, 2), ALU.mult)
                link(TT(t2, br, spread(spread(fim[:, quad], 2, 32), 1, 2), ALU.mult))
                dve.wait_ge(bt_done, i)
                TT(bbq[:, 0, :], m1[:, 0, 0:P], m2[:, 1, 0:P], ALU.subtract)
                TT(bbq[:, 1, :], m1[:, 1, 0:P], m2[:, 0, 0:P], ALU.add).then_inc(bb_ready, 1)
                dve.wait_ge(bb_ready, i + 1)
                for j in range(PER_QUAD):
                    states(i, j)
                dve.wait_ge(y_done, i * PER_QUAD + (PER_QUAD + 2))
                dve.wait_ge(g_ready, i)
                STT(ypre, uq, dskip[:, bass.ds(i, 1)], ps[:, 6, 0:T], ALU.mult, ALU.add).then_inc(ypre_ready, 1)

            for m in range(QUADS):
                dve.wait_ge(sig_ready, m + 1)
                if m == 0:
                    dve.wait_ge(fin_done, STILES + 2)
                TT(so[:, m, :], gT[:, m, :], sig[:, m % 2, :], ALU.mult).then_inc(so_ready, 1)

            dve.wait_ge(att_in, 4 * 16)
            with chain.loop(NJ, 7) as j:
                link(dve.tensor_copy(nsl, slopes[:, j, :]))

                def negative_max(w, s, rows):
                    dve.tensor_reduce(st[0:rows, w, 0:1], s, AX.XY if len(s.shape) == 3 else AX.X, ALU.max,
                                      negate=True).then_inc(mx, 1)

                def normalise(w, s, rows):
                    dve.wait_ge(ex, j * 3 + (w + 1))
                    link(dve.reciprocal(st[0:rows, w, 2:3], st[0:rows, w, 1:2]))
                    TS(s, s, st[0:rows, w, 2:3], None, ALU.mult).then_inc(p_ready, 1)

                dve.wait_ge(sc0_done, j + 1)
                dve.wait_ge(pt_done, j * 3)
                for g in range(NG):
                    ins = STT(s0[:, g, :], dist[:, g, P:SEQ], nsl[:, g:g + 1], ps[:, 3, g * P:(g + 1) * P],
                              ALU.mult, ALU.add)
                link(ins)
                negative_max(0, s0, P)
                dve.wait_ge(sc1_done, j + 1)
                for g in range(NG):
                    ins = STT(s1[:, g, :], dist[:, g, :], nsl[:, g:g + 1],
                              ps[:, 4 + g // 2, (g % 2) * SEQ:(g % 2 + 1) * SEQ], ALU.mult, ALU.add)
                link(ins)
                negative_max(1, s1, P)
                normalise(0, s0, P)
                normalise(1, s1, P)
                dve.wait_ge(k_used, j * NB + (NB + 2))
                R = SAMPLE
                for g in range(NG):
                    STT(sc[0:R, g, :], dist_c[0:R, g, :], nsl[0:R, g:g + 1], ps[0:R, 6, g * P:(g + 1) * P],
                        ALU.mult, ALU.add)
                    ins = STT(sn[0:R, g, :], dist_n[0:R, g, :], nsl[0:R, g:g + 1], ps[0:R, 7, g * R:(g + 1) * R],
                              ALU.mult, ALU.add)
                link(ins)
                negative_max(2, scn[0:R], R)
                normalise(2, scn[0:R], R)

            with chain.loop(KT // 4, 4) as i:
                for k in range(4):
                    p = k % 2
                    dve.wait_ge(sg_ready, i * 4 + (k + 1))
                    dve.wait_ge(used, i * 12 + (N_GLU + 3 * k + 3))
                    link(TT(gp[:, p], gsg[:, p], ps[:, 4 * p + 2:4 * p + 4, 0:T], ALU.mult))
                    TT(mT[:, i * 4 + k, :], gp[:, p, 0, :], gp[:, p, 1, :], ALU.add).then_inc(merged, 1)
            with dve.Fori(0, KT // RING) as i:
                for k in range(RING):
                    dve.wait_ge(used, i * RING + (N_MERGE + k + 1))
                    STT(xT[:, i * RING + k, :], xT[:, i * RING + k, :], ALPHA, ps[:, k, 0:T],
                        ALU.mult, ALU.add).then_inc(resid, 1)
            dve.wait_ge(mean_done, 1)
            TT(xT, xT, spread(ps[:, 4, 0:T], 1, KT), ALU.subtract).then_inc(cent, 1)
            dve.wait_ge(var_done, 1)
            link(TS(var, ps[:, 5, 0:T], EPS, None, ALU.add))
            dve.reciprocal(rv, var).then_inc(rv_ready, 1)
            dve.wait_ge(rs_ready, 1)
            link(TT(nt, var, rs, ALU.mult))
            link(TT(nt, nt, rs, ALU.mult))
            link(TS(nt, nt, -0.5, 1.5, ALU.mult, ALU.add))
            link(TT(rs, rs, nt, ALU.mult))
            TT(xT, xT, spread(rs, 1, KT), ALU.mult).then_inc(nrm, 1)

            dve.wait_ge(peer_in, 2 * 16)
            dve.wait_ge(sx_ready, KT + 2)
            dve.wait_ge(stored, 2 * 16)
            TS(adiag, ident, ALPHA, None, ALU.mult).then_inc(seeded, 1)
            for a, rows in TOK_TILES:
                R = slice(0, rows)
                with chain.loop(PH, 14) as h:
                    link(dve.tensor_copy(sc2[R], sx[R, a, bass.ds(h * 2, 2), :]))
                    hold(dve)
                    for lo in (0, 8):
                        for s in range(2):
                            ins = dve.max(v16[R, s, lo:lo + 8], sc2[R, s, :])
                        link(ins)
                        hold(dve)
                        for s in range(2):
                            ins = dve.max_index(i16[R, s, lo:lo + 8].bitcast(U32), v16[R, s, lo:lo + 8], sc2[R, s, :])
                        if lo == 0:
                            for s in range(2):
                                ins = dve.match_replace(sc2[R, s, :], v16[R, s, 0:8], sc2[R, s, :], NEG)
                            link(ins)
                            hold(dve)
                    link(TT(cand[R], spread(v16[R, 0, :], 2, PTOP), spread(v16[R, 1, :], 1, PTOP), ALU.add))
                    cflat = cand[R].rearrange("p a b -> p (a b)")
                    for lo in (0, 8):
                        hold(dve)
                        link(dve.max(t16[R, lo:lo + 8], cflat))
                        hold(dve)
                        ins = dve.max_index(p16[R, lo:lo + 8].bitcast(U32), t16[R, lo:lo + 8], cflat)
                        if lo == 0:
                            link(dve.match_replace(cflat, t16[R, 0:8], cflat, NEG))
                    link(ins)
                    TS(gate[R, a, bass.ds(h * PTOP, PTOP)], t16[R], t16[R, 0:1], None, ALU.subtract)
                    dve.tensor_copy(if16[R], i16[R].bitcast(U32))
                    TS(ab[R, 0, :].bitcast(U32), p16[R].bitcast(U32), 4, None, ALU.logical_shift_right)
                    link(TS(ab[R, 1, :].bitcast(U32), p16[R].bitcast(U32), PTOP - 1, None, ALU.bitwise_and))
                    link(dve.tensor_copy(abf[R], ab[R].bitcast(U32)))
                    io = spread(spread(iota[R], 1, PTOP), 1, 2)
                    link(TT(oh[R], spread(abf[R], 3, PTOP), io, ALU.is_equal))
                    link(TT(oh[R], oh[R], spread(if16[R], 2, PTOP), ALU.mult))
                    link(dve.tensor_reduce(e12[R], oh[R], AX.X, ALU.add))
                    STT(eidx[R, a, bass.ds(h * PTOP, PTOP)].bitcast(I32), e12[R, 0, :], float(PK), e12[R, 1, :],
                        ALU.mult, ALU.add)
                dve.sem_inc(gd_ready, 1)
                dve.wait_ge(ge_ready, a + 1)
                gv = gate[R, a, :].rearrange("p (h k) -> p h k", h=PH)
                link(dve.tensor_reduce(gsum[R], gv, AX.X, ALU.add))
                link(dve.reciprocal(gsum[R], gsum[R]))
                TT(gv, gv, spread(gsum[R], 2, PTOP), ALU.mult).then_inc(topk_done, 1)

            dve.wait_ge(topk_done, 3)
            dve.wait_ge(ht_ready, 12)
            for a, rows in TOK_TILES:
                R = slice(0, rows)
                with chain.loop(EXPERTS // (2 * CHUNK), 2) as i:
                    for c in range(2):
                        for k in range(CHUNK):
                            dve.wait_ge(usem[k], i * 32 + 16 * (a * EXPERTS // URING + c + 1))
                            dve.tensor_tensor_reduce(ub[k][R], ub[k][R], htok[R, a, :], 1.0, 0.0, ALU.mult,
                                                     ALU.add, act_[R, c, k:k + 1]).then_inc(u_used, 1)
                        dve.wait_ge(gelu_ready, i * 2 + (a * EXPERTS // CHUNK + c + 1))
                        link(TT(wgt[R, c, :], gel[R, c, :], gate[R, a, bass.ds(i * 8 + c * CHUNK, CHUNK)], ALU.mult))
                        for k in range(CHUNK):
                            n = a * EXPERTS + c * CHUNK + k
                            dve.wait_ge(v_used2, i * 8 + (n + 1 + VRING - CHUNK))
                            TS(diag[R, k, 0:rows], ident[R, 0:rows], wgt[R, c, k:k + 1], None,
                               ALU.mult).then_inc(dg_ready, 1)
                f = ps[R, 4 * (a % 2):4 * (a % 2) + 4, :]
                dve.wait_ge(v_used2, VRING + (a + 1) * EXPERTS)
                for q in range(4):
                    ins = dve.bn_stats(bns[R, q, :], f[:, q, :])
                link(ins)
                link(dve.bn_aggr(bna[R], bns[R].rearrange("p a b -> p (a b)")))
                link(TS(lnr[R, 2:3], bna[R, 1:2], EPS, None, ALU.add))
                dve.reciprocal(lnr[R, 0:1], lnr[R, 2:3]).then_inc(l2_sq, 1)
                dve.wait_ge(rs_ready, a + 2)
                link(TT(lnr[R, 3:4], lnr[R, 2:3], lnr[R, 1:2], ALU.mult))
                link(TT(lnr[R, 3:4], lnr[R, 3:4], lnr[R, 1:2], ALU.mult))
                link(TS(lnr[R, 3:4], lnr[R, 3:4], -0.5, 1.5, ALU.mult, ALU.add))
                link(TT(lnr[R, 1:2], lnr[R, 1:2], lnr[R, 3:4], ALU.mult))
                if a == 0:
                    dve.wait_ge(l2_in, 2 * 16)
                else:
                    dve.wait_ge(y_out, 16 * a)
                y4 = yt[R].rearrange("p (q n) -> p q n", q=4)
                link(TS(y4, f, bna[R, 0:1], lnr[R, 1:2], ALU.subtract, ALU.mult))
                link(TT(yt[R], yt[R], g2[R], ALU.mult))
                TT(yt[R], yt[R], b2[R], ALU.add).then_inc(y_ready, 1)


def tiles_of(w, k, n):
    K, N = w.shape
    assert K == k * P
    return np.ascontiguousarray(w.reshape(k, P, N // n, n).transpose(2, 1, 0, 3))


def constants():
    f = np.float32
    slopes = -(2.0 ** (-8.0 * np.arange(1, NHEAD + 1) / NHEAD))
    dist = np.full((P, NG, SEQ), FAR)
    dist_c = np.full((SAMPLE, NG, P), FAR)
    dist_n = np.full((SAMPLE, NG, SAMPLE), FAR)
    for g, (w, d) in enumerate(zip(WINDOWS, DILS)):
        off = (P + np.arange(P))[:, None] - np.arange(SEQ)[None, :]
        ok = (off >= 0) & (off <= w) & (off % d == 0)
        dist[:, g] = np.where(ok, off, FAR)
        for b in range(NB):
            for i in range(NS):
                row = i % CLASSES[g] + d * np.arange(P)
                off = w + i - row
                dist_c[b * NS + i, g] = np.where(off <= w, off, FAR)
                for l in range(i + 1):
                    if (i - l) % d == 0:
                        dist_n[b * NS + i, g, b * NS + l] = i - l
    mask = np.ones((P, T))
    mask[:, SEQ::NS] = 0
    mask[:, 0] = 0
    return {
        "ident": np.eye(P, dtype=f), "ones": np.full((P, P), 1.0 / D, f), "mask": mask.astype(f),
        "iota": np.tile(np.arange(PTOP, dtype=f), (P, 1)),
        "slopes": np.tile(slopes.reshape(NG, NJ).T.astype(f)[None], (P, 1, 1)),
        "dist": dist.astype(f), "dist_c": dist_c.astype(f), "dist_n": dist_n.astype(f),
    }


def lay_out(x):
    tok = np.concatenate([x["x_prompt"].reshape(SEQ, D), x["x_sample"].reshape(SAMPLE, D)])
    out = constants()
    out["xT"] = tok.T.reshape(KT, P, T).transpose(1, 0, 2)
    w = tiles_of(x["w_in"], KT, P)
    u, heads, gs, ga = w[:QUADS], w[QUADS:QUADS + QKV_TILES], w[N_X:N_X + KT], w[N_X + KT:]
    order = list(heads[:N_PRE])
    for q in range(QUADS):
        order += [u[q]] + list(heads[N_PRE + 3 * q:N_PRE + 3 * q + 3])
    order += list(heads[N_PRE + 3 * QUADS:])
    out["w_x"] = np.stack(order).reshape(N_X, P, WSLOT)
    glu = tiles_of(x["ssm_w_glu"], QUADS, P)
    out["w_glu"] = glu.reshape(QUADS // 2, 2, P, QUADS * P).transpose(0, 2, 1, 3).reshape(QUADS // 2, P, WSLOT)
    bs, ba = tiles_of(x["w_branch_ssm"], QUADS, P), tiles_of(x["w_branch_attn"], NJ, P)
    branch = np.zeros((KT, P, KT, P), np.float32)
    branch[:, :, :QUADS] = bs
    branch[:, :, QUADS:QUADS + NJ] = ba
    out["w_merge"] = np.stack([gs, ga, branch], axis=1).reshape(3 * KT, P, WSLOT)
    out["w_op"] = np.concatenate([tiles_of(x["w_out"], KT, P), tiles_of(x["peer_w_q"], KT, P)]).reshape(2 * KT, P, WSLOT)

    def states(a):
        return np.moveaxis(a.reshape(STILES, P, *a.shape[2:]), 1, 0)

    out["log_dt"] = states(np.repeat(x["ssm_log_dt"][:, None], 64, axis=1))
    out["a_re"], out["a_im"] = states(x["ssm_a_re"]), states(x["ssm_a_im"])
    out["h0"] = states(np.transpose(x["state_ssm"], (1, 2, 3, 0)))
    out["dskip"] = x["ssm_d"].reshape(QUADS, P).T

    def blocks(re, im):
        both = np.stack([re, im], axis=2).reshape(QUADS, PER_QUAD, 2, 64, 2, 16)
        o = np.zeros((QUADS + 1, 2, 64, 2, PER_QUAD, 2, 16), np.float32)
        for half in range(2):
            o[:QUADS, half, :, :, :, half] = both[:, :, half].transpose(0, 2, 3, 1, 4)
        return o.reshape(QUADS + 1, P, 2, P)

    out["ssm_b"] = blocks(x["ssm_b_re"], x["ssm_b_im"])
    out["ssm_c"] = blocks(x["ssm_c_re"].transpose(0, 2, 1), x["ssm_c_im"].transpose(0, 2, 1))

    ks, vs = [], []
    for g, (name, d) in enumerate(zip(("cache_kv_w128", "cache_kv_w512", "cache_kv_w2048"), DILS)):
        c = x[name].reshape(NB, P, d, 2, NJ, HD)[:, :, :CLASSES[g]]
        ks.append(c[:, :, :, 0].transpose(3, 0, 4, 2, 1))
        vs.append(c[:, :, :, 1].transpose(3, 0, 1, 2, 4))
    out["k_cache"] = np.concatenate(ks, axis=3).reshape(NJ * NB, P, CBLK, P)
    out["v_cache"] = np.concatenate(vs, axis=3).reshape(NJ * NB, P, CBLK, P)
    out["ln1"] = np.stack([x["ln1_g"].reshape(KT, P).T, x["ln1_b"].reshape(KT, P).T], axis=1)
    out["ln2"] = np.stack([np.tile(x["ln2_g"], (P, 1)), np.tile(x["ln2_b"], (P, 1))])
    out["sub_keys"] = np.stack([x["peer_sub_keys_1"].T, x["peer_sub_keys_2"].T], axis=1)
    out["peer_u"], out["peer_v"] = x["peer_u"], x["peer_v"]
    return {k: np.ascontiguousarray(v) for k, v in out.items()}


OUTS = {"y": (T, D), "kv": (P, 2 * NHEAD, T), "ssm": (P, STILES, 2, NFIN)}


def kernel(**inputs):
    import concourse.bacc as bacc
    from concourse.bass_utils import run_bass_kernel_spmd

    arrays = lay_out({k: np.asarray(v) for k, v in inputs.items()})
    nc = bacc.Bacc("TRN2", target_bir_lowering=False, num_devices=1)
    A = {k: nc.dram_tensor(f"in_{k}", v.shape, F32, kind="ExternalInput").ap() for k, v in arrays.items()}
    O = {k: nc.dram_tensor(f"out_{k}", s, F32, kind="ExternalOutput").ap() for k, s in OUTS.items()}
    layer_kernel(nc, A, O)
    r = run_bass_kernel_spmd(nc, [{f"in_{k}": v for k, v in arrays.items()}], core_ids=[0]).results[0]
    y, kv, ssm = r["out_y"], r["out_kv"], r["out_ssm"]
    kv = kv.reshape(HD, 2, NG, NJ, T).transpose(2, 4, 1, 3, 0)
    prompt = [kv[g, max(0, SEQ - w):SEQ][None] for g, w in enumerate(WINDOWS)]
    sample = [kv[g, SEQ:].reshape(NB, NS, 2, NJ, HD) for g in range(NG)]
    ssm = ssm.reshape(2, 64, STILES, 2, NFIN).transpose(4, 2, 0, 1, 3).reshape(NFIN, 64, 64, 2)
    return (y[:SEQ][None], y[SEQ:].reshape(NB, NS, D), *prompt, ssm[:1], *sample, ssm[1:])
```

```python
from contextlib import ExitStack, contextmanager

import numpy as np

import concourse.bass as bass
from concourse import mybir

F32 = mybir.dt.float32
I32 = mybir.dt.int32
U32 = mybir.dt.uint32
ALU = mybir.AluOpType
ACT = mybir.ActivationFunctionType
AX = mybir.AxisListType

P = 128
D = 2048
KT = D // P
SEQ = 256
NB, NS = 8, 8
SAMPLE = NB * NS
T = SEQ + SAMPLE
PT = SEQ // P
TOK_TILES = [(0, P), (1, P), (2, SAMPLE)]

WS = 1024
QUADS = WS // P
STILES = 64 * 64 // P
PER_QUAD = STILES // QUADS
NFIN = 1 + NB

HD = 128
NG, NJ = 3, 4
WINDOWS, DILS = (128, 512, 2048), (1, 4, 16)
NHEAD = NG * NJ
QKV_TILES = 3 * NHEAD
CLASSES = (1, 4, NS)
CBLK = sum(CLASSES)
CSLOTS = 2
FAR = 1.0e30

PH, PK, PTOP = 8, 128, 16
EXPERTS = PH * PTOP
TILE_HEADS = (PH, PH, PH // 2)
CHUNK = 4
URING, VRING = 4, 8

ALPHA = 2.0 ** 0.25
EPS = 1e-5
NEG = -3.0e38
ROUND = 1.5 * 2.0 ** 23
TWO_PI_HI = 6.28125
TWO_PI_LO = 2.0 * float(np.pi) - TWO_PI_HI
PI_SAFE = 3.1415925

RING = 4
WSLOT = KT * P
PER_HEAD = 3 * NG
N_PRE = 4
N_SSM = N_PRE + 2 * QUADS
FILL = 8
O_FILL = N_PRE + QUADS
N_X = QUADS + QKV_TILES
N_GLU = N_X + QUADS // 2
N_MERGE = N_GLU + 3 * KT
N_OUT = N_MERGE + KT
N_ALL = N_OUT + KT
assert N_SSM + (NJ - 1) * FILL == N_X


class Chain:

    def __init__(self, eng, sem):
        self.eng, self.sem, self.done, self.base, self.i, self.per = eng, sem, 0, 0, None, 0

    def link(self, ins):
        self.done += 1
        ins.then_inc(self.sem, 1)
        if self.i is None:
            self.eng.wait_ge(self.sem, self.done)
        else:
            self.eng.wait_ge(self.sem, self.i * self.per + self.done)

    @contextmanager
    def loop(self, steps, per):
        base = self.done
        with self.eng.Fori(0, steps) as i:
            self.i, self.per = i, per
            yield i
        assert self.done - base == per, (self.done - base, per)
        self.i, self.done = None, base + steps * per


class Region:

    def __init__(self, arena, lo, hi):
        self.arena, self.at, self.hi = arena, lo, hi

    def take(self, *shape):
        n = int(np.prod(shape))
        lo = self.at
        self.at += n + n % 2
        assert self.at <= self.hi, (self.at, self.hi, shape)
        v = self.arena[:, lo:lo + n]
        if len(shape) > 1:
            c = "abcd"[:len(shape)]
            v = v.rearrange(f"p ({' '.join(c)}) -> p {' '.join(c)}", **dict(zip(c[1:], shape[1:])))
        return v


def spread(ap, dim, n):
    shape = list(ap.shape)
    return ap.unsqueeze(dim).to_broadcast(shape[:dim] + [n] + shape[dim:])


def layer_kernel(nc, A, O):
    with ExitStack() as ctx:
        COLS = 53200
        arena = ctx.enter_context(nc.sbuf_tensor("arena", [P, COLS], F32))
        ps = ctx.enter_context(nc.psum_tensor("ps", [P, 8, 512], F32))

        def sem(name):
            return ctx.enter_context(nc.semaphore(name))

        r = Region(arena, 0, COLS)
        xT = r.take(KT, T)
        ring = r.take(RING, WSLOT)
        ident = r.take(P)
        lo_qkv = r.at
        qkv = r.take(QKV_TILES, T)
        lo_g = r.at
        gT = r.take(QUADS, T)
        lo_a = r.at

        r = Region(arena, lo_a, COLS)
        rot = r.take(2, STILES, SEQ)
        hi_rot = r.at
        mag = r.take(STILES)
        fre = r.take(STILES)
        fim = r.take(STILES)
        h0m = r.take(STILES, 2, NB)
        rotx = r.take(2, 2, T)
        magx = r.take(2, T)
        mask = r.take(T)
        lo_m = r.at
        m1 = r.take(2, T)
        m2 = r.take(2, T)
        gw = r.take(2, T)
        hs = r.take(2, 2, T)
        hi_m = r.at
        uq = r.take(T)
        ypre = r.take(T)
        braw = r.take(2, P)
        craw = r.take(2, P)
        bbq = r.take(2, P)
        btq = r.take(2, P)
        ccq = r.take(2, P)
        dskip = r.take(QUADS)
        lo_fin = COLS - STILES * 2 * NFIN
        assert r.at <= lo_fin
        fin = Region(arena, lo_fin, COLS).take(STILES, 2, NFIN)
        r = Region(arena, lo_qkv + 8 * T, lo_g)
        half = r.take(2, STILES, SEQ // 2)
        r = Region(arena, lo_m, hi_m)
        s_h0 = r.take(STILES, 2, NB)
        s_dt, s_are, s_aim, s_x, s_n, s_r, s_u, s_sin, s_cos, s_br, s_bi, s_den, s_p, s_q = (
            r.take(STILES) for _ in range(14))

        r = Region(arena, lo_a, hi_rot)
        kc = r.take(CSLOTS, CBLK, P)
        vc = r.take(CSLOTS, CBLK, P)
        lo_qz = r.at
        qz0 = r.take(NB * 72)
        qz1 = r.take(NB * 264)
        qz2 = r.take(SAMPLE * 65)
        hi_qz = r.at
        qs = r.take(NG, T)
        vs = r.take(NG, T)
        pt1 = r.take(NG * PT, P)
        ptc = r.take(NG, SAMPLE)
        r = Region(arena, hi_rot, COLS)
        so = r.take(QUADS, T)
        dist = r.take(NG, SEQ)
        dist_c = r.take(NG, P)
        dist_n = r.take(NG, SAMPLE)
        slopes = r.take(NJ, NG)
        nsl = r.take(NG)
        vtok = r.take(PT, NG, P)
        vnew = r.take(NG, P)
        s0 = r.take(NG, P)
        sc = r.take(NG, P)
        sn = r.take(NG, SAMPLE)
        scn = arena[:, r.at - NG * (P + SAMPLE):r.at]
        st = r.take(3, 4)
        sig = r.take(2, T)
        s1 = r.take(NG, SEQ)
        pt0 = r.take(NG, P)
        ptn = r.take(NG, SAMPLE)
        assert r.at <= lo_fin

        r = Region(arena, lo_a, hi_rot)
        mT = r.take(KT, T)
        gsg = r.take(2, 2, T)
        gp = r.take(2, 2, T)
        sq = r.take(KT, T)
        var, rv, rs, nt = (r.take(T) for _ in range(4))
        ln1 = r.take(2, KT)
        onesm = r.take(P)

        r = Region(arena, lo_qkv, lo_a)
        htok = r.take(3, D)
        v16 = r.take(2, PTOP)
        i16 = r.take(2, PTOP)
        if16 = r.take(2, PTOP)
        t16 = r.take(PTOP)
        p16 = r.take(PTOP)
        ab = r.take(2, PTOP)
        abf = r.take(2, PTOP)
        e12 = r.take(2, PTOP)
        iota = r.take(PTOP)
        gsum = r.take(PH)
        oh = r.take(2, PTOP, PTOP)
        cand = r.take(PTOP, PTOP)
        sc2 = r.take(2, PK)
        eidx = r.take(3, EXPERTS)
        gate = r.take(3, EXPERTS)
        idxs = r.take(2, 2 * CHUNK)
        act_ = r.take(2, CHUNK)
        gel = r.take(2, CHUNK)
        wgt = r.take(2, CHUNK)
        bns = r.take(4, 6)
        bna = r.take(2)
        lnr = r.take(4)
        r = Region(arena, lo_a, COLS)
        sx = r.take(3, 2 * PH, PK)
        qh = r.take(2, T)
        k12 = r.take(2, PK)
        diag = r.take(CHUNK, P)
        adiag = r.take(P)
        pairs = r.take(SAMPLE)
        g2 = r.take(D)
        b2 = r.take(D)
        bufs = [r.take(D) for _ in range(6)]
        r = Region(arena, 0, KT * T + RING * WSLOT)
        bufs += [r.take(D) for _ in range(6)]
        ub, vb = bufs[:URING], bufs[URING:]
        assert len(vb) == VRING
        yt = Region(arena, lo_a, COLS).take(D)

        wsem = [sem(f"weights_{k}") for k in range(RING)]
        used = sem("tile_multiplied")
        evac = sem("tile_evacuated")
        x_in = [sem(f"x_in_{c}") for c in range(4)]
        small_in = sem("ssm_small_in")
        dvc, acc, poc = sem("dve_chain"), sem("act_chain"), sem("pool_chain")
        su_dt, su_trig, su_rot, su_act = sem("dt"), sem("trig"), sem("tables"), sem("setup_act")
        pq_done = sem("queries_done")
        su_arg = sem("trig_args")
        idx_ready = sem("expert_indices")
        b_in, c_in = sem("b_in"), sem("c_in")
        bb_ready, bt_done, bt_ready = sem("b_scaled"), sem("b_transposed"), sem("b_staged")
        cc_ready = sem("c_staged")
        bu_ready, bu_free = sem("bu_ready"), sem("bu_free")
        rotx_ready, magx_ready = sem("rotx_ready"), sem("magx_ready")
        h_ready, y_done, fin_done = sem("h_ready"), sem("y_done"), sem("final_copied")
        ypre_ready, g_ready = sem("ypre_ready"), sem("gelu_ready")
        stored = sem("outputs_stored")
        sig_ready, so_ready, glu_done = sem("glu_sigmoid"), sem("s5_out"), sem("glu_multiplied")
        att_in = sem("attention_constants")
        kcs = [sem(f"k_cache_{k}") for k in range(CSLOTS)]
        vcs = [sem(f"v_cache_{k}") for k in range(CSLOTS)]
        k_used, v_used = sem("k_cache_used"), sem("v_cache_used")
        qz_zero, qs_ready, vs_ready, qz_ready = sem("qz_zero"), sem("qs"), sem("vs"), sem("qz")
        nsl_ready = sem("slopes_staged")
        vt_done, vt_ready = sem("v_transposed"), sem("v_token_major")
        sc0_done, sc1_done, scs_done = sem("scores_0"), sem("scores_1"), sem("scores_sample")
        mx, ex = sem("softmax_max"), sem("softmax_exp")
        p_ready = sem("probabilities")
        pt_done, pt_ready = sem("p_transposed"), sem("p_staged")
        o_done, o_ready = sem("attended"), sem("attention_out")
        sg_ready, merged = sem("gates_sigmoid"), sem("merged")
        ln_in = sem("ln1_in")
        resid, mean_done, cent, sq_ready, var_done = (
            sem("residual"), sem("mean"), sem("centred"), sem("squared"), sem("variance"))
        rv_ready, rs_ready, nrm, h_done = sem("rv"), sem("rsqrt"), sem("normed"), sem("h_feature")
        qh_ready, psc_done, sx_ready = sem("query_staged"), sem("subkey_scores"), sem("scores_out")
        packed = sem("sample_heads_packed")
        ht_done, ht_ready = sem("h_transposed"), sem("h_token_major")
        peer_in = sem("peer_small_in")
        gd_ready, ge_ready, topk_done = sem("gate_diff"), sem("gate_exp"), sem("topk")
        usem = [sem(f"u_rows_{k}") for k in range(URING)]
        vsem = [sem(f"v_rows_{k}") for k in range(VRING)]
        u_used, v_used2 = sem("u_rows_used"), sem("v_rows_used")
        gelu_ready, dg_ready = sem("expert_gelu"), sem("diagonals")
        seeded = sem("alpha_h_seeded")
        l2_in, l2_sq, y_ready, y_out = sem("ln2_in"), sem("ln2_sqrt"), sem("y_ready"), sem("y_out")

        passed = sem("waits_passed")

        def hold(eng):
            eng.sem_inc(passed, 1)

        def slot(k):
            return ring[:, k, :].rearrange("p (k m) -> p k m", m=P)

        block = ctx.enter_context(nc.Block())

        @block.sync
        def _(sp):
            def load(k, src, cols=WSLOT):
                sp.dma_start(ring[:, k, 0:cols], src).then_inc(wsem[k], 16)

            def w(n, k=None):
                load(n % RING, A["w"][n])

            for c in range(4):
                sp.dma_start(xT[:, 4 * c:4 * c + 4, :], A["xT"][:, 4 * c:4 * c + 4, :]).then_inc(x_in[c], 16)
                if c == 0:
                    w(0)
            for dst, name in ((s_dt, "log_dt"), (s_are, "a_re"), (s_aim, "a_im"),
                              (s_h0, "h0"), (mask, "mask"), (dskip, "dskip"), (ident, "ident")):
                sp.dma_start(dst, A[name]).then_inc(small_in, 16)
            for n in range(1, RING):
                w(n)
            sp.dma_start(braw, A["ssm_b"][0]).then_inc(b_in, 16)
            sp.dma_start(craw, A["ssm_c"][0]).then_inc(c_in, 16)
            with sp.Fori(0, QUADS // 2) as i:
                for k in range(RING):
                    sp.wait_ge(used, i * RING + (k + 1))
                    load(k, A["w"][i * RING + (N_PRE + k)])
                    if k % 2 == 1:
                        q = i * 2 + k // 2
                        sp.wait_ge(bb_ready, q + 1)
                        sp.dma_start(braw, A["ssm_b"][q + 1]).then_inc(b_in, 16)
                        sp.wait_ge(cc_ready, q + 1)
                        sp.dma_start(craw, A["ssm_c"][q + 1]).then_inc(c_in, 16)
            for n in range(N_SSM, N_SSM + RING - 1):
                sp.wait_ge(used, n - RING + 1)
                w(n)
            sp.wait_ge(fin_done, STILES + 2)
            sp.dma_start(O["ssm"], fin).then_inc(stored, 16)
            sp.wait_ge(g_ready, QUADS + 1)
            for dst, name in ((dist, "dist"), (slopes, "slopes")):
                sp.dma_start(dst, A[name]).then_inc(att_in, 16)
            sp.dma_start(dist_c[0:SAMPLE], A["dist_c"]).then_inc(att_in, 16)
            sp.dma_start(dist_n[0:SAMPLE], A["dist_n"]).then_inc(att_in, 16)

            def caches(j, bs, name, buf, sems, used_):
                for b in bs:
                    sp.wait_ge(used_, j * NB + (b + 1))
                    sp.dma_start(buf[:, b % CSLOTS], A[name][j * NB + b]).then_inc(sems[b % CSLOTS], 16)

            def keys(j, *bs):
                caches(j, bs, "k_cache", kc, kcs, k_used)

            def values(j, *bs):
                caches(j, bs, "v_cache", vc, vcs, v_used)

            def fill(j, x):
                sp.wait_ge(used, j * FILL + (N_SSM + x - RING + 1))
                load(x % RING, A["w"][j * FILL + (N_SSM + x)])

            with sp.Fori(0, NJ - 1) as j:
                keys(j, 0, 1)
                values(j, 0, 1)
                fill(j, 3)
                keys(j, 2, 3)
                fill(j, 4)
                keys(j, 4, 5)
                fill(j, 5)
                keys(j, 6, 7)
                fill(j, 6)
                values(j, 2, 3)
                fill(j, 7)
                values(j, 4, 5)
                fill(j, 8)
                values(j, 6, 7)
                fill(j, 9)
                fill(j, 10)
            j = NJ - 1
            keys(j, 0, 1)
            values(j, 0, 1)
            fill(j, 3)
            keys(j, 2, 3, 4, 5)
            fill(j, 4)
            keys(j, 6, 7)
            values(j, 2, 3)
            fill(j, 5)
            values(j, 4, 5)
            fill(j, 6)
            values(j, 6, 7)
            fill(j, 7)
            sp.wait_ge(evac, N_X)
            for j in range(NJ):
                sp.dma_start(O["kv"][:, 2 * NG * j:2 * NG * (j + 1), :],
                             qkv[:, PER_HEAD * j + NG:PER_HEAD * (j + 1), :]).then_inc(stored, 16)
            assert (N_MERGE - N_GLU - RING) % (2 * RING) == RING and 3 * KT % RING == 0
            with sp.Fori(0, (N_MERGE - N_GLU - RING) // RING) as i:
                for k in range(RING):
                    sp.wait_ge(used, i * RING + (N_GLU + k + 1))
                    load(k, A["w"][i * RING + (N_GLU + RING + k)])
            sp.wait_ge(o_ready, NJ + 1)
            sp.dma_start(ln1, A["ln1"]).then_inc(ln_in, 16)
            sp.dma_start(onesm, A["ones"]).then_inc(ln_in, 16)
            steps = KT // RING + 1
            with sp.Fori(0, steps) as i:
                for k in range(RING):
                    sp.wait_ge(used, i * RING + (N_MERGE - RING + k + 1))
                    load(k, A["w"][i * RING + (N_MERGE + k)])
            sp.wait_ge(h_done, KT)
            sp.dma_start(k12, A["sub_keys"]).then_inc(peer_in, 16)
            sp.dma_start(iota, A["iota"]).then_inc(peer_in, 16)
            sp.dma_start(g2, A["ln2"][0]).then_inc(l2_in, 16)
            sp.dma_start(b2, A["ln2"][1]).then_inc(l2_in, 16)
            with sp.Fori(0, 2 * KT // RING - steps) as i:
                for k in range(RING):
                    sp.wait_ge(used, i * RING + (N_MERGE + (steps - 1) * RING + k + 1))
                    load(k, A["w"][i * RING + (N_MERGE + steps * RING + k)])
            sp.wait_ge(sx_ready, KT + 2)
            sp.dma_start(sx[SAMPLE:P, PT, 0:PH, :], sx[0:SAMPLE, PT, PH:2 * PH, :]).then_inc(packed, 16)
            sp.wait_ge(ht_ready, 12)
            sp.dma_start(htok[SAMPLE:P, PT, :], htok[0:SAMPLE, PT, :]).then_inc(packed, 16)
            for a, rows in TOK_TILES:
                sp.wait_ge(y_ready, a + 1)
                sp.dma_start(O["y"][a * P:a * P + rows, :], yt[0:rows, :]).then_inc(y_out, 16)
            sp.wait_ge(stored, (NJ + 1) * 16)
            sp.wait_ge(y_out, 3 * 16)

        @block.tensor
        def _(pe):
            for s, n in ((y_done, 2), (k_used, CSLOTS), (v_used, CSLOTS), (psc_done, 2), (v_used2, VRING),
                         (bt_done, 1), (bu_ready, 1), (vt_done, 1), (pt_done, 1)):
                pe.sem_inc(s, n)

            def matmuls(out, lhs, rhs, n, skip=False):
                for k in range(n):
                    ins = pe.matmul(out, lhs(k), rhs(k), start=(k == 0), stop=(k == n - 1))
                return ins

            def project(k, bank):
                return matmuls(ps[:, bank, 0:T], lambda t: slot(k)[:, t, :], lambda t: xT[:, t, :], KT)

            for n in range(N_PRE):
                pe.wait_ge(wsem[n], 16)
                if n >= 2:
                    pe.wait_ge(evac, n - 1)
                for t in range(KT):
                    if n == 0 and t % 4 == 0:
                        pe.wait_ge(x_in[t // 4], 16)
                    ins = pe.matmul(ps[:, n % 2, 0:T], slot(n)[:, t, :], xT[:, t, :], start=(t == 0), stop=(t == KT - 1))
                ins.then_inc(used, 1)

            def tile(i, k):
                pe.wait_ge(wsem[k], i * 16 + 32)
                pe.wait_ge(evac, i * RING + (N_PRE + k - 1))
                project(k, k % 2).then_inc(used, 1)

            def b_u(i, j):
                pe.wait_ge(bu_free, i * PER_QUAD + (j + 1))
                lo = 32 * j
                for part in range(2):
                    ins = pe.matmul(ps[:, 2 + 2 * (j % 2) + part, 0:T], btq[lo:lo + 32, part, :],
                                    uq[lo:lo + 32, :], start=True, stop=True)
                ins.then_inc(bu_ready, 1)

            def c_h(i, j):
                lo = 32 * j
                pe.wait_ge(h_ready, i * PER_QUAD + (j + 3))
                for part in range(2):
                    ins = pe.matmul(ps[lo:lo + 32, 6, 0:T], ccq[:, part, lo:lo + 32], hs[:, j % 2, part, :],
                                    start=(part == 0), stop=(part == 1))
                ins.then_inc(y_done, 1)

            with pe.Fori(0, QUADS // 2) as i:
                for k in (0, 2):
                    q = i * 2 + k // 2
                    tile(i, k)
                    pe.wait_ge(bb_ready, q + 1)
                    pe.wait_ge(bt_ready, q + 1)
                    for part in range(2):
                        ins = pe.transpose(ps[:, 7, part * P:part * P + P], bbq[:, part, :], ident)
                    ins.then_inc(bt_done, 1)
                    pe.wait_ge(bt_ready, q + 2)
                    pe.wait_ge(evac, q * 2 + (N_PRE + 1))
                    b_u(q, 0)
                    b_u(q, 1)
                    tile(i, k + 1)
                    pe.wait_ge(cc_ready, q + 1)
                    pe.wait_ge(ypre_ready, q + 1)
                    c_h(q, 0)
                    b_u(q, 2)
                    c_h(q, 1)
                    b_u(q, 3)
                    c_h(q, 2)
                    c_h(q, 3)

            def heads_tile(j, f):
                pe.wait_ge(wsem[f % RING], j * (16 * FILL // RING) + 16 * ((N_SSM + f) // RING + 1))
                pe.wait_ge(evac, j * FILL + (N_SSM + f))
                project(f % RING, 7).then_inc(used, 1)

            def gate_tile(j, m):
                k = (N_X + m // 2) % RING
                if m % 2 == 0:
                    pe.wait_ge(wsem[k], 16 * ((N_X + m // 2) // RING + 1))
                if m == 0:
                    pe.wait_ge(g_ready, QUADS + 1)
                    pe.wait_ge(evac, N_X)
                else:
                    pe.wait_ge(sig_ready, m)
                s = slot(k)[:, (m % 2) * QUADS:(m % 2 + 1) * QUADS, :]
                matmuls(ps[:, 7, 0:T], lambda t: s[:, t, :], lambda t: gT[:, t, :],
                        QUADS).then_inc(used if m % 2 else glu_done, 1)

            def attention(j, between):
                pe.wait_ge(vs_ready, j + 1)
                pe.wait_ge(o_ready, j + 1)
                for a in range(PT):
                    for g in range(NG):
                        pe.transpose(ps[:, a, g * P:g * P + P], vs[:, g, a * P:a * P + P], ident)
                for g in range(NG):
                    ins = pe.transpose(ps[0:SAMPLE, 2, g * P:g * P + P], vs[:, g, SEQ:T], ident)
                ins.then_inc(vt_done, 1)
                pe.wait_ge(qs_ready, j + 1)
                for g in range(NG):
                    ins = pe.matmul(ps[:, 3, g * P:g * P + P], qs[:, g, 0:P],
                                    qkv[:, j * PER_HEAD + (NG + g), 0:P],
                                    start=(g == 0), stop=(g == NG - 1), skip_group_check=True)
                ins.then_inc(sc0_done, 1)
                for g in range(NG):
                    pe.matmul(ps[:, 4 + g // 2, (g % 2) * SEQ:(g % 2) * SEQ + SEQ], qs[:, g, P:SEQ],
                              qkv[:, j * PER_HEAD + (NG + g), 0:SEQ],
                              start=(g % 2 == 0), stop=(g > 0), skip_group_check=True)
                for g in range(NG):
                    ins = pe.matmul(ps[0:SAMPLE, 5, SEQ + g * SAMPLE:SEQ + (g + 1) * SAMPLE], qs[:, g, SEQ:T],
                                    qkv[:, j * PER_HEAD + (NG + g), SEQ:T],
                                    start=False, stop=(g == NG - 1), skip_group_check=True)
                ins.then_inc(sc1_done, 1)
                pe.wait_ge(qz_ready, j + 1)
                for b in range(NB):
                    pe.wait_ge(kcs[b % CSLOTS], j * (16 * NB // CSLOTS) + 16 * (b // CSLOTS + 1))
                    blk = 0
                    for g, qz in enumerate((qz0, qz1, qz2)):
                        for c in range(CLASSES[g]):
                            w = 64 * (b * CLASSES[g] + c)
                            ins = pe.matmul(ps[0:SAMPLE, 6, g * P:g * P + P], qz[:, w:w + 64],
                                            kc[:, b % CSLOTS, blk, :], start=(b == 0 and blk == 0),
                                            stop=(b == NB - 1 and blk == CBLK - 1), skip_group_check=True)
                            blk += 1
                    ins.then_inc(k_used, 1)
                    if b % 2 == 1:
                        between(j, b // 2)
                pe.wait_ge(p_ready, j * 3 + 1)
                for g in range(NG):
                    ins = pe.transpose(ps[:, 3, g * P:g * P + P], s0[:, g, :], ident)
                ins.then_inc(pt_done, 1)
                pe.wait_ge(p_ready, j * 3 + 2)
                pe.wait_ge(vt_ready, j + 1)
                for g in range(NG):
                    for a in range(PT):
                        t = g * PT + a
                        ins = pe.transpose(ps[:, (4, 2)[t // 4], (t % 4) * P:(t % 4) * P + P],
                                           s1[:, g, a * P:a * P + P], ident)
                ins.then_inc(pt_done, 1)
                pe.wait_ge(p_ready, j * 3 + 3)
                hold(pe)
                for g in range(NG):
                    pe.transpose(ps[:, 1, g * SAMPLE:(g + 1) * SAMPLE], sc[0:SAMPLE, g, :],
                                 ident[0:SAMPLE, 0:SAMPLE])
                for g in range(NG):
                    ins = pe.transpose(ps[0:SAMPLE, 1, (NG + g) * SAMPLE:(NG + g + 1) * SAMPLE], sn[0:SAMPLE, g, :],
                                       ident[0:SAMPLE, 0:SAMPLE])
                ins.then_inc(pt_done, 1)
                pe.wait_ge(pt_ready, j * 3 + 1)
                for g in range(NG):
                    pe.matmul(ps[:, 0, 0:P], vtok[:, 0, g, :], pt0[:, g, :],
                              start=(g == 0), stop=(g == NG - 1), skip_group_check=True)
                pe.wait_ge(pt_ready, j * 3 + 2)
                for t in range(NG * PT):
                    pe.matmul(ps[:, 0, P:SEQ], vtok[:, t % PT, t // PT, :], pt1[:, t, :],
                              start=False, stop=(t == NG * PT - 1), skip_group_check=True)
                pe.wait_ge(pt_ready, j * 3 + 3)
                hold(pe)
                for g in range(NG):
                    pe.matmul(ps[:, 0, SEQ:T], vnew[0:SAMPLE, g, :], ptn[0:SAMPLE, g, :],
                              start=False, stop=False, skip_group_check=True)
                for b in range(NB):
                    pe.wait_ge(vcs[b % CSLOTS], j * (16 * NB // CSLOTS) + 16 * (b // CSLOTS + 1))
                    blk = 0
                    for g in range(NG):
                        n = CLASSES[g]
                        for c in range(n):
                            lo, hi = b * NS + c, (b + 1) * NS
                            last = b == NB - 1 and blk == CBLK - 1
                            ins = pe.matmul(ps[:, 0, SEQ + lo:SEQ + hi:n], vc[:, b % CSLOTS, blk, :],
                                            ptc[:, g, lo:hi:n], start=False, stop=last, skip_group_check=True)
                            blk += 1
                    ins.then_inc(v_used, 1)
                    if b % 2 == 1:
                        between(j, NB // 2 + b // 2)

            with pe.Fori(0, NJ - 1) as j:
                attention(j, heads_tile)
            attention(NJ - 1, gate_tile)

            def merge_tile(i, k):
                p = 4 * (k % 2)

                def at(t):
                    n = 3 * k + t
                    pe.wait_ge(wsem[n % RING], i * (3 * 16) + 16 * (N_GLU // RING + n // RING + 1))
                    return slot(n % RING)

                s = at(0)
                pe.wait_ge(merged, i * 4 + (k + 1))
                matmuls(ps[:, p, 0:T], lambda t: s[:, t, :], lambda t: xT[:, t, :], KT).then_inc(used, 1)
                s = at(1)
                matmuls(ps[:, p + 1, 0:T], lambda t: s[:, t, :], lambda t: xT[:, t, :], KT).then_inc(used, 1)
                s = at(2)
                matmuls(ps[:, p + 2, 0:T], lambda t: s[:, t, :], lambda t: so[:, t, :], QUADS)
                matmuls(ps[:, p + 3, 0:T], lambda t: s[:, QUADS + t, :], lambda t: qkv[:, PER_HEAD * t, :],
                        NJ).then_inc(used, 1)

            pe.wait_ge(so_ready, QUADS)
            pe.wait_ge(o_ready, NJ + 1)
            with pe.Fori(0, KT // 4) as i:
                for k in range(4):
                    merge_tile(i, k)

            pe.wait_ge(merged, KT + 2)
            with pe.Fori(0, KT // RING) as i:
                for k in range(RING):
                    pe.wait_ge(wsem[k], i * 16 + (16 * (N_MERGE // RING) + 16))
                    pe.wait_ge(resid, i * RING + (k + 1))
                    matmuls(ps[:, k, 0:T], lambda t: slot(k)[:, t, :], lambda t: mT[:, t, :],
                            KT).then_inc(used, 1)
            pe.wait_ge(ln_in, 2 * 16)
            for t in range(KT):
                if t % RING == 0:
                    pe.wait_ge(resid, t + RING + RING)
                ins = pe.matmul(ps[:, 4, 0:T], onesm, xT[:, t, :], start=(t == 0), stop=(t == KT - 1))
            ins.then_inc(mean_done, 1)
            for t in range(KT):
                if t % 4 == 0:
                    pe.wait_ge(sq_ready, t // 4 + 1)
                ins = pe.matmul(ps[:, 5, 0:T], onesm, sq[:, t, :], start=(t == 0), stop=(t == KT - 1))
            ins.then_inc(var_done, 1)

            pe.wait_ge(h_done, KT)
            for a, rows in TOK_TILES:
                for q in range(4):
                    n = 4 * a + q
                    if n >= 4:
                        pe.wait_ge(ht_ready, n - 3)
                    for t in range(4):
                        ins = pe.transpose(ps[0:rows, 4 + q, t * P:(t + 1) * P],
                                           xT[:, 4 * q + t, a * P:a * P + rows], ident)
                    ins.then_inc(ht_done, 1)

            pe.wait_ge(peer_in, 2 * 16)

            def subkey_scores(i, k):
                p = k % 2
                pe.wait_ge(qh_ready, i * RING + (k + 3))
                pe.wait_ge(sx_ready, i * RING + (k + 1))
                for a, rows in TOK_TILES:
                    ins = pe.matmul(ps[0:rows, 2 + p, a * PK:(a + 1) * PK], qh[:, p, a * P:a * P + rows],
                                    k12[:, p, :], start=(a == 0), stop=(a == 2), skip_group_check=True)
                ins.then_inc(psc_done, 1)

            with pe.Fori(0, KT // RING) as i:
                for k in range(RING):
                    pe.wait_ge(wsem[k], i * 16 + (16 * (N_OUT // RING) + 16))
                    pe.wait_ge(qh_ready, i * RING + (k + 1))
                    matmuls(ps[:, k % 2, 0:T], lambda t: slot(k)[:, t, :], lambda t: xT[:, t, :],
                            KT).then_inc(used, 1)
                    if k:
                        subkey_scores(i, k - 1)
                subkey_scores(i, RING - 1)
            pe.nop().then_inc(pq_done, 1)

            pe.wait_ge(ht_ready, 12)
            for a, rows in TOK_TILES:
                b0 = 4 * (a % 2)
                if a == 0:
                    pe.wait_ge(sx_ready, KT + 2)
                if a == 2:
                    pe.wait_ge(y_ready, 1)
                pe.wait_ge(seeded, 1)
                for q in range(4):
                    ins = pe.matmul(ps[0:rows, b0 + q, :], adiag[0:rows, 0:rows], htok[0:rows, a, q * 512:(q + 1) * 512],
                                    start=True, stop=False, skip_group_check=True)
                with pe.Fori(0, TILE_HEADS[a]) as h:
                    for e in range(PTOP):
                        n = a * EXPERTS + e
                        v = e % VRING
                        pe.wait_ge(vsem[v], h * (16 * PTOP // VRING) + 16 * (n // VRING + 1))
                        pe.wait_ge(dg_ready, h * PTOP + (n + 1))
                        hold(pe)
                        for q in range(4):
                            ins = pe.matmul(ps[0:rows, b0 + q, :], diag[:, e % CHUNK, 0:rows],
                                            vb[v][:, q * 512:(q + 1) * 512],
                                            start=False, stop=True, skip_group_check=True)
                        ins.then_inc(v_used2, 1)

        @block.scalar
        def _(act):
            for s, n in ((qh_ready, 2), (sx_ready, 2), (bt_ready, 1), (g_ready, 1), (o_ready, 1)):
                act.sem_inc(s, n)
            act.wait_ge(small_in, 7 * 16)
            act.activation(s_dt, s_dt, ACT.Exp).then_inc(su_dt, 1)
            act.wait_ge(su_arg, 1)
            act.activation(mag, s_u, ACT.Exp).then_inc(su_act, 1)
            act.wait_ge(su_arg, 2)
            act.activation(s_sin, s_r, ACT.Sin)
            act.activation(s_cos, s_p, ACT.Sin).then_inc(su_trig, 1)

            def evacuate(dst, bank):
                act.activation(dst, ps[:, bank, 0:T], ACT.Copy).then_inc(evac, 1)

            for n in range(N_PRE):
                act.wait_ge(used, n + 1)
                evacuate(qkv[:, n, :], n % 2)

            def mag_row(i, j):
                act.wait_ge(h_ready, i * PER_QUAD + (j + 1))
                hold(act)
                act.activation(magx[:, j % 2, :], mask, ACT.Copy,
                               scale=mag[:, bass.ds(i * PER_QUAD + j, 1)]).then_inc(magx_ready, 1)

            act.wait_ge(su_act, 1)
            with act.Fori(0, QUADS // 2) as i:
                for k in (0, 2):
                    q = i * 2 + k // 2
                    act.wait_ge(used, q * 2 + (N_PRE + 1))
                    act.wait_ge(bu_ready, q * PER_QUAD + 1)
                    act.wait_ge(ypre_ready, q + 1)
                    evacuate(uq, 0)
                    mag_row(q, 0)
                    mag_row(q, 1)
                    act.wait_ge(bt_done, q + 2)
                    act.activation(btq, ps[:, 7, 0:2 * P].rearrange("p (a b) -> p a b", a=2),
                                   ACT.Copy).then_inc(bt_ready, 1)
                    act.wait_ge(c_in, q * 16 + 16)
                    act.wait_ge(y_done, q * PER_QUAD + 2)
                    act.activation(ccq[:, 0, :], craw[:, 0, :], ACT.Copy)
                    act.activation(ccq[:, 1, :], craw[:, 1, :], ACT.Copy, scale=-1.0).then_inc(cc_ready, 1)
                    act.wait_ge(used, q * 2 + (N_PRE + 2))
                    hold(act)
                    evacuate(qkv[:, i * 2 + (N_PRE + k // 2), :], 1)
                    mag_row(q, 2)
                    mag_row(q, 3)
                    act.wait_ge(ypre_ready, q + 2)
                    hold(act)
                    act.activation(gT[:, i * 2 + k // 2, :], ypre, ACT.Gelu_apprx_tanh).then_inc(g_ready, 1)

            def heads_tile(j, f):
                act.wait_ge(used, j * FILL + (N_SSM + f + 1))
                hold(act)
                evacuate(qkv[:, j * FILL + (O_FILL + f), :], 7)

            def gate_tile(j, m):
                if m % 2 == 0:
                    act.wait_ge(glu_done, m // 2 + 1)
                else:
                    act.wait_ge(used, N_X + m // 2 + 1)
                if m >= 2:
                    act.wait_ge(so_ready, m - 1)
                act.activation(sig[:, m % 2, :], ps[:, 7, 0:T], ACT.Sigmoid).then_inc(sig_ready, 1)

            def attention(j, between):
                act.wait_ge(evac, j * PER_HEAD + (2 * PER_HEAD - 1))
                act.wait_ge(k_used, j * NB + 2)
                hold(act)
                act.activation(qs, qkv[:, bass.ds(j * PER_HEAD, NG), :], ACT.Copy, scale=HD ** -0.5).then_inc(qs_ready, 1)
                act.wait_ge(vt_done, j + 2)
                act.activation(vtok.rearrange("p a g d -> p a (g d)"), ps[:, 0:PT, 0:NG * P], ACT.Copy)
                act.activation(vnew[0:SAMPLE], ps[0:SAMPLE, 2, 0:NG * P].rearrange("p (g d) -> p g d", g=NG),
                               ACT.Copy).then_inc(vt_ready, 1)

                def exp(w, s, rows):
                    act.wait_ge(mx, j * 3 + (w + 1))
                    act.activation(s, s, ACT.Exp, bias=st[0:rows, w, 0:1], accum_out=st[0:rows, w, 1:2]).then_inc(ex, 1)

                exp(0, s0, P)
                exp(1, s1, P)
                for f in range(3):
                    between(j, f)
                exp(2, scn[0:SAMPLE], SAMPLE)
                between(j, 3)
                act.wait_ge(pt_done, j * 3 + 2)
                act.activation(pt0, ps[:, 3, 0:NG * P].rearrange("p (g d) -> p g d", g=NG), ACT.Copy).then_inc(pt_ready, 1)
                act.wait_ge(pt_done, j * 3 + 3)
                act.activation(pt1[:, 0:4, :], ps[:, 4, :].rearrange("p (g d) -> p g d", g=4), ACT.Copy)
                act.activation(pt1[:, 4:6, :], ps[:, 2, 0:2 * P].rearrange("p (g d) -> p g d", g=2),
                               ACT.Copy).then_inc(pt_ready, 1)
                act.wait_ge(pt_done, j * 3 + 4)
                blocks_ = ps[:, 1, 0:2 * NG * SAMPLE].rearrange("p (g d) -> p g d", g=2 * NG)
                act.activation(ptc, blocks_[:, 0:NG, :], ACT.Copy)
                act.activation(ptn[0:SAMPLE], blocks_[0:SAMPLE, NG:2 * NG, :], ACT.Copy).then_inc(pt_ready, 1)
                for f in range(4, FILL):
                    between(j, f)
                act.wait_ge(v_used, j * NB + (NB + 2))
                hold(act)
                act.activation(qkv[:, bass.ds(j * PER_HEAD, 1), :], ps[:, 0:1, 0:T], ACT.Copy).then_inc(o_ready, 1)

            with act.Fori(0, NJ - 1) as j:
                attention(j, heads_tile)
            attention(NJ - 1, gate_tile)

            with act.Fori(0, KT // 4) as i:
                for k in range(4):
                    act.wait_ge(used, i * 12 + (N_GLU + 3 * k + 2))
                    act.wait_ge(merged, i * 4 + (k + 1))
                    b0 = 4 * (k % 2)
                    act.activation(gsg[:, k % 2], ps[:, b0:b0 + 2, 0:T], ACT.Sigmoid).then_inc(sg_ready, 1)

            for c in range(4):
                act.wait_ge(cent, c + 1)
                act.activation(sq[:, 4 * c:4 * c + 4, :], xT[:, 4 * c:4 * c + 4, :], ACT.Square).then_inc(sq_ready, 1)
            act.wait_ge(rv_ready, 1)
            act.activation(rs, rv, ACT.Sqrt).then_inc(rs_ready, 1)
            act.wait_ge(nrm, 1)
            with act.Fori(0, KT) as i:
                act.activation(xT[:, i, :], xT[:, i, :], ACT.Identity, bias=ln1[:, 1, bass.ds(i, 1)],
                               scale=ln1[:, 0, bass.ds(i, 1)]).then_inc(h_done, 1)

            act.wait_ge(stored, (NJ + 1) * 16)
            for a, rows in TOK_TILES:
                for q in range(4):
                    act.wait_ge(ht_done, 4 * a + q + 1)
                    act.activation(htok[0:rows, a, q * 512:(q + 1) * 512], ps[0:rows, 4 + q, :],
                                   ACT.Copy).then_inc(ht_ready, 1)
            with act.Fori(0, KT // RING) as i:
                for k in range(RING):
                    p = k % 2
                    act.wait_ge(used, i * RING + (N_OUT + k + 1))
                    act.wait_ge(psc_done, i * RING + (k + 1))
                    act.activation(qh[:, p, :], ps[:, p, 0:T], ACT.Copy).then_inc(qh_ready, 1)
                    act.wait_ge(psc_done, i * RING + (k + 3))
                    hold(act)
                    act.activation(sx[:, 0:PT, i * RING + k, :],
                                   ps[:, 2 + p, 0:PT * PK].rearrange("p (a k) -> p a k", a=PT), ACT.Copy)
                    act.activation(sx[0:SAMPLE, PT, i * RING + k, :], ps[0:SAMPLE, 2 + p, PT * PK:3 * PK],
                                   ACT.Copy).then_inc(sx_ready, 1)

            def gate_exp(a):
                act.wait_ge(gd_ready, a + 1)
                g = gate[:, a, 0:TILE_HEADS[a] * PTOP]
                act.activation(g, g, ACT.Exp).then_inc(ge_ready, 1)

            def chunk_gelu(a, h, c):
                act.wait_ge(u_used, h * PTOP + (a * EXPERTS + CHUNK * (c + 1) + URING))
                act.activation(gel[:, c % 2, :], act_[:, c % 2, :],
                               ACT.Gelu_apprx_tanh).then_inc(gelu_ready, 1)

            def norm_sqrt(a, rows):
                act.wait_ge(l2_sq, a + 1)
                act.activation(lnr[0:rows, 1:2], lnr[0:rows, 0:1], ACT.Sqrt).then_inc(rs_ready, 1)

            gate_exp(0)
            for a, heads in enumerate(TILE_HEADS):
                for c in range(PTOP // CHUNK):
                    chunk_gelu(a, 0, c)
                if a:
                    norm_sqrt(a - 1, P)
                with act.Fori(1, heads) as h:
                    for c in range(PTOP // CHUNK):
                        chunk_gelu(a, h, c)
                if a < 2:
                    gate_exp(a + 1)
            norm_sqrt(2, SAMPLE)

        @block.gpsimd
        def _(pool):
            pool.sem_inc(fin_done, 2)
            chain = Chain(pool, poc)
            pool.wait_ge(su_rot, 1)

            def rotation(i, j):
                pool.wait_ge(h_ready, i * PER_QUAD + (j + 1))
                hold(pool)
                s = i * PER_QUAD + j
                dst = rotx[:, j % 2]
                pool.tensor_copy(dst[:, :, 0:SEQ], rot[:, :, s, :])
                pool.tensor_copy(dst[:, :, SEQ:T].rearrange("p c (b l) -> p c b l", b=NB),
                                 spread(rot[:, :, s, 0:NS], 2, NB)).then_inc(rotx_ready, 1)

            def keep_final(i, j):
                pool.wait_ge(h_ready, i * PER_QUAD + (j + 3))
                hold(pool)
                pool.tensor_copy(fin[:, i * PER_QUAD + j], hs[:, j % 2, :, SEQ - 1:T:NS]).then_inc(fin_done, 1)

            with pool.Fori(0, QUADS) as i:
                rotation(i, 0)
                rotation(i, 1)
                keep_final(i, 0)
                rotation(i, 2)
                keep_final(i, 1)
                rotation(i, 3)
                keep_final(i, 2)
                keep_final(i, 3)

            pool.wait_ge(fin_done, STILES + 2)
            chain.link(pool.memset(arena[:, lo_qz:hi_qz], 0.0))
            with pool.Fori(0, NJ) as j:
                pool.wait_ge(evac, j * PER_HEAD + (2 * PER_HEAD - 1))
                pool.wait_ge(vt_done, j + 1)
                hold(pool)
                pool.tensor_copy(vs, qkv[:, bass.ds(j * PER_HEAD + 2 * NG, NG), :]).then_inc(vs_ready, 1)
                pool.wait_ge(qs_ready, j + 1)
                pool.wait_ge(k_used, j * NB + 2)
                hold(pool)
                pool.tensor_copy(qz0.rearrange("p (b w) -> p b w", b=NB)[:, :, 0:NS],
                                 qs[:, 0, SEQ:T].rearrange("p (b l) -> p b l", b=NB))
                z1 = qz1.rearrange("p (b w) -> p b w", b=NB)[:, :, 0:260].rearrange("p b (c v) -> p b c v", c=4)
                pool.tensor_copy(z1[:, :, :, 0:5:4],
                                 qs[:, 1, SEQ:T].rearrange("p (b e c) -> p b c e", b=NB, c=4))
                pool.tensor_copy(qz2.rearrange("p (n v) -> p n v", v=65)[:, :, 0], qs[:, 2, SEQ:T]).then_inc(qz_ready, 1)

            pool.wait_ge(pq_done, 1)
            pool.wait_ge(ht_done, 12)

            def gather(table, half, s, buf, used_, sems, h, n):
                pool.wait_ge(used_, h * PTOP + (n + 1))
                hold(pool)
                off = bass.IndirectOffsetOnAxis(half[:, n % 8:n % 8 + 1], 0)
                pool.indirect_dma_start(buf[s], None, A[table], off).then_inc(sems[s], 16)

            for a, heads in enumerate(TILE_HEADS):
                with chain.loop(heads, 2) as h:
                    pool.wait_ge(idx_ready, h + (a * PH + 1))
                    for e in range(PTOP):
                        half = idxs[:, e // 8, :].bitcast(I32)
                        if e % 8 == 0:
                            hold(pool)
                            chain.link(pool.tensor_copy(half, eidx[:, a, bass.ds(h * PTOP + e, 8)].bitcast(I32)))
                        n = a * EXPERTS + e
                        gather("peer_u", half, e % URING, ub, u_used, usem, h, n)
                        gather("peer_v", half, e % VRING, vb, v_used2, vsem, h, n)

        @block.vector
        def _(dve):
            for s, n in ((bu_free, 2), (h_ready, 2), (merged, 2), (resid, RING), (u_used, URING),
                         (ypre_ready, 1)):
                dve.sem_inc(s, n)
            chain = Chain(dve, dvc)
            link = chain.link
            TT, TS, STT = dve.tensor_tensor, dve.tensor_scalar, dve.scalar_tensor_tensor

            dve.wait_ge(su_dt, 1)
            TT(s_u, s_are, s_dt, ALU.mult).then_inc(su_arg, 1)
            link(TT(s_x, s_aim, s_dt, ALU.mult))
            link(TS(s_n, s_x, 1.0 / (2.0 * float(np.pi)), ROUND, ALU.mult, ALU.add))
            link(TS(s_n, s_n, -ROUND, None, ALU.add))
            link(STT(s_r, s_n, -TWO_PI_HI, s_x, ALU.mult, ALU.add))
            link(STT(s_r, s_n, -TWO_PI_LO, s_r, ALU.mult, ALU.add))
            link(TS(s_r, s_r, PI_SAFE, -PI_SAFE, ALU.min, ALU.max))
            link(STT(s_p, s_r, -1.0, s_r, ALU.mult, ALU.max))
            TS(s_p, s_p, -1.0, float(np.pi) / 2, ALU.mult, ALU.add).then_inc(su_arg, 1)
            link(TT(s_den, s_are, s_are, ALU.mult))
            link(TT(s_q, s_aim, s_aim, ALU.mult))
            link(TT(s_den, s_den, s_q, ALU.add))
            link(dve.reciprocal(s_den, s_den))
            dve.wait_ge(su_act, 1)
            link(TT(h0m.rearrange("p s c b -> p s (c b)"), s_h0.rearrange("p s c b -> p s (c b)"),
                    spread(mag, 2, 2 * NB), ALU.mult))
            dve.wait_ge(su_trig, 1)
            TT(s_br, mag, s_cos, ALU.mult)
            link(TT(s_bi, mag, s_sin, ALU.mult))
            link(TS(s_br, s_br, -1.0, None, ALU.add))
            TT(fre, s_br, s_are, ALU.mult)
            TT(fim, s_bi, s_are, ALU.mult)
            TT(s_q, s_bi, s_aim, ALU.mult)
            link(TT(s_n, s_br, s_aim, ALU.mult))
            TT(fre, fre, s_q, ALU.add)
            link(TT(fim, fim, s_n, ALU.subtract))
            TT(fre, fre, s_den, ALU.mult)
            link(TT(fim, fim, s_den, ALU.mult))
            dve.tensor_copy(rot[:, 0, :, 0], s_cos)
            link(dve.tensor_copy(rot[:, 1, :, 0], s_sin))
            n = 1
            while n < SEQ:
                c, s = rot[:, 0, :, 0:n], rot[:, 1, :, 0:n]
                cn = rot[:, 0, :, n - 1:n].to_broadcast([P, STILES, n])
                sn_ = rot[:, 1, :, n - 1:n].to_broadcast([P, STILES, n])
                a_, b_ = half[:, 0, :, 0:n], half[:, 1, :, 0:n]
                TT(a_, c, cn, ALU.mult)
                link(TT(b_, s, sn_, ALU.mult))
                link(TT(rot[:, 0, :, n:2 * n], a_, b_, ALU.subtract))
                TT(a_, c, sn_, ALU.mult)
                link(TT(b_, s, cn, ALU.mult))
                link(TT(rot[:, 1, :, n:2 * n], a_, b_, ALU.add))
                n *= 2
            dve.sem_inc(su_rot, 1)

            def states(i, j):
                p = j % 2
                s = i * PER_QUAD + j
                bu = ps[:, 2 + 2 * p:4 + 2 * p, 0:T]
                cos, sin = spread(rotx[:, p, 0, :], 1, 2), spread(rotx[:, p, 1, :], 1, 2)
                dve.wait_ge(bu_ready, i * PER_QUAD + (j + 2))
                dve.wait_ge(rotx_ready, i * PER_QUAD + (j + 1))
                dve.wait_ge(h_ready, i * PER_QUAD + (j + 2))
                TT(m1, bu, cos, ALU.mult)
                TT(m2, bu, sin, ALU.mult).then_inc(bu_free, 1)
                dve.wait_ge(bu_free, i * PER_QUAD + (j + 3))
                TT(gw[:, 0, :], m1[:, 0, :], m2[:, 1, :], ALU.add)
                link(TT(gw[:, 1, :], m1[:, 1, :], m2[:, 0, :], ALU.subtract))
                starts = gw[:, :, SEQ:T:NS]
                link(TT(starts, starts, h0m[:, s], ALU.add))
                dve.wait_ge(magx_ready, i * PER_QUAD + (j + 1))
                for c in range(2):
                    ins = dve.tensor_tensor_scan(m1[:, c, :], magx[:, p, :], gw[:, c, :], 0.0, ALU.mult, ALU.add)
                link(ins)
                TT(m2, m1, cos, ALU.mult)
                link(TT(gw, m1, sin, ALU.mult))
                dve.wait_ge(y_done, i * PER_QUAD + (j + 1))
                dve.wait_ge(fin_done, i * PER_QUAD + (j + 1))
                TT(hs[:, p, 0, :], m2[:, 0, :], gw[:, 1, :], ALU.subtract)
                TT(hs[:, p, 1, :], m2[:, 1, :], gw[:, 0, :], ALU.add).then_inc(h_ready, 1)

            def quad_states(i, q):
                quad = bass.ds(q * PER_QUAD, PER_QUAD)
                br = braw.rearrange("p c (j k) -> p c j k", j=PER_QUAD)
                t1 = m1[:, :, 0:P].rearrange("p c (j k) -> p c j k", j=PER_QUAD)
                t2 = m2[:, :, 0:P].rearrange("p c (j k) -> p c j k", j=PER_QUAD)
                dve.wait_ge(b_in, q * 16 + 16)
                dve.wait_ge(h_ready, q * PER_QUAD + 2)
                TT(t1, br, spread(spread(fre[:, quad], 2, 32), 1, 2), ALU.mult)
                link(TT(t2, br, spread(spread(fim[:, quad], 2, 32), 1, 2), ALU.mult))
                dve.wait_ge(bt_done, q + 1)
                TT(bbq[:, 0, :], m1[:, 0, 0:P], m2[:, 1, 0:P], ALU.subtract)
                TT(bbq[:, 1, :], m1[:, 1, 0:P], m2[:, 0, 0:P], ALU.add).then_inc(bb_ready, 1)
                dve.wait_ge(bb_ready, q + 1)
                for j in range(PER_QUAD):
                    states(q, j)
                dve.wait_ge(y_done, q * PER_QUAD + (PER_QUAD + 2))
                dve.wait_ge(g_ready, q + 1)
                STT(ypre, uq, dskip[:, bass.ds(q, 1)], ps[:, 6, 0:T], ALU.mult, ALU.add).then_inc(ypre_ready, 1)

            with chain.loop(QUADS // 2, 2 * (1 + 4 * PER_QUAD)) as i:
                quad_states(i, i * 2)
                quad_states(i, i * 2 + 1)

            dve.wait_ge(att_in, 4 * 16)
            def gate_product(m):
                dve.wait_ge(sig_ready, m + 1)
                TT(so[:, m, :], gT[:, m, :], sig[:, m % 2, :], ALU.mult).then_inc(so_ready, 1)

            def attention(j, products):
                link(dve.tensor_copy(nsl, slopes[:, j, :]))

                def negative_max(w, s, rows):
                    dve.tensor_reduce(st[0:rows, w, 0:1], s, AX.XY if len(s.shape) == 3 else AX.X, ALU.max,
                                      negate=True).then_inc(mx, 1)

                def normalise(w, s, rows):
                    dve.wait_ge(ex, j * 3 + (w + 1))
                    link(dve.reciprocal(st[0:rows, w, 2:3], st[0:rows, w, 1:2]))
                    TS(s, s, st[0:rows, w, 2:3], None, ALU.mult).then_inc(p_ready, 1)

                dve.wait_ge(sc0_done, j + 1)
                dve.wait_ge(pt_done, j * 3 + 1)
                for g in range(NG):
                    ins = STT(s0[:, g, :], dist[:, g, P:SEQ], nsl[:, g:g + 1], ps[:, 3, g * P:(g + 1) * P],
                              ALU.mult, ALU.add)
                link(ins)
                negative_max(0, s0, P)
                dve.wait_ge(sc1_done, j + 1)
                for g in range(NG):
                    ins = STT(s1[:, g, :], dist[:, g, :], nsl[:, g:g + 1],
                              ps[:, 4 + g // 2, (g % 2) * SEQ:(g % 2 + 1) * SEQ], ALU.mult, ALU.add)
                link(ins)
                negative_max(1, s1, P)
                normalise(0, s0, P)
                normalise(1, s1, P)
                for m in products[:3]:
                    gate_product(m)
                dve.wait_ge(k_used, j * NB + (NB + 2))
                R = SAMPLE
                for g in range(NG):
                    STT(sc[0:R, g, :], dist_c[0:R, g, :], nsl[0:R, g:g + 1], ps[0:R, 6, g * P:(g + 1) * P],
                        ALU.mult, ALU.add)
                    ins = STT(sn[0:R, g, :], dist_n[0:R, g, :], nsl[0:R, g:g + 1], ps[0:R, 5, SEQ + g * R:SEQ + (g + 1) * R],
                              ALU.mult, ALU.add)
                link(ins)
                negative_max(2, scn[0:R], R)
                for m in products[3:4]:
                    gate_product(m)
                normalise(2, scn[0:R], R)
                for m in products[4:]:
                    gate_product(m)

            with chain.loop(NJ - 1, 7) as j:
                attention(j, ())
            attention(NJ - 1, range(QUADS))

            with chain.loop(KT // 4, 4) as i:
                for k in range(4):
                    p = k % 2
                    dve.wait_ge(sg_ready, i * 4 + (k + 1))
                    dve.wait_ge(used, i * 12 + (N_GLU + 3 * k + 3))
                    link(TT(gp[:, p], gsg[:, p], ps[:, 4 * p + 2:4 * p + 4, 0:T], ALU.mult))
                    TT(mT[:, i * 4 + k, :], gp[:, p, 0, :], gp[:, p, 1, :], ALU.add).then_inc(merged, 1)
            with dve.Fori(0, KT // RING) as i:
                for k in range(RING):
                    dve.wait_ge(used, i * RING + (N_MERGE + k + 1))
                    STT(xT[:, i * RING + k, :], xT[:, i * RING + k, :], ALPHA, ps[:, k, 0:T],
                        ALU.mult, ALU.add).then_inc(resid, 1)
            dve.wait_ge(mean_done, 1)
            for c in range(4):
                part = xT[:, 4 * c:4 * c + 4, :]
                TT(part, part, spread(ps[:, 4, 0:T], 1, 4), ALU.subtract).then_inc(cent, 1)
            dve.wait_ge(var_done, 1)
            link(TS(var, ps[:, 5, 0:T], EPS, None, ALU.add))
            dve.reciprocal(rv, var).then_inc(rv_ready, 1)
            dve.wait_ge(rs_ready, 1)
            link(TT(nt, var, rs, ALU.mult))
            link(TT(nt, nt, rs, ALU.mult))
            link(TS(nt, nt, -0.5, 1.5, ALU.mult, ALU.add))
            link(TT(rs, rs, nt, ALU.mult))
            TT(xT, xT, spread(rs, 1, KT), ALU.mult).then_inc(nrm, 1)

            dve.wait_ge(peer_in, 2 * 16)
            dve.wait_ge(stored, (NJ + 1) * 16)
            TT(pairs, ident[:, 0:SAMPLE], ident[:, SAMPLE:P], ALU.add)
            link(TS(adiag, ident, ALPHA, None, ALU.mult))
            dve.sem_inc(seeded, 1)

            def topk_head(a, h):
                link(dve.tensor_copy(sc2, sx[:, a, bass.ds(h * 2, 2), :]))
                hold(dve)
                for lo in (0, 8):
                    for s in range(2):
                        ins = dve.max(v16[:, s, lo:lo + 8], sc2[:, s, :])
                    link(ins)
                    hold(dve)
                    for s in range(2):
                        ins = dve.max_index(i16[:, s, lo:lo + 8].bitcast(U32), v16[:, s, lo:lo + 8], sc2[:, s, :])
                    if lo == 0:
                        for s in range(2):
                            ins = dve.match_replace(sc2[:, s, :], v16[:, s, 0:8], sc2[:, s, :], NEG)
                        link(ins)
                        hold(dve)
                link(TT(cand, spread(v16[:, 0, :], 2, PTOP), spread(v16[:, 1, :], 1, PTOP), ALU.add))
                cflat = cand.rearrange("p a b -> p (a b)")
                for lo in (0, 8):
                    hold(dve)
                    link(dve.max(t16[:, lo:lo + 8], cflat))
                    hold(dve)
                    ins = dve.max_index(p16[:, lo:lo + 8].bitcast(U32), t16[:, lo:lo + 8], cflat)
                    if lo == 0:
                        link(dve.match_replace(cflat, t16[:, 0:8], cflat, NEG))
                link(ins)
                TS(gate[:, a, bass.ds(h * PTOP, PTOP)], t16, t16[:, 0:1], None, ALU.subtract)
                dve.tensor_copy(if16, i16.bitcast(U32))
                TS(ab[:, 0, :].bitcast(U32), p16.bitcast(U32), 4, None, ALU.logical_shift_right)
                link(TS(ab[:, 1, :].bitcast(U32), p16.bitcast(U32), PTOP - 1, None, ALU.bitwise_and))
                link(dve.tensor_copy(abf, ab.bitcast(U32)))
                io = spread(spread(iota, 1, PTOP), 1, 2)
                link(TT(oh, spread(abf, 3, PTOP), io, ALU.is_equal))
                link(TT(oh, oh, spread(if16, 2, PTOP), ALU.mult))
                link(dve.tensor_reduce(e12, oh, AX.X, ALU.add))
                STT(eidx[:, a, bass.ds(h * PTOP, PTOP)].bitcast(I32), e12[:, 0, :], float(PK), e12[:, 1, :],
                    ALU.mult, ALU.add).then_inc(idx_ready, 1)

            TOPK_LINKS = 14

            def gates(a):
                dve.sem_inc(gd_ready, 1)
                dve.wait_ge(ge_ready, a + 1)
                heads = TILE_HEADS[a]
                gv = gate[:, a, 0:heads * PTOP].rearrange("p (h k) -> p h k", h=heads)
                gs = gsum[:, 0:heads]
                link(dve.tensor_reduce(gs, gv, AX.X, ALU.add))
                link(dve.reciprocal(gs, gs))
                link(TT(gv, gv, spread(gs, 2, PTOP), ALU.mult))

            with chain.loop(PH, TOPK_LINKS) as h:
                dve.wait_ge(sx_ready, h * 2 + 4)
                topk_head(0, h)
            gates(0)

            CHUNKS = PTOP // CHUNK

            def dot(a, h, c, k):
                dve.wait_ge(usem[k], h * (16 * CHUNKS) + 16 * (a * (EXPERTS // URING) + c + 1))
                dve.tensor_tensor_reduce(ub[k], ub[k], htok[:, a, :], 1.0, 0.0, ALU.mult,
                                         ALU.add, act_[:, c % 2, k:k + 1]).then_inc(u_used, 1)

            def weights(a, h, c):
                dve.wait_ge(gelu_ready, h * CHUNKS + (a * (EXPERTS // CHUNK) + c + 1))
                link(TT(wgt[:, c % 2, :], gel[:, c % 2, :], gate[:, a, bass.ds(h * PTOP + c * CHUNK, CHUNK)],
                        ALU.mult))

            def diagonal(a, h, c, k):
                dve.wait_ge(v_used2, h * PTOP + (a * EXPERTS + c * CHUNK + k + 1 + VRING - CHUNK))
                n = P if a < PT else SAMPLE
                TS(diag[:, k, 0:n], (ident if a < PT else pairs)[:, 0:n], wgt[:, c % 2, k:k + 1], None,
                   ALU.mult).then_inc(dg_ready, 1)

            def head_experts(a, h, first=False, between=None):
                for c in range(CHUNKS):
                    prev = (a, h, c - 1)
                    if first and c == 0:
                        prev = (a - 1, TILE_HEADS[a - 1] - 1, CHUNKS - 1) if a else None
                    for k in range(CHUNK):
                        dot(a, h, c, k)
                        if prev and k == 0:
                            weights(*prev)
                        if prev:
                            diagonal(*prev, k)
                    if c == 1 and between:
                        between(h)

            def second_norm(a, rows):
                R = slice(0, rows)
                f = ps[R, 4 * (a % 2):4 * (a % 2) + 4, :]
                dve.wait_ge(v_used2, VRING + PTOP * sum(TILE_HEADS[:a + 1]))
                for q in range(4):
                    ins = dve.bn_stats(bns[R, q, :], f[:, q, :])
                link(ins)
                link(dve.bn_aggr(bna[R], bns[R].rearrange("p a b -> p (a b)")))
                link(TS(lnr[R, 2:3], bna[R, 1:2], EPS, None, ALU.add))
                dve.reciprocal(lnr[R, 0:1], lnr[R, 2:3]).then_inc(l2_sq, 1)
                dve.wait_ge(rs_ready, a + 2)
                link(TT(lnr[R, 3:4], lnr[R, 2:3], lnr[R, 1:2], ALU.mult))
                link(TT(lnr[R, 3:4], lnr[R, 3:4], lnr[R, 1:2], ALU.mult))
                link(TS(lnr[R, 3:4], lnr[R, 3:4], -0.5, 1.5, ALU.mult, ALU.add))
                link(TT(lnr[R, 1:2], lnr[R, 1:2], lnr[R, 3:4], ALU.mult))
                if a == 0:
                    dve.wait_ge(l2_in, 2 * 16)
                else:
                    dve.wait_ge(y_out, 16 * a)
                y4 = yt[R].rearrange("p (q n) -> p q n", q=4)
                link(TS(y4, f, bna[R, 0:1], lnr[R, 1:2], ALU.subtract, ALU.mult))
                link(TT(yt[R], yt[R], g2[R], ALU.mult))
                TT(yt[R], yt[R], b2[R], ALU.add).then_inc(y_ready, 1)

            dve.wait_ge(packed, 2 * 16)
            for a, heads in enumerate(TILE_HEADS):
                ahead = TILE_HEADS[a + 1] if a < 2 else 1
                topk_next = (lambda h: topk_head(a + 1, h)) if a < 2 else None
                head_experts(a, 0, first=True, between=topk_next)
                if a:
                    second_norm(a - 1, P)
                if a < 2:
                    with chain.loop(ahead - 1, CHUNKS + TOPK_LINKS) as g:
                        head_experts(a, g + 1, between=topk_next)
                if heads > ahead:
                    with chain.loop(heads - ahead, CHUNKS) as g:
                        head_experts(a, g + ahead)
                if a < 2:
                    gates(a + 1)
            weights(2, TILE_HEADS[2] - 1, CHUNKS - 1)
            for k in range(CHUNK):
                diagonal(2, TILE_HEADS[2] - 1, CHUNKS - 1, k)
            second_norm(2, SAMPLE)


def tiles_of(w, k, n):
    K, N = w.shape
    assert K == k * P
    return np.ascontiguousarray(w.reshape(k, P, N // n, n).transpose(2, 1, 0, 3))


def constants():
    f = np.float32
    slopes = -(2.0 ** (-8.0 * np.arange(1, NHEAD + 1) / NHEAD))
    dist = np.full((P, NG, SEQ), FAR)
    dist_c = np.full((SAMPLE, NG, P), FAR)
    dist_n = np.full((SAMPLE, NG, SAMPLE), FAR)
    for g, (w, d) in enumerate(zip(WINDOWS, DILS)):
        off = (P + np.arange(P))[:, None] - np.arange(SEQ)[None, :]
        ok = (off >= 0) & (off <= w) & (off % d == 0)
        dist[:, g] = np.where(ok, off, FAR)
        for b in range(NB):
            for i in range(NS):
                row = i % CLASSES[g] + d * np.arange(P)
                off = w + i - row
                dist_c[b * NS + i, g] = np.where(off <= w, off, FAR)
                for l in range(i + 1):
                    if (i - l) % d == 0:
                        dist_n[b * NS + i, g, b * NS + l] = i - l
    mask = np.ones((P, T))
    mask[:, SEQ::NS] = 0
    mask[:, 0] = 0
    return {
        "ident": np.eye(P, dtype=f), "ones": np.full((P, P), 1.0 / D, f), "mask": mask.astype(f),
        "iota": np.tile(np.arange(PTOP, dtype=f), (P, 1)),
        "slopes": np.tile(slopes.reshape(NG, NJ).T.astype(f)[None], (P, 1, 1)),
        "dist": dist.astype(f), "dist_c": dist_c.astype(f), "dist_n": dist_n.astype(f),
    }


def lay_out(x):
    tok = np.concatenate([x["x_prompt"].reshape(SEQ, D), x["x_sample"].reshape(SAMPLE, D)])
    out = constants()
    out["xT"] = tok.T.reshape(KT, P, T).transpose(1, 0, 2)
    w = tiles_of(x["w_in"], KT, P)
    u, heads, gs, ga = w[:QUADS], w[QUADS:QUADS + QKV_TILES], w[N_X:N_X + KT], w[N_X + KT:]
    heads = heads.reshape(3, NG, NJ, *heads.shape[1:]).swapaxes(1, 2).swapaxes(0, 1)
    heads = heads.reshape(QKV_TILES, *heads.shape[3:])
    order = list(heads[:N_PRE])
    for q in range(QUADS):
        order += [u[q], heads[N_PRE + q]]
    order += list(heads[O_FILL:])
    glu = tiles_of(x["ssm_w_glu"], QUADS, P).reshape(QUADS // 2, 2, P, QUADS * P).swapaxes(1, 2)
    bs, ba = tiles_of(x["w_branch_ssm"], QUADS, P), tiles_of(x["w_branch_attn"], NJ, P)
    branch = np.zeros((KT, P, KT, P), np.float32)
    branch[:, :, :QUADS] = bs
    branch[:, :, QUADS:QUADS + NJ] = ba
    parts = (np.stack(order), glu, np.stack([gs, ga, branch], axis=1), tiles_of(x["w_out"], KT, P),
             tiles_of(x["peer_w_q"], KT, P))
    out["w"] = np.concatenate([p.reshape(-1, P, WSLOT) for p in parts])

    def states(a):
        return np.moveaxis(a.reshape(STILES, P, *a.shape[2:]), 1, 0)

    out["log_dt"] = states(np.repeat(x["ssm_log_dt"][:, None], 64, axis=1))
    out["a_re"], out["a_im"] = states(x["ssm_a_re"]), states(x["ssm_a_im"])
    out["h0"] = states(np.transpose(x["state_ssm"], (1, 2, 3, 0)))
    out["dskip"] = x["ssm_d"].reshape(QUADS, P).T

    def blocks(re, im):
        both = np.stack([re, im], axis=2).reshape(QUADS, PER_QUAD, 2, 64, 2, 16)
        o = np.zeros((QUADS + 1, 2, 64, 2, PER_QUAD, 2, 16), np.float32)
        for half in range(2):
            o[:QUADS, half, :, :, :, half] = both[:, :, half].transpose(0, 2, 3, 1, 4)
        return o.reshape(QUADS + 1, P, 2, P)

    out["ssm_b"] = blocks(x["ssm_b_re"], x["ssm_b_im"])
    out["ssm_c"] = blocks(x["ssm_c_re"].transpose(0, 2, 1), x["ssm_c_im"].transpose(0, 2, 1))

    ks, vs = [], []
    for g, (name, d) in enumerate(zip(("cache_kv_w128", "cache_kv_w512", "cache_kv_w2048"), DILS)):
        c = x[name].reshape(NB, P, d, 2, NJ, HD)[:, :, :CLASSES[g]]
        ks.append(c[:, :, :, 0].transpose(3, 0, 4, 2, 1))
        vs.append(c[:, :, :, 1].transpose(3, 0, 1, 2, 4))
    out["k_cache"] = np.concatenate(ks, axis=3).reshape(NJ * NB, P, CBLK, P)
    out["v_cache"] = np.concatenate(vs, axis=3).reshape(NJ * NB, P, CBLK, P)
    out["ln1"] = np.stack([x["ln1_g"].reshape(KT, P).T, x["ln1_b"].reshape(KT, P).T], axis=1)
    out["ln2"] = np.stack([np.tile(x["ln2_g"], (P, 1)), np.tile(x["ln2_b"], (P, 1))])
    out["sub_keys"] = np.stack([x["peer_sub_keys_1"].T, x["peer_sub_keys_2"].T], axis=1)
    out["peer_u"], out["peer_v"] = x["peer_u"], x["peer_v"]
    return {k: np.ascontiguousarray(v) for k, v in out.items()}


OUTS = {"y": (T, D), "kv": (P, 2 * NHEAD, T), "ssm": (P, STILES, 2, NFIN)}


def kernel(**inputs):
    import concourse.bacc as bacc
    from concourse.bass_utils import run_bass_kernel_spmd

    arrays = lay_out({k: np.asarray(v) for k, v in inputs.items()})
    nc = bacc.Bacc("TRN2", target_bir_lowering=False, num_devices=1)
    A = {k: nc.dram_tensor(f"in_{k}", v.shape, F32, kind="ExternalInput").ap() for k, v in arrays.items()}
    O = {k: nc.dram_tensor(f"out_{k}", s, F32, kind="ExternalOutput").ap() for k, s in OUTS.items()}
    layer_kernel(nc, A, O)
    r = run_bass_kernel_spmd(nc, [{f"in_{k}": v for k, v in arrays.items()}], core_ids=[0]).results[0]
    y, kv, ssm = r["out_y"], r["out_kv"], r["out_ssm"]
    kv = kv.reshape(HD, NJ, 2, NG, T).transpose(3, 4, 2, 1, 0)
    prompt = [kv[g, max(0, SEQ - w):SEQ][None] for g, w in enumerate(WINDOWS)]
    sample = [kv[g, SEQ:].reshape(NB, NS, 2, NJ, HD) for g in range(NG)]
    ssm = ssm.reshape(2, 64, STILES, 2, NFIN).transpose(4, 2, 0, 1, 3).reshape(NFIN, 64, 64, 2)
    return (y[:SEQ][None], y[SEQ:].reshape(NB, NS, D), *prompt, ssm[:1], *sample, ssm[1:])
```

```python
from contextlib import ExitStack, contextmanager

import numpy as np

import concourse.bass as bass
from concourse import mybir

F32 = mybir.dt.float32
I32 = mybir.dt.int32
U32 = mybir.dt.uint32
ALU = mybir.AluOpType
ACT = mybir.ActivationFunctionType
AX = mybir.AxisListType

P = 128
D = 2048
KT = D // P
SEQ = 256
NB, NS = 8, 8
SAMPLE = NB * NS
T = SEQ + SAMPLE
PT = SEQ // P
TOK_TILES = [(0, P), (1, P), (2, SAMPLE)]

WS = 1024
QUADS = WS // P
STILES = 64 * 64 // P
PER_QUAD = STILES // QUADS
NFIN = 1 + NB

HD = 128
NG, NJ = 3, 4
WINDOWS, DILS = (128, 512, 2048), (1, 4, 16)
NHEAD = NG * NJ
QKV_TILES = 3 * NHEAD
CLASSES = (1, 4, NS)
CBLK = sum(CLASSES)
CSLOTS = 2
FAR = 1.0e30

PH, PK, PTOP = 8, 128, 16
EXPERTS = PH * PTOP
TILE_HEADS = (PH, PH, PH // 2)
HEADS = sum(TILE_HEADS)
LAG = 2
DIAGS = 4
URING, VRING = 4, 8

ALPHA = 2.0 ** 0.25
EPS = 1e-5
NEG = -3.0e38
ROUND = 1.5 * 2.0 ** 23
TWO_PI_HI = 6.28125
TWO_PI_LO = 2.0 * float(np.pi) - TWO_PI_HI
PI_SAFE = 3.1415925

RING = 4
WSLOT = KT * P
PER_HEAD = 3 * NG
N_PRE = 8
N_SSM = N_PRE + 3 * QUADS
BODY = 4
FILL = 4
O_FILL = N_PRE + 2 * QUADS
N_X = QUADS + QKV_TILES
N_GLU = N_X + QUADS // 2
N_MERGE = N_GLU + 3 * KT
N_OUT = N_MERGE + KT
N_ALL = N_OUT + KT
assert N_SSM + (NJ - 1) * FILL == N_X
EVAC_0 = N_X - (NJ - 1) * PER_HEAD
assert all(N_SSM - O_FILL + PER_HEAD * (j + 1) <= PER_HEAD * j + EVAC_0 for j in range(NJ))


class Chain:

    def __init__(self, eng, sem):
        self.eng, self.sem, self.done, self.base, self.i, self.per = eng, sem, 0, 0, None, 0

    def link(self, ins):
        self.done += 1
        ins.then_inc(self.sem, 1)
        if self.i is None:
            self.eng.wait_ge(self.sem, self.done)
        else:
            self.eng.wait_ge(self.sem, self.i * self.per + self.done)

    @contextmanager
    def loop(self, steps, per):
        base = self.done
        with self.eng.Fori(0, steps) as i:
            self.i, self.per = i, per
            yield i
        assert self.done - base == per, (self.done - base, per)
        self.i, self.done = None, base + steps * per


class Region:

    def __init__(self, arena, lo, hi):
        self.arena, self.at, self.hi = arena, lo, hi

    def take(self, *shape):
        n = int(np.prod(shape))
        lo = self.at
        self.at += n + n % 2
        assert self.at <= self.hi, (self.at, self.hi, shape)
        v = self.arena[:, lo:lo + n]
        if len(shape) > 1:
            c = "abcd"[:len(shape)]
            v = v.rearrange(f"p ({' '.join(c)}) -> p {' '.join(c)}", **dict(zip(c[1:], shape[1:])))
        return v


def spread(ap, dim, n):
    shape = list(ap.shape)
    return ap.unsqueeze(dim).to_broadcast(shape[:dim] + [n] + shape[dim:])


def layer_kernel(nc, A, O):
    with ExitStack() as ctx:
        COLS = 53200
        arena = ctx.enter_context(nc.sbuf_tensor("arena", [P, COLS], F32))
        ps = ctx.enter_context(nc.psum_tensor("ps", [P, 8, 512], F32))

        def sem(name):
            return ctx.enter_context(nc.semaphore(name))

        r = Region(arena, 0, COLS)
        xT = r.take(KT, T)
        ring = r.take(RING, WSLOT)
        ident = r.take(P)
        lo_qkv = r.at
        qkv = r.take(QKV_TILES, T)
        lo_g = r.at
        gT = r.take(QUADS, T)
        lo_a = r.at

        r = Region(arena, lo_a, COLS)
        rot = r.take(2, STILES, SEQ)
        hi_rot = r.at
        mag = r.take(STILES)
        fre_z, fim_z = (r.take(STILES + PER_QUAD) for _ in range(2))
        fre, fim = fre_z[:, 0:STILES], fim_z[:, 0:STILES]
        h0m = r.take(STILES, 2, NB)
        rotx = r.take(2, 2, T)
        magx = r.take(2, T)
        mask = r.take(T)
        lo_m = r.at
        m1 = r.take(2, T)
        m2 = r.take(2, T)
        gw = r.take(2, T)
        hs = r.take(2, 2, T)
        hi_m = r.at
        uq = r.take(2, T)
        ypre = r.take(T)
        braw = r.take(2, P)
        craw = r.take(2, P)
        bbq = r.take(2, P)
        btq = r.take(2, P)
        ccq = r.take(2, P)
        dskip = r.take(QUADS)
        lo_fin = COLS - STILES * 2 * NFIN
        assert r.at <= lo_fin
        fin = Region(arena, lo_fin, COLS).take(STILES, 2, NFIN)
        r = Region(arena, lo_qkv + 8 * T, lo_g)
        half = r.take(2, STILES, SEQ // 2)
        r = Region(arena, lo_m, hi_m)
        s_h0 = r.take(STILES, 2, NB)
        s_dt, s_are, s_aim, s_x, s_n, s_r, s_u, s_sin, s_cos, s_br, s_bi, s_den, s_p, s_q = (
            r.take(STILES) for _ in range(14))

        r = Region(arena, lo_a, hi_rot)
        kc = r.take(CSLOTS, CBLK, P)
        vc = r.take(CSLOTS, CBLK, P)
        lo_qz = r.at
        qz0 = r.take(NB * 72)
        qz1 = r.take(NB * 264)
        qz2 = r.take(SAMPLE * 65)
        hi_qz = r.at
        qs = r.take(NG, T)
        vs = r.take(NG, T)
        pt1 = r.take(NG * PT, P)
        ptc = r.take(NG, SAMPLE)
        r = Region(arena, hi_rot, COLS)
        so = r.take(QUADS, T)
        dist = r.take(NG, SEQ)
        dist_c = r.take(NG, P)
        dist_n = r.take(NG, SAMPLE)
        slopes = r.take(NJ, NG)
        nsl = r.take(NG)
        vtok = r.take(PT, NG, P)
        vnew = r.take(NG, P)
        s0 = r.take(NG, P)
        sc = r.take(NG, P)
        sn = r.take(NG, SAMPLE)
        scn = arena[:, r.at - NG * (P + SAMPLE):r.at]
        st = r.take(3, 4)
        sig = r.take(2, T)
        s1 = r.take(NG, SEQ)
        pt0 = r.take(NG, P)
        ptn = r.take(NG, SAMPLE)
        osamp = r.take(P)
        assert r.at <= lo_fin

        r = Region(arena, lo_a, hi_rot)
        mT = r.take(KT, T)
        gsg = r.take(2, 2, T)
        gp = r.take(2, 2, T)
        sq = r.take(KT, T)
        var, rv, rs, nt = (r.take(T) for _ in range(4))
        ln1 = r.take(2, KT)
        onesm = r.take(P)

        r = Region(arena, lo_qkv, lo_a)
        htok = r.take(3, D)
        v16 = r.take(2, PTOP)
        i16 = r.take(2, PTOP)
        if16 = r.take(2, PTOP)
        t16 = r.take(PTOP)
        p16 = r.take(PTOP)
        ab = r.take(2, PTOP)
        abf = r.take(2, PTOP)
        e12 = r.take(2, PTOP)
        iota = r.take(PTOP)
        gsum = r.take(PH)
        oh = r.take(2, PTOP, PTOP)
        cand = r.take(PTOP, PTOP)
        sc2 = r.take(2, PK)
        eidx = r.take(3, EXPERTS)
        gate = r.take(3, EXPERTS)
        idxs = r.take(2, 2, 8)
        act_ = r.take(LAG, PTOP)
        gel = r.take(HEADS, PTOP)
        wgt = r.take(PTOP)
        bns = r.take(4, 6)
        bna = r.take(2)
        lnr = r.take(4)
        r = Region(arena, lo_a, COLS)
        sx = r.take(3, 2 * PH, PK)
        qh = r.take(2, T)
        k12 = r.take(2, PK)
        diag = r.take(DIAGS, P)
        adiag = r.take(P)
        pairs = r.take(SAMPLE)
        g2 = r.take(D)
        b2 = r.take(D)
        bufs = [r.take(D) for _ in range(6)]
        r = Region(arena, 0, KT * T + RING * WSLOT)
        bufs += [r.take(D) for _ in range(6)]
        ub, vb = bufs[:URING], bufs[URING:]
        assert len(vb) == VRING
        yt = Region(arena, lo_a, COLS).take(D)

        wsem = [sem(f"weights_{k}") for k in range(RING)]
        used = sem("tile_multiplied")
        evac = sem("tile_evacuated")
        x_in = [sem(f"x_in_{c}") for c in range(4)]
        small_in = sem("ssm_small_in")
        dvc, poc = sem("dve_chain"), sem("pool_chain")
        su_dt, su_trig, su_rot, su_act = sem("dt"), sem("trig"), sem("tables"), sem("setup_act")
        pq_done = sem("queries_done")
        su_arg = sem("trig_args")
        idx_ready = sem("expert_indices")
        b_in, c_in = sem("b_in"), sem("c_in")
        bb_ready, bt_done, bt_ready = sem("b_scaled"), sem("b_transposed"), sem("b_staged")
        cc_ready = sem("c_staged")
        bu_ready, bu_free = sem("bu_ready"), sem("bu_free")
        rotx_ready, magx_ready = sem("rotx_ready"), sem("magx_ready")
        h_ready, y_done, fin_done = sem("h_ready"), sem("y_done"), sem("final_copied")
        ypre_ready, g_ready = sem("ypre_ready"), sem("gelu_ready")
        stored = sem("outputs_stored")
        sig_ready, so_ready, glu_done = sem("glu_sigmoid"), sem("s5_out"), sem("glu_multiplied")
        att_in = sem("attention_constants")
        kcs = [sem(f"k_cache_{k}") for k in range(CSLOTS)]
        vcs = [sem(f"v_cache_{k}") for k in range(CSLOTS)]
        k_used, v_used = sem("k_cache_used"), sem("v_cache_used")
        qz_zero, qs_ready, vs_ready, qz_ready = sem("qz_zero"), sem("qs"), sem("vs"), sem("qz")
        vt_done, vt_ready = sem("v_transposed"), sem("v_token_major")
        sc0_done, sc1_done = sem("scores_0"), sem("scores_1")
        mx, ex = sem("softmax_max"), sem("softmax_exp")
        p_ready = sem("probabilities")
        pt_done, pt_ready = sem("p_transposed"), sem("p_staged")
        o_done, o_ready = sem("attended"), sem("attention_out")
        os_ready = sem("sample_attention_staged")
        sg_ready, merged = sem("gates_sigmoid"), sem("merged")
        ln_in = sem("ln1_in")
        resid, mean_done, cent, sq_ready, var_done = (
            sem("residual"), sem("mean"), sem("centred"), sem("squared"), sem("variance"))
        rv_ready, rs_ready, nrm, h_done = sem("rv"), sem("rsqrt"), sem("normed"), sem("h_feature")
        qh_ready, psc_done, sx_ready = sem("query_staged"), sem("subkey_scores"), sem("scores_out")
        packed = sem("sample_heads_packed")
        ht_done, ht_ready = sem("h_transposed"), sem("h_token_major")
        peer_in = sem("peer_small_in")
        gd_ready, ge_ready = sem("gate_diff"), sem("gate_exp")
        usem = [sem(f"u_rows_{k}") for k in range(URING)]
        vsem = [sem(f"v_rows_{k}") for k in range(VRING)]
        u_used, v_used2 = sem("u_rows_used"), sem("v_rows_used")
        gelu_ready, dg_ready = sem("expert_gelu"), sem("diagonals")
        seeded = sem("alpha_h_seeded")
        l2_in, l2_sq, y_ready, y_out = sem("ln2_in"), sem("ln2_sqrt"), sem("y_ready"), sem("y_out")

        passed = sem("waits_passed")

        def hold(eng):
            eng.sem_inc(passed, 1)

        def slot(k):
            return ring[:, k, :].rearrange("p (k m) -> p k m", m=P)

        block = ctx.enter_context(nc.Block())

        @block.sync
        def _(sp):
            def load(k, src, cols=WSLOT):
                sp.dma_start(ring[:, k, 0:cols], src).then_inc(wsem[k], 16)

            def w(n, k=None):
                load(n % RING, A["w"][n])

            for c in range(4):
                sp.dma_start(xT[:, 4 * c:4 * c + 4, :], A["xT"][:, 4 * c:4 * c + 4, :]).then_inc(x_in[c], 16)
                if c == 0:
                    w(0)
            for dst, name in ((s_dt, "log_dt"), (s_are, "a_re"), (s_aim, "a_im"),
                              (s_h0, "h0"), (mask, "mask"), (dskip, "dskip"), (ident, "ident")):
                sp.dma_start(dst, A[name]).then_inc(small_in, 16)
            for n in range(1, RING):
                w(n)
            sp.dma_start(braw, A["ssm_b"][0]).then_inc(b_in, 16)
            sp.dma_start(craw, A["ssm_c"][0]).then_inc(c_in, 16)
            for n in range(RING, N_PRE):
                sp.wait_ge(used, n - RING + 1)
                w(n)
            with sp.Fori(0, QUADS // BODY) as i:
                for k in range(3 * BODY):
                    q = i * BODY + k // 3
                    sp.wait_ge(used, i * (3 * BODY) + (N_PRE - RING + k + 1))
                    load(k % RING, A["w"][i * (3 * BODY) + (N_PRE + k)])
                    if k % 3 == 2:
                        sp.wait_ge(bb_ready, q + 1)
                        sp.dma_start(braw, A["ssm_b"][q + 1]).then_inc(b_in, 16)
                        sp.wait_ge(cc_ready, q + 1)
                        sp.dma_start(craw, A["ssm_c"][q + 1]).then_inc(c_in, 16)
            for n in range(N_SSM, N_SSM + RING - 1):
                sp.wait_ge(used, n - RING + 1)
                w(n)
            sp.wait_ge(fin_done, STILES + 2)
            sp.dma_start(O["ssm"], fin).then_inc(stored, 16)
            sp.wait_ge(g_ready, QUADS + 1)
            for dst, name in ((dist, "dist"), (slopes, "slopes")):
                sp.dma_start(dst, A[name]).then_inc(att_in, 16)
            sp.dma_start(dist_c[0:SAMPLE], A["dist_c"]).then_inc(att_in, 16)
            sp.dma_start(dist_n[0:SAMPLE], A["dist_n"]).then_inc(att_in, 16)

            def caches(j, bs, name, buf, sems, used_):
                for b in bs:
                    sp.wait_ge(used_, j * NB + (b + 1))
                    sp.dma_start(buf[:, b % CSLOTS], A[name][j * NB + b]).then_inc(sems[b % CSLOTS], 16)

            def keys(j, *bs):
                caches(j, bs, "k_cache", kc, kcs, k_used)

            def values(j, *bs):
                caches(j, bs, "v_cache", vc, vcs, v_used)

            def fill(j, x):
                sp.wait_ge(used, j * FILL + (N_SSM + x - RING + 1))
                load(x % RING, A["w"][j * FILL + (N_SSM + x)])

            with sp.Fori(0, NJ) as j:
                keys(j, 0, 1)
                values(j, 0, 1)
                fill(j, 3)
                keys(j, 2, 3, 4, 5)
                fill(j, 4)
                keys(j, 6, 7)
                values(j, 2, 3)
                fill(j, 5)
                values(j, 4, 5)
                fill(j, 6)
                values(j, 6, 7)
            fill(NJ - 1, 7)
            sp.wait_ge(evac, N_X)
            for j in range(NJ):
                sp.dma_start(O["kv"][:, 2 * NG * j:2 * NG * (j + 1), :],
                             qkv[:, PER_HEAD * j + NG:PER_HEAD * (j + 1), :]).then_inc(stored, 16)
            assert (N_MERGE - N_GLU - RING) % (2 * RING) == RING and 3 * KT % RING == 0
            with sp.Fori(0, (N_MERGE - N_GLU - RING) // RING) as i:
                for k in range(RING):
                    sp.wait_ge(used, i * RING + (N_GLU + k + 1))
                    load(k, A["w"][i * RING + (N_GLU + RING + k)])
            sp.wait_ge(o_ready, NJ + 1)
            sp.dma_start(ln1, A["ln1"]).then_inc(ln_in, 16)
            sp.dma_start(onesm, A["ones"]).then_inc(ln_in, 16)
            steps = KT // RING + 1
            with sp.Fori(0, steps) as i:
                for k in range(RING):
                    sp.wait_ge(used, i * RING + (N_MERGE - RING + k + 1))
                    load(k, A["w"][i * RING + (N_MERGE + k)])
            sp.wait_ge(h_done, KT)
            sp.dma_start(k12, A["sub_keys"]).then_inc(peer_in, 16)
            sp.dma_start(iota, A["iota"]).then_inc(peer_in, 16)
            sp.dma_start(g2, A["ln2"][0]).then_inc(l2_in, 16)
            sp.dma_start(b2, A["ln2"][1]).then_inc(l2_in, 16)
            with sp.Fori(0, 2 * KT // RING - steps) as i:
                for k in range(RING):
                    sp.wait_ge(used, i * RING + (N_MERGE + (steps - 1) * RING + k + 1))
                    load(k, A["w"][i * RING + (N_MERGE + steps * RING + k)])
            sp.wait_ge(sx_ready, KT + 2)
            sp.dma_start(sx[SAMPLE:P, PT, 0:PH, :], sx[0:SAMPLE, PT, PH:2 * PH, :]).then_inc(packed, 16)
            sp.wait_ge(ht_ready, 12)
            sp.dma_start(htok[SAMPLE:P, PT, :], htok[0:SAMPLE, PT, :]).then_inc(packed, 16)
            for a, rows in TOK_TILES:
                sp.wait_ge(y_ready, a + 1)
                sp.dma_start(O["y"][a * P:a * P + rows, :], yt[0:rows, :]).then_inc(y_out, 16)
            sp.wait_ge(stored, (NJ + 1) * 16)
            sp.wait_ge(y_out, 3 * 16)

        @block.tensor
        def _(pe):
            for s, n in ((y_done, 2), (k_used, CSLOTS), (v_used, CSLOTS), (psc_done, 2), (v_used2, VRING),
                         (bt_done, 1), (bu_ready, 1), (vt_done, 1), (pt_done, 1)):
                pe.sem_inc(s, n)

            def matmuls(out, lhs, rhs, n, skip=False):
                for k in range(n):
                    ins = pe.matmul(out, lhs(k), rhs(k), start=(k == 0), stop=(k == n - 1))
                return ins

            def project(k, bank):
                return matmuls(ps[:, bank, 0:T], lambda t: slot(k)[:, t, :], lambda t: xT[:, t, :], KT)

            for n in range(N_PRE):
                pe.wait_ge(wsem[n % RING], 16 * (n // RING + 1))
                if n >= 2:
                    pe.wait_ge(evac, n - 1)
                for t in range(KT):
                    if n == 0 and t % 4 == 0:
                        pe.wait_ge(x_in[t // 4], 16)
                    ins = pe.matmul(ps[:, n % 2, 0:T], slot(n % RING)[:, t, :], xT[:, t, :], start=(t == 0),
                                    stop=(t == KT - 1))
                ins.then_inc(used, 1)

            def tile(i, k):
                pe.wait_ge(wsem[k % RING], i * (3 * BODY // RING * 16) + 16 * ((N_PRE + k) // RING + 1))
                pe.wait_ge(evac, i * (3 * BODY) + (N_PRE + k - 1))
                project(k % RING, k % 2).then_inc(used, 1)

            def b_transposed(q):
                pe.wait_ge(bb_ready, q + 1)
                pe.wait_ge(bt_ready, q + 1)
                for part in range(2):
                    ins = pe.transpose(ps[:, 7, part * P:part * P + P], bbq[:, part, :], ident)
                ins.then_inc(bt_done, 1)

            def b_u(q, j, u):
                pe.wait_ge(bu_free, q * PER_QUAD + (j + 1))
                lo = 32 * j
                for part in range(2):
                    ins = pe.matmul(ps[:, 2 + 2 * (j % 2) + part, 0:T], btq[lo:lo + 32, part, :],
                                    u[lo:lo + 32, :], start=True, stop=True)
                ins.then_inc(bu_ready, 1)

            def c_h(q, j):
                lo = 32 * j
                pe.wait_ge(h_ready, q * PER_QUAD + (j + 3))
                for part in range(2):
                    ins = pe.matmul(ps[lo:lo + 32, 6, 0:T], ccq[:, part, lo:lo + 32], hs[:, j % 2, part, :],
                                    start=(part == 0), stop=(part == 1))
                ins.then_inc(y_done, 1)

            b_transposed(0)
            with pe.Fori(0, QUADS // BODY) as i:
                tile(i, 0)
                for k in range(BODY):
                    q = i * BODY + k
                    u = uq[:, k % 2]
                    pe.wait_ge(bt_ready, q + 2)
                    pe.wait_ge(evac, q * 3 + (N_PRE + 1))
                    b_u(q, 0, u)
                    b_u(q, 1, u)
                    tile(i, 3 * k + 1)
                    pe.wait_ge(cc_ready, q + 1)
                    pe.wait_ge(ypre_ready, q + 1)
                    c_h(q, 0)
                    b_u(q, 2, u)
                    c_h(q, 1)
                    b_u(q, 3, u)
                    tile(i, 3 * k + 2)
                    c_h(q, 2)
                    b_transposed(q + 1)
                    if k < BODY - 1:
                        tile(i, 3 * k + 3)
                    c_h(q, 3)

            def heads_half(j, x):
                f, half = x // 2, x % 2
                if half == 0:
                    pe.wait_ge(wsem[f % RING], j * (16 * FILL // RING) + 16 * ((N_SSM + f) // RING + 1))
                    pe.wait_ge(evac, j * FILL + (N_SSM + f))
                for t in range(half * KT // 2, (half + 1) * KT // 2):
                    ins = pe.matmul(ps[:, 7, 0:T], slot(f % RING)[:, t, :], xT[:, t, :], start=(t == 0),
                                    stop=(t == KT - 1), skip_group_check=True)
                if half == 1:
                    ins.then_inc(used, 1)

            def gate_tile(j, m):
                k = (N_X + m // 2) % RING
                if m % 2 == 0:
                    pe.wait_ge(wsem[k], 16 * ((N_X + m // 2) // RING + 1))
                if m == 0:
                    pe.wait_ge(g_ready, QUADS + 1)
                    pe.wait_ge(evac, N_X)
                else:
                    pe.wait_ge(sig_ready, m)
                s = slot(k)[:, (m % 2) * QUADS:(m % 2 + 1) * QUADS, :]
                matmuls(ps[:, 7, 0:T], lambda t: s[:, t, :], lambda t: gT[:, t, :],
                        QUADS).then_inc(used if m % 2 else glu_done, 1)

            def attention(j, between):
                pe.wait_ge(vs_ready, j + 1)
                pe.wait_ge(o_ready, j + 1)
                for a in range(PT):
                    for g in range(NG):
                        pe.transpose(ps[:, a, g * P:g * P + P], vs[:, g, a * P:a * P + P], ident)
                for g in range(NG):
                    ins = pe.transpose(ps[0:SAMPLE, 2, g * P:g * P + P], vs[:, g, SEQ:T], ident)
                ins.then_inc(vt_done, 1)
                pe.wait_ge(qs_ready, j + 1)
                for g in range(NG):
                    ins = pe.matmul(ps[:, 3, g * P:g * P + P], qs[:, g, 0:P],
                                    qkv[:, j * PER_HEAD + (NG + g), 0:P],
                                    start=(g == 0), stop=(g == NG - 1), skip_group_check=True)
                ins.then_inc(sc0_done, 1)
                for g in range(NG):
                    pe.matmul(ps[:, 4 + g // 2, (g % 2) * SEQ:(g % 2) * SEQ + SEQ], qs[:, g, P:SEQ],
                              qkv[:, j * PER_HEAD + (NG + g), 0:SEQ],
                              start=(g % 2 == 0), stop=(g > 0), skip_group_check=True)
                for g in range(NG):
                    ins = pe.matmul(ps[0:SAMPLE, 5, SEQ + g * SAMPLE:SEQ + (g + 1) * SAMPLE], qs[:, g, SEQ:T],
                                    qkv[:, j * PER_HEAD + (NG + g), SEQ:T],
                                    start=False, stop=(g == NG - 1), skip_group_check=True)
                ins.then_inc(sc1_done, 1)
                pe.wait_ge(qz_ready, j * 2 + 1)
                for b in range(NB):
                    pe.wait_ge(kcs[b % CSLOTS], j * (16 * NB // CSLOTS) + 16 * (b // CSLOTS + 1))
                    blk = 0
                    for g, qz in enumerate((qz0, qz1, qz2)):
                        for c in range(CLASSES[g]):
                            w = 64 * (b * CLASSES[g] + c)
                            ins = pe.matmul(ps[0:SAMPLE, 6, g * P:g * P + P], qz[:, w:w + 64],
                                            kc[:, b % CSLOTS, blk, :], start=(b == 0 and blk == 0),
                                            stop=(b == NB - 1 and blk == CBLK - 1), skip_group_check=True)
                            blk += 1
                    ins.then_inc(k_used, 1)
                    if b % 2 == 1:
                        between(j, b // 2)
                pe.wait_ge(p_ready, j * 3 + 1)
                for g in range(NG):
                    ins = pe.transpose(ps[:, 3, g * P:g * P + P], s0[:, g, :], ident)
                ins.then_inc(pt_done, 1)
                pe.wait_ge(p_ready, j * 3 + 2)
                pe.wait_ge(vt_ready, j + 1)
                for g in range(NG):
                    for a in range(PT):
                        t = g * PT + a
                        ins = pe.transpose(ps[:, (4, 2)[t // 4], (t % 4) * P:(t % 4) * P + P],
                                           s1[:, g, a * P:a * P + P], ident)
                ins.then_inc(pt_done, 1)
                pe.wait_ge(p_ready, j * 3 + 3)
                hold(pe)
                for g in range(NG):
                    pe.transpose(ps[:, 1, g * SAMPLE:(g + 1) * SAMPLE], sc[0:SAMPLE, g, :],
                                 ident[0:SAMPLE, 0:SAMPLE])
                for g in range(NG):
                    ins = pe.transpose(ps[0:SAMPLE, 1, (NG + g) * SAMPLE:(NG + g + 1) * SAMPLE], sn[0:SAMPLE, g, :],
                                       ident[0:SAMPLE, 0:SAMPLE])
                ins.then_inc(pt_done, 1)
                pe.wait_ge(pt_ready, j * 3 + 1)
                for g in range(NG):
                    pe.matmul(ps[:, 0, 0:P], vtok[:, 0, g, :], pt0[:, g, :],
                              start=(g == 0), stop=(g == NG - 1), skip_group_check=True)
                pe.wait_ge(pt_ready, j * 3 + 2)
                for t in range(NG * PT):
                    pe.matmul(ps[:, 0, P:SEQ], vtok[:, t % PT, t // PT, :], pt1[:, t, :],
                              start=False, stop=(t == NG * PT - 1), skip_group_check=True)
                pe.wait_ge(pt_ready, j * 3 + 3)
                hold(pe)
                out = ps[0:SAMPLE, 3, NG * P:(NG + 1) * P]
                for g in range(NG):
                    pe.matmul(out, ptn[0:SAMPLE, g, :], vnew[0:SAMPLE, g, :],
                              start=(g == 0), stop=False, skip_group_check=True)
                pe.wait_ge(qz_ready, j * 2 + 2)
                for b in range(NB):
                    pe.wait_ge(vcs[b % CSLOTS], j * (16 * NB // CSLOTS) + 16 * (b // CSLOTS + 1))
                    blk = 0
                    for g, qz in enumerate((qz0, qz1, qz2)):
                        for c in range(CLASSES[g]):
                            w = 64 * (b * CLASSES[g] + c)
                            ins = pe.matmul(out, qz[:, w:w + 64], vc[:, b % CSLOTS, blk, :], start=False,
                                            stop=(b == NB - 1 and blk == CBLK - 1), skip_group_check=True)
                            blk += 1
                    ins.then_inc(v_used, 1)
                    if b % 2 == 1:
                        between(j, NB // 2 + b // 2)
                pe.wait_ge(os_ready, j + 1)
                hold(pe)
                pe.transpose(ps[:, 0, SEQ:T], osamp[0:SAMPLE, :], ident[0:SAMPLE, 0:SAMPLE]).then_inc(o_done, 1)

            pe.wait_ge(evac, N_SSM)
            with pe.Fori(0, NJ - 1) as j:
                attention(j, heads_half)
            attention(NJ - 1, gate_tile)

            def merge_tile(i, k):
                p = 4 * (k % 2)

                def at(t):
                    n = 3 * k + t
                    pe.wait_ge(wsem[n % RING], i * (3 * 16) + 16 * (N_GLU // RING + n // RING + 1))
                    return slot(n % RING)

                s = at(0)
                pe.wait_ge(merged, i * 4 + (k + 1))
                matmuls(ps[:, p, 0:T], lambda t: s[:, t, :], lambda t: xT[:, t, :], KT).then_inc(used, 1)
                s = at(1)
                matmuls(ps[:, p + 1, 0:T], lambda t: s[:, t, :], lambda t: xT[:, t, :], KT).then_inc(used, 1)
                s = at(2)
                matmuls(ps[:, p + 2, 0:T], lambda t: s[:, t, :], lambda t: so[:, t, :], QUADS)
                matmuls(ps[:, p + 3, 0:T], lambda t: s[:, QUADS + t, :], lambda t: qkv[:, PER_HEAD * t, :],
                        NJ).then_inc(used, 1)

            pe.wait_ge(so_ready, QUADS)
            pe.wait_ge(o_ready, NJ + 1)
            with pe.Fori(0, KT // 4) as i:
                for k in range(4):
                    merge_tile(i, k)

            pe.wait_ge(merged, KT + 2)
            with pe.Fori(0, KT // RING) as i:
                for k in range(RING):
                    pe.wait_ge(wsem[k], i * 16 + (16 * (N_MERGE // RING) + 16))
                    pe.wait_ge(resid, i * RING + (k + 1))
                    matmuls(ps[:, k, 0:T], lambda t: slot(k)[:, t, :], lambda t: mT[:, t, :],
                            KT).then_inc(used, 1)
            pe.wait_ge(ln_in, 2 * 16)
            for t in range(KT):
                if t % RING == 0:
                    pe.wait_ge(resid, t + RING + RING)
                ins = pe.matmul(ps[:, 4, 0:T], onesm, xT[:, t, :], start=(t == 0), stop=(t == KT - 1))
            ins.then_inc(mean_done, 1)
            for t in range(KT):
                if t % 4 == 0:
                    pe.wait_ge(sq_ready, t // 4 + 1)
                ins = pe.matmul(ps[:, 5, 0:T], onesm, sq[:, t, :], start=(t == 0), stop=(t == KT - 1))
            ins.then_inc(var_done, 1)

            for q in range(4):
                pe.wait_ge(h_done, 4 * (q + 1))
                for a, rows in TOK_TILES:
                    n = 3 * q + a
                    if n >= 4:
                        pe.wait_ge(ht_ready, n - 3)
                    for t in range(4):
                        ins = pe.transpose(ps[0:rows, 4 + n % 4, t * P:(t + 1) * P],
                                           xT[:, 4 * q + t, a * P:a * P + rows], ident)
                    ins.then_inc(ht_done, 1)

            pe.wait_ge(peer_in, 2 * 16)

            def subkey_scores(i, k):
                p = k % 2
                pe.wait_ge(qh_ready, i * RING + (k + 3))
                pe.wait_ge(sx_ready, i * RING + (k + 1))
                for a, rows in TOK_TILES:
                    ins = pe.matmul(ps[0:rows, 2 + p, a * PK:(a + 1) * PK], qh[:, p, a * P:a * P + rows],
                                    k12[:, p, :], start=(a == 0), stop=(a == 2), skip_group_check=True)
                ins.then_inc(psc_done, 1)

            with pe.Fori(0, KT // RING) as i:
                for k in range(RING):
                    pe.wait_ge(wsem[k], i * 16 + (16 * (N_OUT // RING) + 16))
                    pe.wait_ge(qh_ready, i * RING + (k + 1))
                    matmuls(ps[:, k % 2, 0:T], lambda t: slot(k)[:, t, :], lambda t: xT[:, t, :],
                            KT).then_inc(used, 1)
                    if k:
                        subkey_scores(i, k - 1)
                subkey_scores(i, RING - 1)
            pe.nop().then_inc(pq_done, 1)

            pe.wait_ge(ht_ready, 12)
            for a, rows in TOK_TILES:
                b0 = 4 * (a % 2)
                if a == 0:
                    pe.wait_ge(sx_ready, KT + 2)
                if a == 2:
                    pe.wait_ge(y_ready, 1)
                pe.wait_ge(seeded, 1)
                for q in range(4):
                    ins = pe.matmul(ps[0:rows, b0 + q, :], adiag[0:rows, 0:rows], htok[0:rows, a, q * 512:(q + 1) * 512],
                                    start=True, stop=False, skip_group_check=True)
                with pe.Fori(0, TILE_HEADS[a]) as h:
                    for e in range(PTOP):
                        n = a * EXPERTS + e
                        v = e % VRING
                        pe.wait_ge(vsem[v], h * (16 * PTOP // VRING) + 16 * (n // VRING + 1))
                        pe.wait_ge(dg_ready, h * PTOP + (n + 2))
                        hold(pe)
                        for q in range(4):
                            ins = pe.matmul(ps[0:rows, b0 + q, :], diag[:, e % DIAGS, 0:rows],
                                            vb[v][:, q * 512:(q + 1) * 512],
                                            start=False, stop=True, skip_group_check=True)
                        ins.then_inc(v_used2, 1)

        @block.scalar
        def _(act):
            for s, n in ((qh_ready, 2), (sx_ready, 2), (bt_ready, 1), (g_ready, 1), (o_ready, 1)):
                act.sem_inc(s, n)
            act.wait_ge(small_in, 7 * 16)
            act.activation(s_dt, s_dt, ACT.Exp).then_inc(su_dt, 1)
            act.wait_ge(su_arg, 1)
            act.activation(mag, s_u, ACT.Exp).then_inc(su_act, 1)
            act.wait_ge(su_arg, 2)
            act.activation(s_sin, s_r, ACT.Sin)
            act.activation(s_cos, s_p, ACT.Sin).then_inc(su_trig, 1)

            def evacuate(dst, bank):
                act.activation(dst, ps[:, bank, 0:T], ACT.Copy).then_inc(evac, 1)

            for n in range(N_PRE):
                act.wait_ge(used, n + 1)
                evacuate(qkv[:, n, :], n % 2)

            def mag_row(i, j):
                act.wait_ge(h_ready, i * PER_QUAD + (j + 1))
                hold(act)
                act.activation(magx[:, j % 2, :], mask, ACT.Copy,
                               scale=mag[:, bass.ds(i * PER_QUAD + j, 1)]).then_inc(magx_ready, 1)

            def stage_b(q):
                act.wait_ge(bt_done, q + 2)
                act.wait_ge(bu_ready, q * PER_QUAD + 1)
                act.activation(btq, ps[:, 7, 0:2 * P].rearrange("p (a b) -> p a b", a=2),
                               ACT.Copy).then_inc(bt_ready, 1)

            def stage_u(q, k):
                act.wait_ge(used, q * 3 + (N_PRE + 1))
                act.wait_ge(ypre_ready, q + (0 if k else 1))
                hold(act)
                evacuate(uq[:, k % 2], 3 * k % 2)

            def stage_head(i, q, k, x):
                act.wait_ge(used, q * 3 + (N_PRE + x + 2))
                hold(act)
                evacuate(qkv[:, i * (2 * BODY) + (N_PRE + 2 * k + x), :], (3 * k + 1 + x) % 2)

            act.wait_ge(su_act, 1)
            stage_b(0)
            with act.Fori(0, QUADS // BODY) as i:
                stage_u(i * BODY, 0)
                for k in range(BODY):
                    q = i * BODY + k
                    mag_row(q, 0)
                    mag_row(q, 1)
                    act.wait_ge(c_in, q * 16 + 16)
                    act.wait_ge(y_done, q * PER_QUAD + 2)
                    act.activation(ccq[:, 0, :], craw[:, 0, :], ACT.Copy)
                    act.activation(ccq[:, 1, :], craw[:, 1, :], ACT.Copy, scale=-1.0).then_inc(cc_ready, 1)
                    stage_head(i, q, k, 0)
                    mag_row(q, 2)
                    mag_row(q, 3)
                    stage_head(i, q, k, 1)
                    stage_b(q + 1)
                    if k < BODY - 1:
                        stage_u(q + 1, k + 1)
                    act.wait_ge(ypre_ready, q + 2)
                    hold(act)
                    act.activation(gT[:, i * BODY + k, :], ypre, ACT.Gelu_apprx_tanh).then_inc(g_ready, 1)

            def heads_tile(j, f):
                act.wait_ge(used, j * FILL + (N_SSM + f + 1))
                hold(act)
                evacuate(qkv[:, j * FILL + (O_FILL + f), :], 7)

            def fill_tile(j, x):
                if x % 2 == 1:
                    heads_tile(j, x // 2)

            def gate_tile(j, m):
                if m % 2 == 0:
                    act.wait_ge(glu_done, m // 2 + 1)
                else:
                    act.wait_ge(used, N_X + m // 2 + 1)
                if m >= 2:
                    act.wait_ge(so_ready, m - 1)
                act.activation(sig[:, m % 2, :], ps[:, 7, 0:T], ACT.Sigmoid).then_inc(sig_ready, 1)

            def attention(j, between):
                act.wait_ge(evac, j * PER_HEAD + EVAC_0)
                act.wait_ge(k_used, j * NB + 2)
                hold(act)
                act.activation(qs, qkv[:, bass.ds(j * PER_HEAD, NG), :], ACT.Copy, scale=HD ** -0.5).then_inc(qs_ready, 1)
                act.wait_ge(vt_done, j + 2)
                act.activation(vtok.rearrange("p a g d -> p a (g d)"), ps[:, 0:PT, 0:NG * P], ACT.Copy)
                act.activation(vnew[0:SAMPLE], ps[0:SAMPLE, 2, 0:NG * P].rearrange("p (g d) -> p g d", g=NG),
                               ACT.Copy).then_inc(vt_ready, 1)

                def exp(w, s, rows):
                    act.wait_ge(mx, j * 3 + (w + 1))
                    act.activation(s, s, ACT.Exp, bias=st[0:rows, w, 0:1], accum_out=st[0:rows, w, 1:2]).then_inc(ex, 1)

                exp(0, s0, P)
                exp(1, s1, P)
                for x in range(3):
                    between(j, x)
                exp(2, scn[0:SAMPLE], SAMPLE)
                between(j, 3)
                act.wait_ge(pt_done, j * 3 + 2)
                act.activation(pt0, ps[:, 3, 0:NG * P].rearrange("p (g d) -> p g d", g=NG), ACT.Copy).then_inc(pt_ready, 1)
                act.wait_ge(pt_done, j * 3 + 3)
                act.activation(pt1[:, 0:4, :], ps[:, 4, :].rearrange("p (g d) -> p g d", g=4), ACT.Copy)
                act.activation(pt1[:, 4:6, :], ps[:, 2, 0:2 * P].rearrange("p (g d) -> p g d", g=2),
                               ACT.Copy).then_inc(pt_ready, 1)
                act.wait_ge(pt_done, j * 3 + 4)
                blocks_ = ps[:, 1, 0:2 * NG * SAMPLE].rearrange("p (g d) -> p g d", g=2 * NG)
                act.activation(ptc, blocks_[:, 0:NG, :], ACT.Copy)
                act.activation(ptn[0:SAMPLE], blocks_[0:SAMPLE, NG:2 * NG, :], ACT.Copy).then_inc(pt_ready, 1)
                for x in range(4, NB - 1):
                    between(j, x)
                act.wait_ge(v_used, j * NB + (NB + 2))
                hold(act)
                act.activation(osamp[0:SAMPLE, :], ps[0:SAMPLE, 3, NG * P:(NG + 1) * P], ACT.Copy).then_inc(os_ready, 1)
                between(j, NB - 1)
                act.wait_ge(o_done, j + 1)
                hold(act)
                act.activation(qkv[:, bass.ds(j * PER_HEAD, 1), :], ps[:, 0:1, 0:T], ACT.Copy).then_inc(o_ready, 1)

            with act.Fori(0, NJ - 1) as j:
                attention(j, fill_tile)
            attention(NJ - 1, gate_tile)

            with act.Fori(0, KT // 4) as i:
                for k in range(4):
                    act.wait_ge(used, i * 12 + (N_GLU + 3 * k + 2))
                    act.wait_ge(merged, i * 4 + (k + 1))
                    b0 = 4 * (k % 2)
                    act.activation(gsg[:, k % 2], ps[:, b0:b0 + 2, 0:T], ACT.Sigmoid).then_inc(sg_ready, 1)

            for c in range(4):
                act.wait_ge(cent, c + 1)
                act.activation(sq[:, 4 * c:4 * c + 4, :], xT[:, 4 * c:4 * c + 4, :], ACT.Square).then_inc(sq_ready, 1)
            act.wait_ge(rv_ready, 1)
            act.activation(rs, rv, ACT.Sqrt).then_inc(rs_ready, 1)
            for t in range(KT):
                act.wait_ge(nrm, t // 4 + 1)
                act.activation(xT[:, t, :], xT[:, t, :], ACT.Identity, bias=ln1[:, 1, t:t + 1],
                               scale=ln1[:, 0, t:t + 1]).then_inc(h_done, 1)

            for q in range(4):
                for a, rows in TOK_TILES:
                    n = 3 * q + a
                    act.wait_ge(ht_done, n + 1)
                    act.activation(htok[0:rows, a, q * 512:(q + 1) * 512], ps[0:rows, 4 + n % 4, :],
                                   ACT.Copy).then_inc(ht_ready, 1)
            with act.Fori(0, KT // RING) as i:
                for k in range(RING):
                    p = k % 2
                    act.wait_ge(used, i * RING + (N_OUT + k + 1))
                    act.wait_ge(psc_done, i * RING + (k + 1))
                    act.activation(qh[:, p, :], ps[:, p, 0:T], ACT.Copy).then_inc(qh_ready, 1)
                    act.wait_ge(psc_done, i * RING + (k + 3))
                    hold(act)
                    act.activation(sx[:, 0:PT, i * RING + k, :],
                                   ps[:, 2 + p, 0:PT * PK].rearrange("p (a k) -> p a k", a=PT), ACT.Copy)
                    act.activation(sx[0:SAMPLE, PT, i * RING + k, :], ps[0:SAMPLE, 2 + p, PT * PK:3 * PK],
                                   ACT.Copy).then_inc(sx_ready, 1)

            def gate_exp(a):
                act.wait_ge(gd_ready, a + 1)
                g = gate[:, a, 0:TILE_HEADS[a] * PTOP]
                act.activation(g, g, ACT.Exp).then_inc(ge_ready, 1)

            def head_gelu(h, place):
                act.wait_ge(u_used, h * PTOP + (PTOP + URING))
                hold(act)
                act.activation(gel[:, bass.ds(h, 1), :], act_[:, place:place + 1, :],
                               ACT.Gelu_apprx_tanh).then_inc(gelu_ready, 1)

            def norm_sqrt(a, rows):
                act.wait_ge(l2_sq, a + 1)
                act.activation(lnr[0:rows, 1:2], lnr[0:rows, 0:1], ACT.Sqrt).then_inc(rs_ready, 1)

            for h in range(LAG):
                head_gelu(h, h)
            gate_exp(0)
            for a in range(1, 3):
                first = PH * (a - 1) + LAG
                with act.Fori(first, PH + LAG if a == 1 else 2 * PH) as h:
                    head_gelu(h, 0)
                gate_exp(a)
                if a == 1:
                    norm_sqrt(0, P)
            for h in range(2 * PH, 2 * PH + LAG):
                head_gelu(h, 0)
            norm_sqrt(1, P)
            for h in range(2 * PH + LAG, HEADS):
                head_gelu(h, 0)
            norm_sqrt(2, SAMPLE)

        @block.gpsimd
        def _(pool):
            pool.sem_inc(fin_done, 2)
            chain = Chain(pool, poc)
            pool.wait_ge(su_rot, 1)

            def rotation(i, j):
                pool.wait_ge(h_ready, i * PER_QUAD + (j + 1))
                hold(pool)
                s = i * PER_QUAD + j
                dst = rotx[:, j % 2]
                pool.tensor_copy(dst[:, :, 0:SEQ], rot[:, :, s, :])
                pool.tensor_copy(dst[:, :, SEQ:T].rearrange("p c (b l) -> p c b l", b=NB),
                                 spread(rot[:, :, s, 0:NS], 2, NB)).then_inc(rotx_ready, 1)

            def keep_final(i, j):
                pool.wait_ge(h_ready, i * PER_QUAD + (j + 3))
                hold(pool)
                pool.tensor_copy(fin[:, i * PER_QUAD + j], hs[:, j % 2, :, SEQ - 1:T:NS]).then_inc(fin_done, 1)

            with pool.Fori(0, QUADS) as i:
                rotation(i, 0)
                rotation(i, 1)
                keep_final(i, 0)
                rotation(i, 2)
                keep_final(i, 1)
                rotation(i, 3)
                keep_final(i, 2)
                keep_final(i, 3)

            def spread_sample(src):
                pool.tensor_copy(qz0.rearrange("p (b w) -> p b w", b=NB)[:, :, 0:NS],
                                 src[:, 0].rearrange("p (b l) -> p b l", b=NB))
                z1 = qz1.rearrange("p (b w) -> p b w", b=NB)[:, :, 0:260].rearrange("p b (c v) -> p b c v", c=4)
                pool.tensor_copy(z1[:, :, :, 0:5:4],
                                 src[:, 1].rearrange("p (b e c) -> p b c e", b=NB, c=4))
                pool.tensor_copy(qz2.rearrange("p (n v) -> p n v", v=65)[:, :, 0], src[:, 2]).then_inc(qz_ready, 1)

            pool.wait_ge(fin_done, STILES + 2)
            with pool.Fori(0, NJ) as j:
                pool.wait_ge(evac, j * PER_HEAD + EVAC_0)
                pool.wait_ge(vt_done, j + 1)
                hold(pool)
                pool.tensor_copy(vs, qkv[:, bass.ds(j * PER_HEAD + 2 * NG, NG), :]).then_inc(vs_ready, 1)
                pool.wait_ge(qs_ready, j + 1)
                pool.wait_ge(qz_zero, 1)
                pool.wait_ge(v_used, j * NB + 2)
                hold(pool)
                spread_sample(qs[:, :, SEQ:T])
                pool.wait_ge(pt_ready, j * 3 + 3)
                hold(pool)
                spread_sample(ptc)

            eflat = eidx.rearrange("p a e -> p (a e)")

            def stage(which, h, e):
                half = idxs[:, which, e // 8, :].bitcast(I32)
                hold(pool)
                chain.link(pool.tensor_copy(half, eflat[:, bass.ds(h * PTOP + e, 8)].bitcast(I32)))
                return half

            def gather(table, half, e, bufs_, used_, sems, h):
                pool.wait_ge(used_, h * PTOP + (e + 1))
                hold(pool)
                off = bass.IndirectOffsetOnAxis(half[:, e % 8:e % 8 + 1], 0)
                s = e % len(bufs_)
                pool.indirect_dma_start(bufs_[s], None, A[table], off).then_inc(sems[s], 16)

            def rows(u, v):
                if u is not None:
                    pool.wait_ge(idx_ready, u + 1)
                for e in range(PTOP):
                    if e % 8 == 0:
                        uh = stage(0, u, e) if u is not None else None
                        vh = stage(1, v, e) if v is not None else None
                    if u is not None:
                        gather("peer_u", uh, e, ub, u_used, usem, u)
                    if v is not None:
                        gather("peer_v", vh, e, vb, v_used2, vsem, v)

            for h in range(LAG):
                rows(h, None)
            pool.wait_ge(pq_done, 1)
            pool.wait_ge(ht_done, 12)
            with chain.loop(HEADS - LAG, 4) as h:
                rows(h + LAG, h)
            with chain.loop(LAG, 2) as h:
                rows(None, h + (HEADS - LAG))

        @block.vector
        def _(dve):
            for s, n in ((bu_free, 2), (h_ready, 2), (merged, 2), (resid, RING), (u_used, URING),
                         (ypre_ready, 1), (dg_ready, 1)):
                dve.sem_inc(s, n)
            chain = Chain(dve, dvc)
            link = chain.link
            TT, TS, STT = dve.tensor_tensor, dve.tensor_scalar, dve.scalar_tensor_tensor

            dve.wait_ge(su_dt, 1)
            TT(s_u, s_are, s_dt, ALU.mult).then_inc(su_arg, 1)
            link(TT(s_x, s_aim, s_dt, ALU.mult))
            link(TS(s_n, s_x, 1.0 / (2.0 * float(np.pi)), ROUND, ALU.mult, ALU.add))
            link(TS(s_n, s_n, -ROUND, None, ALU.add))
            link(STT(s_r, s_n, -TWO_PI_HI, s_x, ALU.mult, ALU.add))
            link(STT(s_r, s_n, -TWO_PI_LO, s_r, ALU.mult, ALU.add))
            link(TS(s_r, s_r, PI_SAFE, -PI_SAFE, ALU.min, ALU.max))
            link(STT(s_p, s_r, -1.0, s_r, ALU.mult, ALU.max))
            TS(s_p, s_p, -1.0, float(np.pi) / 2, ALU.mult, ALU.add).then_inc(su_arg, 1)
            dve.memset(fre_z[:, STILES:], 0.0)
            dve.memset(fim_z[:, STILES:], 0.0)
            link(TT(s_den, s_are, s_are, ALU.mult))
            link(TT(s_q, s_aim, s_aim, ALU.mult))
            link(TT(s_den, s_den, s_q, ALU.add))
            link(dve.reciprocal(s_den, s_den))
            dve.wait_ge(su_act, 1)
            link(TT(h0m.rearrange("p s c b -> p s (c b)"), s_h0.rearrange("p s c b -> p s (c b)"),
                    spread(mag, 2, 2 * NB), ALU.mult))
            dve.wait_ge(su_trig, 1)
            TT(s_br, mag, s_cos, ALU.mult)
            link(TT(s_bi, mag, s_sin, ALU.mult))
            link(TS(s_br, s_br, -1.0, None, ALU.add))
            TT(fre, s_br, s_are, ALU.mult)
            TT(fim, s_bi, s_are, ALU.mult)
            TT(s_q, s_bi, s_aim, ALU.mult)
            link(TT(s_n, s_br, s_aim, ALU.mult))
            TT(fre, fre, s_q, ALU.add)
            link(TT(fim, fim, s_n, ALU.subtract))
            TT(fre, fre, s_den, ALU.mult)
            link(TT(fim, fim, s_den, ALU.mult))
            dve.tensor_copy(rot[:, 0, :, 0], s_cos)
            link(dve.tensor_copy(rot[:, 1, :, 0], s_sin))
            n = 1
            while n < SEQ:
                c, s = rot[:, 0, :, 0:n], rot[:, 1, :, 0:n]
                cn = rot[:, 0, :, n - 1:n].to_broadcast([P, STILES, n])
                sn_ = rot[:, 1, :, n - 1:n].to_broadcast([P, STILES, n])
                a_, b_ = half[:, 0, :, 0:n], half[:, 1, :, 0:n]
                TT(a_, c, cn, ALU.mult)
                link(TT(b_, s, sn_, ALU.mult))
                link(TT(rot[:, 0, :, n:2 * n], a_, b_, ALU.subtract))
                TT(a_, c, sn_, ALU.mult)
                link(TT(b_, s, cn, ALU.mult))
                link(TT(rot[:, 1, :, n:2 * n], a_, b_, ALU.add))
                n *= 2
            dve.sem_inc(su_rot, 1)

            def states(i, j):
                p = j % 2
                s = i * PER_QUAD + j
                bu = ps[:, 2 + 2 * p:4 + 2 * p, 0:T]
                cos, sin = spread(rotx[:, p, 0, :], 1, 2), spread(rotx[:, p, 1, :], 1, 2)
                dve.wait_ge(bu_ready, i * PER_QUAD + (j + 2))
                dve.wait_ge(rotx_ready, i * PER_QUAD + (j + 1))
                dve.wait_ge(h_ready, i * PER_QUAD + (j + 2))
                TT(m1, bu, cos, ALU.mult)
                TT(m2, bu, sin, ALU.mult).then_inc(bu_free, 1)
                dve.wait_ge(bu_free, i * PER_QUAD + (j + 3))
                TT(gw[:, 0, :], m1[:, 0, :], m2[:, 1, :], ALU.add)
                link(TT(gw[:, 1, :], m1[:, 1, :], m2[:, 0, :], ALU.subtract))
                starts = gw[:, :, SEQ:T:NS]
                link(TT(starts, starts, h0m[:, s], ALU.add))
                dve.wait_ge(magx_ready, i * PER_QUAD + (j + 1))
                for c in range(2):
                    ins = dve.tensor_tensor_scan(m1[:, c, :], magx[:, p, :], gw[:, c, :], 0.0, ALU.mult, ALU.add)
                link(ins)
                TT(m2, m1, cos, ALU.mult)
                link(TT(gw, m1, sin, ALU.mult))
                dve.wait_ge(y_done, i * PER_QUAD + (j + 1))
                dve.wait_ge(fin_done, i * PER_QUAD + (j + 1))
                TT(hs[:, p, 0, :], m2[:, 0, :], gw[:, 1, :], ALU.subtract)
                TT(hs[:, p, 1, :], m2[:, 1, :], gw[:, 0, :], ALU.add).then_inc(h_ready, 1)

            def scale_b(q):
                quad = bass.ds(q * PER_QUAD, PER_QUAD)
                br = braw.rearrange("p c (j k) -> p c j k", j=PER_QUAD)
                t1 = m1[:, :, 0:P].rearrange("p c (j k) -> p c j k", j=PER_QUAD)
                t2 = m2[:, :, 0:P].rearrange("p c (j k) -> p c j k", j=PER_QUAD)
                dve.wait_ge(b_in, q * 16 + 16)
                TT(t1, br, spread(spread(fre_z[:, quad], 2, 32), 1, 2), ALU.mult)
                link(TT(t2, br, spread(spread(fim_z[:, quad], 2, 32), 1, 2), ALU.mult))
                dve.wait_ge(bt_done, q + 1)
                TT(bbq[:, 0, :], m1[:, 0, 0:P], m2[:, 1, 0:P], ALU.subtract)
                TT(bbq[:, 1, :], m1[:, 1, 0:P], m2[:, 0, 0:P], ALU.add).then_inc(bb_ready, 1)
                dve.wait_ge(bb_ready, q + 1)

            scale_b(0)
            with chain.loop(QUADS // BODY, BODY * (1 + 4 * PER_QUAD)) as i:
                for k in range(BODY):
                    q = i * BODY + k
                    for j in range(PER_QUAD - 1):
                        states(q, j)
                    dve.wait_ge(h_ready, q * PER_QUAD + (PER_QUAD + 1))
                    scale_b(q + 1)
                    states(q, PER_QUAD - 1)
                    dve.wait_ge(y_done, q * PER_QUAD + (PER_QUAD + 2))
                    dve.wait_ge(g_ready, q + 1)
                    STT(ypre, uq[:, k % 2], dskip[:, bass.ds(q, 1)], ps[:, 6, 0:T], ALU.mult,
                        ALU.add).then_inc(ypre_ready, 1)

            dve.wait_ge(fin_done, STILES + 2)
            dve.memset(arena[:, lo_qz:hi_qz], 0.0).then_inc(qz_zero, 1)
            dve.wait_ge(att_in, 4 * 16)
            def gate_product(m):
                dve.wait_ge(sig_ready, m + 1)
                TT(so[:, m, :], gT[:, m, :], sig[:, m % 2, :], ALU.mult).then_inc(so_ready, 1)

            def attention(j, products):
                link(dve.tensor_copy(nsl, slopes[:, j, :]))

                def negative_max(w, s, rows):
                    dve.tensor_reduce(st[0:rows, w, 0:1], s, AX.XY if len(s.shape) == 3 else AX.X, ALU.max,
                                      negate=True).then_inc(mx, 1)

                def normalise(w, s, rows):
                    dve.wait_ge(ex, j * 3 + (w + 1))
                    link(dve.reciprocal(st[0:rows, w, 2:3], st[0:rows, w, 1:2]))
                    TS(s, s, st[0:rows, w, 2:3], None, ALU.mult).then_inc(p_ready, 1)

                dve.wait_ge(sc0_done, j + 1)
                dve.wait_ge(pt_done, j * 3 + 1)
                for g in range(NG):
                    ins = STT(s0[:, g, :], dist[:, g, P:SEQ], nsl[:, g:g + 1], ps[:, 3, g * P:(g + 1) * P],
                              ALU.mult, ALU.add)
                link(ins)
                negative_max(0, s0, P)
                dve.wait_ge(sc1_done, j + 1)
                for g in range(NG):
                    ins = STT(s1[:, g, :], dist[:, g, :], nsl[:, g:g + 1],
                              ps[:, 4 + g // 2, (g % 2) * SEQ:(g % 2 + 1) * SEQ], ALU.mult, ALU.add)
                link(ins)
                negative_max(1, s1, P)
                normalise(0, s0, P)
                normalise(1, s1, P)
                for m in products[:3]:
                    gate_product(m)
                dve.wait_ge(k_used, j * NB + (NB + 2))
                R = SAMPLE
                for g in range(NG):
                    STT(sc[0:R, g, :], dist_c[0:R, g, :], nsl[0:R, g:g + 1], ps[0:R, 6, g * P:(g + 1) * P],
                        ALU.mult, ALU.add)
                    ins = STT(sn[0:R, g, :], dist_n[0:R, g, :], nsl[0:R, g:g + 1], ps[0:R, 5, SEQ + g * R:SEQ + (g + 1) * R],
                              ALU.mult, ALU.add)
                link(ins)
                negative_max(2, scn[0:R], R)
                for m in products[3:4]:
                    gate_product(m)
                normalise(2, scn[0:R], R)
                for m in products[4:]:
                    gate_product(m)

            with chain.loop(NJ - 1, 7) as j:
                attention(j, ())
            attention(NJ - 1, range(QUADS))

            with chain.loop(KT // 4, 4) as i:
                for k in range(4):
                    p = k % 2
                    dve.wait_ge(sg_ready, i * 4 + (k + 1))
                    dve.wait_ge(used, i * 12 + (N_GLU + 3 * k + 3))
                    link(TT(gp[:, p], gsg[:, p], ps[:, 4 * p + 2:4 * p + 4, 0:T], ALU.mult))
                    TT(mT[:, i * 4 + k, :], gp[:, p, 0, :], gp[:, p, 1, :], ALU.add).then_inc(merged, 1)
            with dve.Fori(0, KT // RING) as i:
                for k in range(RING):
                    dve.wait_ge(used, i * RING + (N_MERGE + k + 1))
                    STT(xT[:, i * RING + k, :], xT[:, i * RING + k, :], ALPHA, ps[:, k, 0:T],
                        ALU.mult, ALU.add).then_inc(resid, 1)
            dve.wait_ge(mean_done, 1)
            for c in range(4):
                part = xT[:, 4 * c:4 * c + 4, :]
                TT(part, part, spread(ps[:, 4, 0:T], 1, 4), ALU.subtract).then_inc(cent, 1)
            dve.wait_ge(var_done, 1)
            link(TS(var, ps[:, 5, 0:T], EPS, None, ALU.add))
            dve.reciprocal(rv, var).then_inc(rv_ready, 1)
            dve.wait_ge(rs_ready, 1)
            link(TT(nt, var, rs, ALU.mult))
            link(TT(nt, nt, rs, ALU.mult))
            link(TS(nt, nt, -0.5, 1.5, ALU.mult, ALU.add))
            link(TT(rs, rs, nt, ALU.mult))
            for c in range(4):
                part = xT[:, 4 * c:4 * c + 4, :]
                TT(part, part, spread(rs, 1, 4), ALU.mult).then_inc(nrm, 1)

            dve.wait_ge(peer_in, 2 * 16)
            dve.wait_ge(stored, (NJ + 1) * 16)
            TT(pairs, ident[:, 0:SAMPLE], ident[:, SAMPLE:P], ALU.add)
            link(TS(adiag, ident, ALPHA, None, ALU.mult))
            dve.sem_inc(seeded, 1)

            def topk_head(a, h):
                link(dve.tensor_copy(sc2, sx[:, a, bass.ds(h * 2, 2), :]))
                hold(dve)
                for lo in (0, 8):
                    for s in range(2):
                        ins = dve.max(v16[:, s, lo:lo + 8], sc2[:, s, :])
                    link(ins)
                    hold(dve)
                    for s in range(2):
                        ins = dve.max_index(i16[:, s, lo:lo + 8].bitcast(U32), v16[:, s, lo:lo + 8], sc2[:, s, :])
                    if lo == 0:
                        for s in range(2):
                            ins = dve.match_replace(sc2[:, s, :], v16[:, s, 0:8], sc2[:, s, :], NEG)
                        link(ins)
                        hold(dve)
                link(TT(cand, spread(v16[:, 0, :], 2, PTOP), spread(v16[:, 1, :], 1, PTOP), ALU.add))
                cflat = cand.rearrange("p a b -> p (a b)")
                for lo in (0, 8):
                    hold(dve)
                    link(dve.max(t16[:, lo:lo + 8], cflat))
                    hold(dve)
                    ins = dve.max_index(p16[:, lo:lo + 8].bitcast(U32), t16[:, lo:lo + 8], cflat)
                    if lo == 0:
                        link(dve.match_replace(cflat, t16[:, 0:8], cflat, NEG))
                link(ins)
                TS(gate[:, a, bass.ds(h * PTOP, PTOP)], t16, t16[:, 0:1], None, ALU.subtract)
                dve.tensor_copy(if16, i16.bitcast(U32))
                TS(ab[:, 0, :].bitcast(U32), p16.bitcast(U32), 4, None, ALU.logical_shift_right)
                link(TS(ab[:, 1, :].bitcast(U32), p16.bitcast(U32), PTOP - 1, None, ALU.bitwise_and))
                link(dve.tensor_copy(abf, ab.bitcast(U32)))
                io = spread(spread(iota, 1, PTOP), 1, 2)
                link(TT(oh, spread(abf, 3, PTOP), io, ALU.is_equal))
                link(TT(oh, oh, spread(if16, 2, PTOP), ALU.mult))
                link(dve.tensor_reduce(e12, oh, AX.X, ALU.add))
                STT(eidx[:, a, bass.ds(h * PTOP, PTOP)].bitcast(I32), e12[:, 0, :], float(PK), e12[:, 1, :],
                    ALU.mult, ALU.add).then_inc(idx_ready, 1)

            TOPK_LINKS = 14

            def gates(a):
                dve.sem_inc(gd_ready, 1)
                dve.wait_ge(ge_ready, a + 1)
                heads = TILE_HEADS[a]
                gv = gate[:, a, 0:heads * PTOP].rearrange("p (h k) -> p h k", h=heads)
                gs = gsum[:, 0:heads]
                link(dve.tensor_reduce(gs, gv, AX.X, ALU.add))
                link(dve.reciprocal(gs, gs))
                link(TT(gv, gv, spread(gs, 2, PTOP), ALU.mult))

            gflat = gate.rearrange("p a e -> p (a e)")

            def dot(a, h, e, place):
                k = e % URING
                dve.wait_ge(usem[k], h * (16 * PTOP // URING) + 16 * (e // URING + 1))
                dve.tensor_tensor_reduce(ub[k], ub[k], htok[:, a, :], 1.0, 0.0, ALU.mult,
                                         ALU.add, act_[:, place, e:e + 1]).then_inc(u_used, 1)

            def weights(h):
                dve.wait_ge(gelu_ready, h + 1)
                dve.wait_ge(dg_ready, h * PTOP + 1)
                link(TT(wgt, gel[:, bass.ds(h, 1), :].rearrange("p a e -> p (a e)"), gflat[:, bass.ds(h * PTOP, PTOP)],
                        ALU.mult))

            def diagonal(a, h, e):
                dve.wait_ge(v_used2, h * PTOP + (e + 1 + VRING - DIAGS))
                n = P if a < PT else SAMPLE
                TS(diag[:, e % DIAGS, 0:n], (ident if a < PT else pairs)[:, 0:n], wgt[:, e:e + 1], None,
                   ALU.mult).then_inc(dg_ready, 1)

            def experts(u_tile, u, v_tile, v):
                dve.wait_ge(gelu_ready, u)
                weights(v)
                for e in range(PTOP):
                    dot(u_tile, u, e, 0)
                    diagonal(v_tile, v, e)

            n = LAG * PTOP // PH
            for h in range(PH):
                dve.wait_ge(sx_ready, h * 2 + 4)
                topk_head(0, h)
                for e in range(h * n, (h + 1) * n):
                    dot(0, e // PTOP, e % PTOP, e // PTOP)
            gates(0)

            def second_norm(a, rows):
                R = slice(0, rows)
                f = ps[R, 4 * (a % 2):4 * (a % 2) + 4, :]
                dve.wait_ge(v_used2, VRING + PTOP * sum(TILE_HEADS[:a + 1]))
                for q in range(4):
                    ins = dve.bn_stats(bns[R, q, :], f[:, q, :])
                link(ins)
                link(dve.bn_aggr(bna[R], bns[R].rearrange("p a b -> p (a b)")))
                link(TS(lnr[R, 2:3], bna[R, 1:2], EPS, None, ALU.add))
                dve.reciprocal(lnr[R, 0:1], lnr[R, 2:3]).then_inc(l2_sq, 1)
                if a == 0:
                    dve.wait_ge(l2_in, 2 * 16)
                else:
                    dve.wait_ge(y_out, 16 * a)
                y4, g4 = (v[R].rearrange("p (q n) -> p q n", q=4) for v in (yt, g2))
                STT(y4, f, bna[R, 0:1], g4, ALU.subtract, ALU.mult)
                dve.wait_ge(rs_ready, a + 2)
                link(TT(lnr[R, 3:4], lnr[R, 2:3], lnr[R, 1:2], ALU.mult))
                link(TT(lnr[R, 3:4], lnr[R, 3:4], lnr[R, 1:2], ALU.mult))
                link(TS(lnr[R, 3:4], lnr[R, 3:4], -0.5, 1.5, ALU.mult, ALU.add))
                link(TT(lnr[R, 1:2], lnr[R, 1:2], lnr[R, 3:4], ALU.mult))
                STT(yt[R], yt[R], lnr[R, 1:2], b2[R], ALU.mult, ALU.add).then_inc(y_ready, 1)

            def steps(u_tile, u, v_tile, v, n, topk_of=None, first=0):
                with chain.loop(n, 1 + (TOPK_LINKS if topk_of else 0)) as g:
                    experts(u_tile, g + u, v_tile, g + v)
                    if topk_of:
                        topk_head(topk_of, g + first)

            steps(0, LAG, 0, 0, PH - LAG, topk_of=1)
            steps(1, PH, 0, PH - LAG, LAG, topk_of=1, first=PH - LAG)
            gates(1)
            second_norm(0, P)
            dve.wait_ge(packed, 2 * 16)
            steps(1, PH + LAG, 1, PH, PH // 2, topk_of=2)
            steps(1, 2 * PH - LAG, 1, 2 * PH - 2 * LAG, LAG)
            gates(2)
            steps(2, 2 * PH, 1, 2 * PH - LAG, LAG)
            second_norm(1, P)
            steps(2, 2 * PH + LAG, 2, 2 * PH, LAG)
            with chain.loop(LAG, 1) as g:
                weights(g + (HEADS - LAG))
                for e in range(PTOP):
                    diagonal(2, g + (HEADS - LAG), e)
            second_norm(2, SAMPLE)


def tiles_of(w, k, n):
    K, N = w.shape
    assert K == k * P
    return np.ascontiguousarray(w.reshape(k, P, N // n, n).transpose(2, 1, 0, 3))


def constants():
    f = np.float32
    slopes = -(2.0 ** (-8.0 * np.arange(1, NHEAD + 1) / NHEAD))
    dist = np.full((P, NG, SEQ), FAR)
    dist_c = np.full((SAMPLE, NG, P), FAR)
    dist_n = np.full((SAMPLE, NG, SAMPLE), FAR)
    for g, (w, d) in enumerate(zip(WINDOWS, DILS)):
        off = (P + np.arange(P))[:, None] - np.arange(SEQ)[None, :]
        ok = (off >= 0) & (off <= w) & (off % d == 0)
        dist[:, g] = np.where(ok, off, FAR)
        for b in range(NB):
            for i in range(NS):
                row = i % CLASSES[g] + d * np.arange(P)
                off = w + i - row
                dist_c[b * NS + i, g] = np.where(off <= w, off, FAR)
                for l in range(i + 1):
                    if (i - l) % d == 0:
                        dist_n[b * NS + i, g, b * NS + l] = i - l
    mask = np.ones((P, T))
    mask[:, SEQ::NS] = 0
    mask[:, 0] = 0
    return {
        "ident": np.eye(P, dtype=f), "ones": np.full((P, P), 1.0 / D, f), "mask": mask.astype(f),
        "iota": np.tile(np.arange(PTOP, dtype=f), (P, 1)),
        "slopes": np.tile(slopes.reshape(NG, NJ).T.astype(f)[None], (P, 1, 1)),
        "dist": dist.astype(f), "dist_c": dist_c.astype(f), "dist_n": dist_n.astype(f),
    }


def lay_out(x):
    tok = np.concatenate([x["x_prompt"].reshape(SEQ, D), x["x_sample"].reshape(SAMPLE, D)])
    out = constants()
    out["xT"] = tok.T.reshape(KT, P, T).transpose(1, 0, 2)
    w = tiles_of(x["w_in"], KT, P)
    u, heads, gs, ga = w[:QUADS], w[QUADS:QUADS + QKV_TILES], w[N_X:N_X + KT], w[N_X + KT:]
    heads = heads.reshape(3, NG, NJ, *heads.shape[1:]).swapaxes(1, 2).swapaxes(0, 1)
    heads = heads.reshape(QKV_TILES, *heads.shape[3:])
    order = list(heads[:N_PRE])
    for q in range(QUADS):
        order += [u[q], heads[N_PRE + 2 * q], heads[N_PRE + 2 * q + 1]]
    order += list(heads[O_FILL:])
    glu = tiles_of(x["ssm_w_glu"], QUADS, P).reshape(QUADS // 2, 2, P, QUADS * P).swapaxes(1, 2)
    bs, ba = tiles_of(x["w_branch_ssm"], QUADS, P), tiles_of(x["w_branch_attn"], NJ, P)
    branch = np.zeros((KT, P, KT, P), np.float32)
    branch[:, :, :QUADS] = bs
    branch[:, :, QUADS:QUADS + NJ] = ba
    parts = (np.stack(order), glu, np.stack([gs, ga, branch], axis=1), tiles_of(x["w_out"], KT, P),
             tiles_of(x["peer_w_q"], KT, P))
    out["w"] = np.concatenate([p.reshape(-1, P, WSLOT) for p in parts])

    def states(a):
        return np.moveaxis(a.reshape(STILES, P, *a.shape[2:]), 1, 0)

    out["log_dt"] = states(np.repeat(x["ssm_log_dt"][:, None], 64, axis=1))
    out["a_re"], out["a_im"] = states(x["ssm_a_re"]), states(x["ssm_a_im"])
    out["h0"] = states(np.transpose(x["state_ssm"], (1, 2, 3, 0)))
    out["dskip"] = x["ssm_d"].reshape(QUADS, P).T

    def blocks(re, im):
        both = np.stack([re, im], axis=2).reshape(QUADS, PER_QUAD, 2, 64, 2, 16)
        o = np.zeros((QUADS + 1, 2, 64, 2, PER_QUAD, 2, 16), np.float32)
        for half in range(2):
            o[:QUADS, half, :, :, :, half] = both[:, :, half].transpose(0, 2, 3, 1, 4)
        return o.reshape(QUADS + 1, P, 2, P)

    out["ssm_b"] = blocks(x["ssm_b_re"], x["ssm_b_im"])
    out["ssm_c"] = blocks(x["ssm_c_re"].transpose(0, 2, 1), x["ssm_c_im"].transpose(0, 2, 1))

    ks, vs = [], []
    for g, (name, d) in enumerate(zip(("cache_kv_w128", "cache_kv_w512", "cache_kv_w2048"), DILS)):
        c = x[name].reshape(NB, P, d, 2, NJ, HD)[:, :, :CLASSES[g]]
        ks.append(c[:, :, :, 0].transpose(3, 0, 4, 2, 1))
        vs.append(c[:, :, :, 1].transpose(3, 0, 1, 2, 4))
    out["k_cache"] = np.concatenate(ks, axis=3).reshape(NJ * NB, P, CBLK, P)
    out["v_cache"] = np.concatenate(vs, axis=3).reshape(NJ * NB, P, CBLK, P)
    out["ln1"] = np.stack([x["ln1_g"].reshape(KT, P).T, x["ln1_b"].reshape(KT, P).T], axis=1)
    out["ln2"] = np.stack([np.tile(x["ln2_g"], (P, 1)), np.tile(x["ln2_b"], (P, 1))])
    out["sub_keys"] = np.stack([x["peer_sub_keys_1"].T, x["peer_sub_keys_2"].T], axis=1)
    out["peer_u"], out["peer_v"] = x["peer_u"], x["peer_v"]
    return {k: np.ascontiguousarray(v) for k, v in out.items()}


OUTS = {"y": (T, D), "kv": (P, 2 * NHEAD, T), "ssm": (P, STILES, 2, NFIN)}


def kernel(**inputs):
    import concourse.bacc as bacc
    from concourse.bass_utils import run_bass_kernel_spmd

    arrays = lay_out({k: np.asarray(v) for k, v in inputs.items()})
    nc = bacc.Bacc("TRN2", target_bir_lowering=False, num_devices=1)
    A = {k: nc.dram_tensor(f"in_{k}", v.shape, F32, kind="ExternalInput").ap() for k, v in arrays.items()}
    O = {k: nc.dram_tensor(f"out_{k}", s, F32, kind="ExternalOutput").ap() for k, s in OUTS.items()}
    layer_kernel(nc, A, O)
    r = run_bass_kernel_spmd(nc, [{f"in_{k}": v for k, v in arrays.items()}], core_ids=[0]).results[0]
    y, kv, ssm = r["out_y"], r["out_kv"], r["out_ssm"]
    kv = kv.reshape(HD, NJ, 2, NG, T).transpose(3, 4, 2, 1, 0)
    prompt = [kv[g, max(0, SEQ - w):SEQ][None] for g, w in enumerate(WINDOWS)]
    sample = [kv[g, SEQ:].reshape(NB, NS, 2, NJ, HD) for g in range(NG)]
    ssm = ssm.reshape(2, 64, STILES, 2, NFIN).transpose(4, 2, 0, 1, 3).reshape(NFIN, 64, 64, 2)
    return (y[:SEQ][None], y[SEQ:].reshape(NB, NS, D), *prompt, ssm[:1], *sample, ssm[1:])
```
